# Optimizing a Trainium2 kernel written in Bass

```python
import math
import jax, jax.numpy as jnp
from jax import lax
import numpy as np

D_MODEL = 1024
BATCH = 1
SEQ = 1024
DEPTH = 1
DEC_BATCH = 8
DEC_SEQ = 8
PAST_LEN = 8192
PAGE_SIZE = 128

BRANCH_W = D_MODEL // 2
S5_W = BRANCH_W
S5_GROUP = 16
S5_GROUPS = S5_W // S5_GROUP
S5_STATE = 64
S5_DT_MIN = 1e-3
S5_DT_MAX = 1e-1
RWKV_W = BRANCH_W
RWKV_HEAD = 64
RWKV_HEADS = RWKV_W // RWKV_HEAD
DECAY_RANK = 64
ICLR_RANK = 64
GN_EPS = 64e-5
POOL_W = BRANCH_W
POOL_WINDOWS = (2, 4, 8, 16)
POOL_GROUPS = len(POOL_WINDOWS)
POOL_GW = POOL_W // POOL_GROUPS
POOL_BUF = max(POOL_WINDOWS) - 1
N_BRANCH = 3
RWKV_SHIFT_W = 3 * RWKV_W + DECAY_RANK + ICLR_RANK
IN_SIZES = (S5_W, S5_W, RWKV_SHIFT_W, RWKV_W, POOL_W, POOL_W, N_BRANCH * D_MODEL)
IN_W = sum(IN_SIZES)
IN_SPLITS = tuple(int(o) for o in np.cumsum(IN_SIZES)[:-1])
RWKV_SPLITS = tuple(int(o) for o in np.cumsum((RWKV_W, RWKV_W, RWKV_W, DECAY_RANK)))
NORM_EPS = 1e-6

kernel_name = "hybrid_s5_rwkv7_pool_gated_decoder_step"

def rmsnorm(x, g):
    xf = x.astype(jnp.float32)
    y = xf * lax.rsqrt(jnp.mean(xf * xf, axis=-1, keepdims=True) + NORM_EPS) * g.astype(jnp.float32)
    return y.astype(x.dtype)

def s5_mix(u, h0_re, h0_im, lam_re, lam_im, log_dt, b_re, b_im, c_re, c_im, d_skip, w_glu):
    f32 = jnp.float32
    bt, t, _ = u.shape
    uf = u.astype(f32).reshape(bt, t, S5_GROUPS, S5_GROUP)
    lr = lam_re.astype(f32)
    li = lam_im.astype(f32)
    dt = jnp.exp(log_dt.astype(f32))[:, None]
    mag = jnp.exp(lr * dt)
    ab_r = mag * jnp.cos(li * dt)
    ab_i = mag * jnp.sin(li * dt)
    den = lr * lr + li * li
    nr = ab_r - 1.0
    co_r = (nr * lr + ab_i * li) / den
    co_i = (ab_i * lr - nr * li) / den
    bu_r = jnp.einsum('btgc,gnc->btgn', uf, b_re.astype(f32))
    bu_i = jnp.einsum('btgc,gnc->btgn', uf, b_im.astype(f32))
    bb_r = co_r * bu_r - co_i * bu_i
    bb_i = co_r * bu_i + co_i * bu_r
    a_r = jnp.broadcast_to(ab_r, bb_r.shape)
    a_i = jnp.broadcast_to(ab_i, bb_i.shape)

    def combine(e1, e2):
        a1r, a1i, b1r, b1i = e1
        a2r, a2i, b2r, b2i = e2
        return (a2r * a1r - a2i * a1i, a2r * a1i + a2i * a1r,
                a2r * b1r - a2i * b1i + b2r, a2r * b1i + a2i * b1r + b2i)

    acr, aci, hr, hi = lax.associative_scan(combine, (a_r, a_i, bb_r, bb_i), axis=1)
    h0r = h0_re.astype(f32)[:, None]
    h0i = h0_im.astype(f32)[:, None]
    hr = hr + acr * h0r - aci * h0i
    hi = hi + acr * h0i + aci * h0r
    y = jnp.einsum('btgn,gcn->btgc', hr, c_re.astype(f32)) - jnp.einsum('btgn,gcn->btgc', hi, c_im.astype(f32))
    y = y + d_skip.astype(f32).reshape(S5_GROUPS, S5_GROUP) * uf
    y = jax.nn.gelu(y.reshape(bt, t, S5_W))
    y = y * jax.nn.sigmoid(y @ w_glu.astype(f32))
    return y.astype(u.dtype), hr[:, -1], hi[:, -1]

def rwkv_mix(p, shift_prev, s0, mu, w0, w_w2, a0, w_a2, k_k, k_a, r_k, gn_w, gn_b):
    f32 = jnp.float32
    bt, t, _ = p.shape
    pf = p.astype(f32)
    prev = jnp.concatenate([shift_prev.astype(f32)[:, None], pf[:, :-1]], axis=1)
    pm = pf + (prev - pf) * mu.astype(f32)
    r, k, v, lw, la = jnp.split(pm, RWKV_SPLITS, axis=-1)
    w_log = -jax.nn.softplus(-(w0.astype(f32) + jnp.tanh(lw) @ w_w2.astype(f32))) - 0.5
    decay = jnp.exp(-jnp.exp(w_log))
    a = jax.nn.sigmoid(a0.astype(f32) + la @ w_a2.astype(f32))
    hd = lambda z: z.reshape(bt, t, RWKV_HEADS, RWKV_HEAD)
    r, k, v, decay, a = hd(r), hd(k), hd(v), hd(decay), hd(a)
    kk = k * k_k.astype(f32).reshape(RWKV_HEADS, RWKV_HEAD)
    kk = kk * lax.rsqrt(jnp.maximum(jnp.sum(kk * kk, axis=-1, keepdims=True), 1e-24))
    k = k * (1.0 + (a - 1.0) * k_a.astype(f32).reshape(RWKV_HEADS, RWKV_HEAD))

    def step(s, inp):
        r_t, w_t, k_t, v_t, kk_t, a_t = inp
        sa = jnp.einsum('bhvk,bhk->bhv', s, -kk_t)
        s = s * w_t[:, :, None, :] + sa[..., None] * (kk_t * a_t)[:, :, None, :] + v_t[..., None] * k_t[:, :, None, :]
        return s, jnp.einsum('bhvk,bhk->bhv', s, r_t)

    tm = lambda z: jnp.moveaxis(z, 1, 0)
    s_fin, o = lax.scan(step, s0.astype(f32), (tm(r), tm(decay), tm(k), tm(v), tm(kk), tm(a)))
    o = jnp.moveaxis(o, 0, 1)
    mean = jnp.mean(o, axis=-1, keepdims=True)
    var = jnp.mean(jnp.square(o - mean), axis=-1, keepdims=True)
    o = (o - mean) * lax.rsqrt(var + GN_EPS) * gn_w.astype(f32).reshape(RWKV_HEADS, RWKV_HEAD) \
        + gn_b.astype(f32).reshape(RWKV_HEADS, RWKV_HEAD)
    o = o + jnp.sum(r * k * r_k.astype(f32), axis=-1, keepdims=True) * v
    return o.reshape(bt, t, RWKV_W).astype(p.dtype), p[:, -1], s_fin

def pool_mix(u, buf, start, pool_w, pool_scale):
    f32 = jnp.float32
    bt, t, _ = u.shape
    uf = u.astype(f32)
    ext = jnp.concatenate([buf.astype(f32), uf], axis=1)
    cs = jnp.concatenate([jnp.zeros((bt, 1, POOL_W), f32), jnp.cumsum(ext, axis=1)], axis=1)
    pos = start + jnp.arange(t)
    outs = []
    for gi, win in enumerate(POOL_WINDOWS):
        sl = slice(gi * POOL_GW, (gi + 1) * POOL_GW)
        end = cs[:, POOL_BUF + 1:, sl]
        beg = cs[:, POOL_BUF + 1 - win:POOL_BUF + 1 - win + t, sl]
        cnt = jnp.minimum(pos + 1, win).astype(f32)[None, :, None]
        outs.append((end - beg) / cnt)
    pooled = jnp.concatenate(outs, axis=-1) - uf
    mixed = jnp.einsum('btgc,gcd->btgd', pooled.reshape(bt, t, POOL_GROUPS, POOL_GW), pool_w.astype(f32))
    mixed = mixed.reshape(bt, t, POOL_W) * pool_scale.astype(f32)
    return mixed.astype(u.dtype), ext[:, -POOL_BUF:].astype(u.dtype)

def trunk_layer(x, s5_re, s5_im, rw_s, rw_shift, pool_buf, start,
                g_pre, g_post, w_in, lam_re, lam_im, log_dt, b_re, b_im, c_re, c_im, d_skip, w_glu,
                mu, w0, w_w2, a0, w_a2, k_k, k_a, r_k, gn_w, gn_b, pool_w, pool_scale,
                w_up_s5, w_up_rwkv, w_up_pool, w_o):
    bt, t, _ = x.shape
    h = rmsnorm(x, g_pre)
    s5_x, s5_z, rw_p, rw_z, pl_x, pl_z, gate_cols = jnp.split(h @ w_in, IN_SPLITS, axis=-1)
    y_s5, n_re, n_im = s5_mix(s5_x, s5_re, s5_im, lam_re, lam_im, log_dt, b_re, b_im, c_re, c_im, d_skip, w_glu)
    y_rw, n_shift, n_s = rwkv_mix(rw_p, rw_shift, rw_s, mu, w0, w_w2, a0, w_a2, k_k, k_a, r_k, gn_w, gn_b)
    y_pl, n_buf = pool_mix(pl_x, pool_buf, start, pool_w, pool_scale)
    u_s5 = (y_s5 * jax.nn.silu(s5_z)) @ w_up_s5
    u_rw = (y_rw * jax.nn.silu(rw_z)) @ w_up_rwkv
    u_pl = (y_pl * jax.nn.silu(pl_z)) @ w_up_pool
    gates = jax.nn.sigmoid(gate_cols.astype(jnp.float32)).reshape(bt, t, N_BRANCH, D_MODEL)
    merged = gates[:, :, 0] * u_s5 + gates[:, :, 1] * u_rw + gates[:, :, 2] * u_pl
    out = merged.astype(x.dtype) @ w_o
    return x + rmsnorm(out, g_post), n_re, n_im, n_s, n_shift, n_buf

def setup_inputs(seed: int = 0) -> dict:
    key = jax.random.key(seed)
    ks = iter(jax.random.split(key, 64))
    f32 = jnp.float32
    L, D = DEPTH, D_MODEL
    G, N, C = S5_GROUPS, S5_STATE, S5_GROUP

    def nrm(shape, scale):
        return jax.random.normal(next(ks), shape, f32) * scale

    return {
        "x_prompt": nrm((BATCH, SEQ, D), 1.0),
        "x_sample": nrm((DEC_BATCH, DEC_SEQ, D), 1.0),
        "state_s5_re": nrm((L, DEC_BATCH, G, N), 0.1),
        "state_s5_im": nrm((L, DEC_BATCH, G, N), 0.1),
        "state_rwkv": nrm((L, DEC_BATCH, RWKV_HEADS, RWKV_HEAD, RWKV_HEAD), 0.1),
        "state_shift": nrm((L, DEC_BATCH, RWKV_SHIFT_W), 1.0),
        "state_pool": nrm((L, DEC_BATCH, POOL_BUF, POOL_W), 1.0),
        "norm_pre": 1.0 + nrm((L, D), 0.05),
        "norm_post": 1.0 + nrm((L, D), 0.05),
        "w_in": nrm((L, D, IN_W), D ** -0.5),
        "s5_lam_re": -0.5 + nrm((L, G, N), 0.01),
        "s5_lam_im": math.pi * jnp.arange(N, dtype=f32) + nrm((L, G, N), 0.01),
        "s5_log_dt": jax.random.uniform(next(ks), (L, G), f32, math.log(S5_DT_MIN), math.log(S5_DT_MAX)),
        "s5_b_re": nrm((L, G, N, C), (2 * C) ** -0.5),
        "s5_b_im": nrm((L, G, N, C), (2 * C) ** -0.5),
        "s5_c_re": nrm((L, G, C, N), (2 * N) ** -0.5),
        "s5_c_im": nrm((L, G, C, N), (2 * N) ** -0.5),
        "s5_d": nrm((L, S5_W), 1.0),
        "s5_w_glu": nrm((L, S5_W, S5_W), S5_W ** -0.5),
        "rwkv_mu": jax.random.uniform(next(ks), (L, RWKV_SHIFT_W), f32),
        "rwkv_w0": jax.random.uniform(next(ks), (L, RWKV_W), f32, -5.0, 0.0),
        "rwkv_w_w2": nrm((L, DECAY_RANK, RWKV_W), 0.1),
        "rwkv_a0": nrm((L, RWKV_W), 0.1),
        "rwkv_w_a2": nrm((L, ICLR_RANK, RWKV_W), 0.1),
        "rwkv_k_k": 0.85 + nrm((L, RWKV_W), 0.02),
        "rwkv_k_a": 1.0 + nrm((L, RWKV_W), 0.02),
        "rwkv_r_k": nrm((L, RWKV_HEADS, RWKV_HEAD), 0.1),
        "rwkv_gn_w": 1.0 + nrm((L, RWKV_W), 0.05),
        "rwkv_gn_b": nrm((L, RWKV_W), 0.01),
        "pool_w": nrm((L, POOL_GROUPS, POOL_GW, POOL_GW), POOL_GW ** -0.5),
        "pool_scale": 1.0 + nrm((L, POOL_W), 0.1),
        "w_up_s5": nrm((L, S5_W, D), S5_W ** -0.5),
        "w_up_rwkv": nrm((L, RWKV_W, D), RWKV_W ** -0.5),
        "w_up_pool": nrm((L, POOL_W, D), POOL_W ** -0.5),
        "w_o": nrm((L, D, D), D ** -0.5),
    }

def reference(x_prompt, x_sample, state_s5_re, state_s5_im, state_rwkv, state_shift, state_pool,
              norm_pre, norm_post, w_in, s5_lam_re, s5_lam_im, s5_log_dt, s5_b_re, s5_b_im,
              s5_c_re, s5_c_im, s5_d, s5_w_glu, rwkv_mu, rwkv_w0, rwkv_w_w2, rwkv_a0, rwkv_w_a2,
              rwkv_k_k, rwkv_k_a, rwkv_r_k, rwkv_gn_w, rwkv_gn_b, pool_w, pool_scale,
              w_up_s5, w_up_rwkv, w_up_pool, w_o):
    f32 = jnp.float32
    xp, xs = x_prompt, x_sample
    bp = xp.shape[0]
    outs_p = [[] for _ in range(5)]
    outs_s = [[] for _ in range(5)]
    for l in range(DEPTH):
        wl = (norm_pre[l], norm_post[l], w_in[l], s5_lam_re[l], s5_lam_im[l], s5_log_dt[l],
              s5_b_re[l], s5_b_im[l], s5_c_re[l], s5_c_im[l], s5_d[l], s5_w_glu[l],
              rwkv_mu[l], rwkv_w0[l], rwkv_w_w2[l], rwkv_a0[l], rwkv_w_a2[l], rwkv_k_k[l], rwkv_k_a[l],
              rwkv_r_k[l], rwkv_gn_w[l], rwkv_gn_b[l], pool_w[l], pool_scale[l],
              w_up_s5[l], w_up_rwkv[l], w_up_pool[l], w_o[l])
        zeros_p = (jnp.zeros((bp, S5_GROUPS, S5_STATE), f32), jnp.zeros((bp, S5_GROUPS, S5_STATE), f32),
                   jnp.zeros((bp, RWKV_HEADS, RWKV_HEAD, RWKV_HEAD), f32),
                   jnp.zeros((bp, RWKV_SHIFT_W), xp.dtype), jnp.zeros((bp, POOL_BUF, POOL_W), xp.dtype))
        xp, *new_p = trunk_layer(xp, *zeros_p, 0, *wl)
        xs, *new_s = trunk_layer(xs, state_s5_re[l], state_s5_im[l], state_rwkv[l], state_shift[l],
                                 state_pool[l], PAST_LEN, *wl)
        for lst, val in zip(outs_p, new_p):
            lst.append(val)
        for lst, val in zip(outs_s, new_s):
            lst.append(val)
    p_s5_re, p_s5_im, p_rwkv, p_shift, p_pool = [jnp.stack(v) for v in outs_p]
    s_s5_re, s_s5_im, s_rwkv, s_shift, s_pool = [jnp.stack(v) for v in outs_s]
    return (xp, xs, p_s5_re, p_s5_im, p_rwkv, p_shift, p_pool, s_s5_re, s_s5_im, s_rwkv, s_shift, s_pool)


_drawn_inputs = setup_inputs


def setup_inputs(seed=0):
    import zlib

    import numpy as np

    out = dict(_drawn_inputs(seed))
    spreads = {}
    factors = {'s5_lam_re': 3.864,
     's5_c_re': 4.629,
     's5_c_im': 4.789,
     'rwkv_k_k': 4.178,
     'rwkv_k_a': 2.667,
     'rwkv_gn_b': 8.0}
    for name, (base, spread) in spreads.items():
        noise = np.random.default_rng([zlib.crc32(name.encode()), seed]).standard_normal(out[name].shape)
        drawn = base * np.exp(spread * noise) if base else spread * noise
        out[name] = __import__('jax').numpy.asarray(drawn.astype(out[name].dtype))
    for name, factor in factors.items():
        out[name] = (out[name] * factor).astype(out[name].dtype)
    return out
```

```python
from contextlib import ExitStack

import numpy as np

import concourse.bass as bass
from concourse import mybir

ALU = mybir.AluOpType
ACT = mybir.ActivationFunctionType
AX = mybir.AxisListType
F32 = mybir.dt.float32
F32R = mybir.dt.float32r

P = 128
D = 1024
KT = D // P
SEQ = 1024
NB, NS = 8, 8
NT = SEQ + NB * NS
W = 512
WB = W // P
H, HD = 8, 64
C = 64
RB = 13
G, GC, N5 = 32, 16, 64
L5 = 8
J5 = NT // L5
JP = SEQ // L5
WIN = (2, 4, 8, 16)
BUF = 15
TILES = SEQ // P
NIN = 57
B_S5X, B_S5Z, B_RW, B_RWZ, B_PLX, B_PLZ, B_GATE = 0, 4, 8, 21, 25, 29, 33
CH = [(0, 384), (384, 384), (768, 320)]
NORM_EPS, GN_EPS = 1e-6, 64e-5
DEC = 0.6065306597126334

MAGIC = 1.5 * 2.0 ** 23
_C2 = float(np.float32(np.round((2 * np.pi - 6.28125) * 2.0 ** 20) / 2.0 ** 20))
TURN = (6.28125, _C2, 2 * np.pi - 6.28125 - _C2)
PI_IN = 3.1415925
LN2 = float(np.log(2.0))
LN2_PARTS = (0.693359375, LN2 - 0.693359375)
EXP_FACT = (1.0, 2.0, 6.0, 24.0, 120.0, 720.0, 5040.0)

VECS = [("mu", 13), ("w0", 4), ("a0", 4), ("k_k", 4), ("k_a", 4), ("r_k", 4), ("gn_w", 4), ("gn_b", 4),
        ("pool_scale", 4), ("s5_d", 4)]
VAT, _n = {}, 0
for _name, _k in VECS:
    VAT[_name] = (_n, _k)
    _n += _k
NVEC = _n


class Chain:

    def __init__(self, eng, sem, base=0):
        self.eng, self.sem, self.base, self.n = eng, sem, base, 0

    def after(self, ins):
        ins.then_inc(self.sem, 1)
        self.n += 1

    def wait(self, back=0):
        self.eng.wait_ge(self.sem, self.base + (self.n - back))


def bc(ap, shape):
    return ap.to_broadcast(shape)


class Env:
    pass


def phase_setup(nc, io, e):
    with ExitStack() as ctx:
        sem = lambda n: ctx.enter_context(nc.semaphore(n))
        rows = ctx.enter_context(nc.sbuf_tensor("vec_rows", [NVEC, P], F32))
        shift = ctx.enter_context(nc.sbuf_tensor("shift_rows", [NB, RB * P], F32))
        ps = ctx.enter_context(nc.psum_tensor("setup_ps", [P, 512], F32))
        ps2 = ctx.enter_context(nc.psum_tensor("setup_ps2", [P, 512], F32))
        loaded, masks, flipped, made = sem("setup_loaded"), sem("setup_masks"), sem("setup_flipped"), sem("setup_made")
        ident_ready = sem("ident_ready")
        vsrc = {"mu": io["rwkv_mu"], "w0": io["rwkv_w0"], "a0": io["rwkv_a0"], "k_k": io["rwkv_k_k"],
                "k_a": io["rwkv_k_a"], "r_k": io["rwkv_r_k"].rearrange("l h n -> l (h n)"), "gn_w": io["rwkv_gn_w"],
                "gn_b": io["rwkv_gn_b"], "pool_scale": io["pool_scale"], "s5_d": io["s5_d"]}
        n_loads = len(VECS) + 3
        with nc.Block() as block:
            @block.sync
            def _(sp):
                for name, (at, k) in VAT.items():
                    sp.dma_start(rows[at:at + k, :], vsrc[name][0].rearrange("(b p) -> b p", p=P)).then_inc(loaded, 16)
                sp.dma_start(shift[:, :], io["state_shift"][0]).then_inc(loaded, 16)
                sp.dma_start(e.lora_w[0:64, :], io["rwkv_w_w2"][0]).then_inc(loaded, 16)
                sp.dma_start(e.lora_w[64:128, :], io["rwkv_w_a2"][0]).then_inc(loaded, 16)

            @block.gpsimd
            def _(pool):
                ch = Chain(pool, masks)

                def select(out, base, pattern, mult, fill=0.0, op=ALU.is_ge):
                    ch.wait()
                    ch.after(pool.affine_select(out=out, in_=out, compare_op=op, fill=fill, base=base,
                                                pattern=pattern, channel_multiplier=mult))

                for t, v in ((e.ident, 0.0), (e.ones_bd, 1.0), (e.lv, 0.0), (e.up_strict, 1.0), (e.up_incl, 1.0),
                             (e.pair_ts, 0.0), (e.pair_st, 0.0), (e.s_strict, 1.0), (e.s_incl, 1.0),
                             (e.keep_p, 1.0), (e.keep_s, 1.0), (e.seq_of, 1.0)):
                    ch.after(pool.memset(t, v))
                ch.wait()
                select(e.ident, 0, [[-1, P]], 1, 1.0, ALU.not_equal)
                ch.wait()
                pool.tensor_copy(e.ident_b[:, :], e.ident).then_inc(ident_ready, 1)
                bd = e.ones_bd.rearrange("p (q r) -> p q r", r=HD)
                select(bd, 0, [[-HD, 2], [0, HD]], 1)
                select(bd, HD - 1, [[HD, 2], [0, HD]], -1)
                for n in range(5):
                    b = 2 << n
                    v = e.lv[:, n, :].rearrange("p (q h r) -> p q h r", h=2, r=b)[:, :, 0, :]
                    ch.wait()
                    ch.after(pool.memset(v, 1.0))
                    select(v, -b, [[-2 * b, P // (2 * b)], [0, b]], 1)
                    select(v, 2 * b - 1, [[2 * b, P // (2 * b)], [0, b]], -1)
                for h0 in (0, C):
                    select(e.up_strict[h0:h0 + C, :], -1, [[1, C]], -1)
                    select(e.up_incl[h0:h0 + C, :], 0, [[1, C]], -1)
                    select(e.pair_ts[h0:h0 + C, :].rearrange("p (q h) -> p q h", h=2)[:, :, 0], -1, [[-2, C // 2]], 1, -1.0, ALU.not_equal)
                    select(e.pair_st[h0:h0 + C, :].rearrange("p (q h) -> p q h", h=2)[:, :, 1], 0, [[-2, C // 2]], 1, -1.0, ALU.not_equal)
                for m, off in ((e.s_strict, -1), (e.s_incl, 0)):
                    v = m.rearrange("p (q r) -> p q r", r=NS)
                    select(v, off, [[NS, NB], [1, NS]], -1)
                    select(v, 0, [[-NS, NB], [0, NS]], 1)
                    select(v, NS - 1, [[NS, NB], [0, NS]], -1)
                select(e.seq_of, 0, [[-NS, NB]], 1)
                select(e.seq_of, NS - 1, [[NS, NB]], -1)
                ch.wait()
                ch.after(pool.memset(e.keep_p.rearrange("p (q r) -> p q r", r=C)[:, :, 0:1], 0.0))
                ch.after(pool.memset(e.keep_s.rearrange("p (q r) -> p q r", r=NS)[:, :, 0:1], 0.0))
                ch.wait()

            @block.tensor
            def _(pe):
                pe.wait_ge(loaded, 16 * n_loads)
                pe.wait_ge(ident_ready, 1)
                pe.transpose(ps[:, 0:NVEC], rows[:, :], e.ident_b[0:NVEC, 0:NVEC]).then_inc(flipped, 1)
                for b in range(RB):
                    pe.transpose(ps2[:, b * NB:(b + 1) * NB], shift[:, b * P:(b + 1) * P],
                                 e.ident_b[0:NB, 0:NB]).then_inc(flipped, 1)

            @block.vector
            def _(dve):
                ch = Chain(dve, made)
                ch.after(dve.memset(e.eps[:, 0:1], NORM_EPS))
                ch.after(dve.memset(e.eps[:, 1:2], GN_EPS))
                dve.wait_ge(flipped, 1 + RB)
                ch.after(dve.tensor_copy(e.vec[:, :], ps[:, 0:NVEC]))
                ch.after(dve.tensor_copy(e.shiftT.rearrange("p r b -> p (r b)"), ps2[:, 0:RB * NB]))
                ch.wait()
                at = VAT["k_a"][0]
                ch.after(dve.tensor_scalar(e.one_minus_ka[:, :], e.vec[:, at:at + 4], -1.0, 1.0, ALU.mult, ALU.add))
                ch.wait()


def phase_norm(nc, io, e):
    with ExitStack() as ctx:
        sem = lambda n: ctx.enter_context(nc.semaphore(n))
        sb = lambda n, s, d=F32: ctx.enter_context(nc.sbuf_tensor(n, s, d))
        xt = sb("xt", [P, 3, D])
        xn = sb("xn", [P, 2, D])
        junk = sb("junk", [P, D])
        gpre_row = sb("gpre_row", [P, D])
        g_loaded = sem("g_loaded")
        ssum, root, rstd = sb("ssum", [P, 9]), sb("root", [P, 9]), sb("rstd", [P, 9])
        ps = [ctx.enter_context(nc.psum_tensor(f"hT{i}", [P, 512], F32)) for i in range(4)]
        x_loaded = [sem(f"x_loaded{i}") for i in range(3)]
        sq_done, root_done, rs_done, xn_done, flipped, hi_done, lo_done = [sem(n) for n in (
            "sq_done", "root_done", "rs_done", "xn_done", "h_flipped", "hi_done", "lo_done")]
        tiles = [(t * P, P if t < TILES else NB * NS) for t in range(TILES + 1)]
        with nc.Block() as block:
            @block.sync
            def _(sp):
                sp.dma_start(gpre_row[:, :], io["norm_pre"].to_broadcast((P, D))).then_inc(g_loaded, 16)
                for t, (at, n) in enumerate(tiles):
                    if t >= 3:
                        sp.wait_ge(xn_done, t - 2)
                        sp.wait_ge(sq_done, t - 2)
                    src = io["x_prompt"][0, at:at + n, :] if t < TILES else io["x_sample"].rearrange("b t d -> (b t) d")
                    sp.dma_start(xt[0:n, t % 3, :], src).then_inc(x_loaded[t % 3], 16)

            @block.scalar
            def _(act):
                def hi(t):
                    at, n = tiles[t]
                    act.wait_ge(flipped, t + 1)
                    for q in range(2):
                        v = ps[2 * (t % 2) + q][:, :].rearrange("p (k t) -> p k t", k=4)[:, :, 0:n]
                        act.activation(e.h_hi[:, 4 * q:4 * q + 4, at:at + n], v, ACT.Copy).then_inc(hi_done, 1)
                for t, (at, n) in enumerate(tiles):
                    act.wait_ge(x_loaded[t % 3], 16 * (t // 3 + 1))
                    if t:
                        act.wait_ge(sq_done, t)
                    act.activation(junk[0:n, :], xt[0:n, t % 3, :], ACT.Square, accum_out=ssum[0:n, t:t + 1]).then_inc(sq_done, 1)
                    act.wait_ge(sq_done, t + 1)
                    act.activation(root[0:n, t:t + 1], ssum[0:n, t:t + 1], ACT.Sqrt, scale=1.0 / D, bias=e.eps[0:n, 0:1]).then_inc(root_done, 1)
                    if t:
                        hi(t - 1)
                hi(len(tiles) - 1)

            @block.vector
            def _(dve):
                def lo(t):
                    at, n = tiles[t]
                    for q in range(2):
                        dve.wait_ge(hi_done, 2 * t + q + 1)
                        v = ps[2 * (t % 2) + q][:, :].rearrange("p (k t) -> p k t", k=4)[:, :, 0:n]
                        dve.tensor_tensor(e.h_lo[:, 4 * q:4 * q + 4, at:at + n], v,
                                          e.h_hi[:, 4 * q:4 * q + 4, at:at + n].bitcast(F32), ALU.subtract).then_inc(lo_done, 1)
                dve.wait_ge(g_loaded, 16)
                for t, (at, n) in enumerate(tiles):
                    dve.wait_ge(root_done, t + 1)
                    dve.reciprocal(rstd[0:n, t:t + 1], root[0:n, t:t + 1]).then_inc(rs_done, 1)
                    dve.wait_ge(rs_done, t + 1)
                    if t >= 2:
                        dve.wait_ge(flipped, t - 1)
                    dve.scalar_tensor_tensor(out=xn[0:n, t % 2, :], in0=xt[0:n, t % 3, :], scalar=rstd[0:n, t:t + 1],
                                             in1=gpre_row[0:n, :], op0=ALU.mult, op1=ALU.mult).then_inc(xn_done, 1)
                    if t:
                        lo(t - 1)
                lo(len(tiles) - 1)

            @block.tensor
            def _(pe):
                for t, (at, n) in enumerate(tiles):
                    pe.wait_ge(xn_done, t + 1)
                    if t >= 2:
                        pe.wait_ge(lo_done, 2 * (t - 1))
                    for k in range(KT):
                        mm = pe.transpose(ps[2 * (t % 2) + k // 4][:, (k % 4) * P:(k % 4) * P + n],
                                          xn[0:n, t % 2, k * P:(k + 1) * P], e.ident[0:n, 0:n])
                    mm.then_inc(flipped, 1)


def split_mm(pe, out, whi, wlo, xhi, xlo, first, last):
    pe.matmul(out, whi, xhi, start=first, stop=False)
    pe.matmul(out, whi, xlo, start=False, stop=False)
    return pe.matmul(out, wlo, xhi, start=False, stop=last)


def phase_project(nc, io, e):
    blocks = [B_RW + b for b in range(RB)] + [B_S5X + b for b in range(4)] + [B_PLX + b for b in range(4)]
    R = 3
    n_it = len(blocks) // R
    with ExitStack() as ctx:
        sem = lambda n: ctx.enter_context(nc.semaphore(n))
        sb = lambda n, s, d=F32: ctx.enter_context(nc.sbuf_tensor(n, s, d))
        wst = sb("wst", [P, R, KT, P])
        whi, wlo = sb("whi", [P, R, KT, P], F32R), sb("wlo", [P, R, KT, P], F32R)
        out = sb("proj_out", [P, R, NT + 1])
        ps = [ctx.enter_context(nc.psum_tensor(f"proj_ps{i}", [P, 512], F32)) for i in range(R)]
        w_loaded = [sem(f"pw_loaded{i}") for i in range(R)]
        stored = [sem(f"p_stored{i}") for i in range(R)]
        hi_done, lo_done, mm_done, ev_done, zero = [sem(n) for n in ("pw_hi", "pw_lo", "p_mm", "p_ev", "p_zero")]
        def store(sp, n):
            sp.wait_ge(ev_done, 3 * (n + 1))
            sp.dma_start(e.scratch[blocks[n]], out[:, n % R, :]).then_inc(stored[n % R], 16)

        with nc.Block() as block:
            @block.sync
            def _(sp):
                for n, b in enumerate(blocks):
                    if n >= R:
                        sp.wait_ge(lo_done, n - R + 1)
                    sp.dma_start(wst[:, n % R], io["w_in"][0, :, b * P:(b + 1) * P].rearrange("(k p) m -> p k m", p=P)).then_inc(w_loaded[n % R], 16)
                    if n >= R:
                        store(sp, n - R)
                for n in range(len(blocks) - R, len(blocks)):
                    store(sp, n)
                for r in range(R):
                    sp.wait_ge(stored[r], 16 * n_it)

            @block.gpsimd
            def _(pool):
                for r in range(R):
                    pool.memset(out[:, r, 0:1], 0.0).then_inc(zero, 1)
                with pool.Fori(0, n_it) as i:
                    for r in range(R):
                        pool.wait_ge(hi_done, i * R + (r + 1))
                        pool.tensor_tensor(wlo[:, r], wst[:, r], whi[:, r].bitcast(F32), ALU.subtract).then_inc(lo_done, 1)

            @block.vector
            def _(dve):
                def split(i, r):
                    dve.wait_ge(w_loaded[r], (i + 1) * 16)
                    dve.tensor_copy(whi[:, r], wst[:, r]).then_inc(hi_done, 1)
                for r in range(R):
                    split(0, r)
                with dve.Fori(1, n_it) as i:
                    for r in range(R):
                        dve.wait_ge(mm_done, (i - 1) * (3 * R) + 3 * (r + 1))
                        split(i, r)

            @block.tensor
            def _(pe):
                def body(i, first):
                    for r in range(R):
                        pe.wait_ge(lo_done, i * R + (r + 1))
                        for c, (at, n) in enumerate(CH):
                            if not (first and r == 0):
                                pe.wait_ge(ev_done, i * (3 * R) + (3 * r + c - 2))
                            for k in range(KT):
                                mm = split_mm(pe, ps[c][:, 0:n], whi[:, r, k], wlo[:, r, k], e.h_hi[:, k, at:at + n],
                                              e.h_lo[:, k, at:at + n], k == 0, k == KT - 1)
                            mm.then_inc(mm_done, 1)
                body(0, True)
                with pe.Fori(1, n_it) as i:
                    body(i, False)

            @block.scalar
            def _(act):
                def body(i, first):
                    for r in range(R):
                        if not first:
                            act.wait_ge(stored[r], i * 16)
                        for c, (at, n) in enumerate(CH):
                            act.wait_ge(mm_done, i * (3 * R) + (3 * r + c + 1))
                            act.activation(out[:, r, 1 + at:1 + at + n], ps[c][:, 0:n], ACT.Copy).then_inc(ev_done, 1)
                act.wait_ge(zero, R)
                body(0, True)
                with act.Fori(1, n_it) as i:
                    body(i, False)


def phase_states(nc, io, e):
    nq = NB * H // 2
    with ExitStack() as ctx:
        sem = lambda n: ctx.enter_context(nc.semaphore(n))
        rows = ctx.enter_context(nc.sbuf_tensor("state_rows", [P, nq, HD], F32))
        turned = ctx.enter_context(nc.sbuf_tensor("state_turned", [HD, NB * H, HD], F32))
        ps = [ctx.enter_context(nc.psum_tensor(f"st_ps{i}", [HD, 512], F32)) for i in range(2)]
        loaded, flipped, copied, stored = sem("st_loaded"), sem("st_flipped"), sem("st_copied"), sem("st_stored")
        with nc.Block() as block:
            @block.sync
            def _(sp):
                sp.dma_start(rows[:, :, :], io["state_rwkv"].rearrange("l b h v k -> (l b h v) k")
                             .rearrange("(q p) k -> p q k", p=P)).then_inc(loaded, 16)
                sp.wait_ge(copied, nq // 4)
                sp.dma_start(e.s0t_scr, turned[:, :, :]).then_inc(stored, 16)
                sp.wait_ge(stored, 16)

            @block.tensor
            def _(pe):
                pe.wait_ge(loaded, 16)
                for n in range(nq // 4):
                    if n >= 2:
                        pe.wait_ge(copied, n - 1)
                    for q in range(4):
                        mm = pe.transpose(ps[n % 2][:, q * P:(q + 1) * P], rows[:, 4 * n + q, :], e.ident)
                    mm.then_inc(flipped, 1)

            @block.vector
            def _(dve):
                dve.memset(e.s_a[:, :, :], 0.0)
                for n in range(nq // 4):
                    dve.wait_ge(flipped, n + 1)
                    dve.tensor_copy(turned[:, 8 * n:8 * n + 8, :].rearrange("k q v -> k (q v)"), ps[n % 2][:, :]).then_inc(copied, 1)
                dve.wait_ge(copied, nq // 4)


FILL_BLOCKS = ([B_S5Z + b for b in range(4)] + [B_RWZ + b for b in range(4)] + [B_PLZ + b for b in range(4)]
               + [B_GATE + b for b in range(24)])
PIECES = 4
BEFORE = {"lora": 14, "ssq": 19, "turn": 25, "A": 25, "X0": 31, "TX0": 32, "X1": 34, "TX1": 35, "X2": 36, "TX2": 37,
          "X3": 38, "TX3": 39, "X4": 40, "TX4": 41, "Y": 42, "GU": 43, "RM": 44, "S0": 45, "O": 45, "S1": 45, "ON": 46, "end": 48}


PROD = [((1, 2), 0), ((1, 2), 1), ((3, 5), 0), ((3, 5), 1), ((4, 0), 0)]
XB, TXB, XTB = (1, 2), (3, 5), (4, 0)


class Tile:

    def __init__(self, e, i, prompt):
        self.i, self.prompt = i, prompt
        self.T = P if prompt else NB * NS
        self.halves = (0, 1) if prompt else (0,)
        self.levels = 5 if prompt else 2
        self.strict = e.up_strict if prompt else e.s_strict
        self.incl = e.up_incl if prompt else e.s_incl
        self.keep = e.keep_p if prompt else e.keep_s
        self.step = C if prompt else NS

    def fv(self, t):
        return t[:, 0:4 * self.T].rearrange("p (b t) -> p b t", b=4)


def phase_rwkv(nc, io, e):
    with ExitStack() as ctx:
        sem = lambda n: nc.alloc_semaphore(name=n)
        sb = lambda n, s, d=F32: ctx.enter_context(nc.sbuf_tensor(n, s, d))
        wst, stage = sb("fw", [P, 2, KT, P]), sb("f_out", [P, 3, CH[0][1]])
        whi, wlo = sb("fw_hi", [P, 2, KT, P], F32R), sb("fw_lo", [P, 2, KT, P], F32R)
        fps = [ctx.enter_context(nc.psum_tensor(f"f_ps{i}", [P, 512], F32)) for i in range(2)]
        fw_loaded = [sem(f"fw_loaded{i}") for i in range(2)]
        f_stored = [sem(f"f_stored{i}") for i in range(3)]
        fw_hi, fw_lo, f_mm, f_free = sem("fw_hi"), sem("fw_lo"), sem("f_mm"), sem("f_bank_free")
        raw, dif, pm = sb("raw", [P, RB, P + 1]), sb("dif", [P, RB, P]), sb("pm", [P, RB, P])
        fm = lambda n: sb(n, [P, 4 * P])[:, :]
        tw = sb("tw", [64, P])
        sg, av, cs, pr, pi, kk0, sq, nr, kk, kf, bonus, y_tile = (fm(n) for n in (
            "sg_on", "a_bC", "cs_yv", "decay_prod", "decay_inv", "kk0_b", "sq_alpha_bonus", "norm_kC", "kk", "kf_gsq", "rk_bonus", "y_tile"))
        bb, bC, kC, alpha, bt, yv = kk0, av, nr, sq, sq, cs
        dflat = dif[:, :, :].rearrange("p r t -> p (r t)")
        beta, kappa, rho = (dflat[:, 4 * P * n:4 * P * (n + 1)] for n in range(3))
        ay, vt = sb("alpha_y", [P, H, P]), sb("v_t", [P, H, HD])
        bCt, kCt = sb("bC_t", [P, H, HD]), sb("kC_t", [P, H, HD])
        n_g, n_u = sb("neg_g", [P, H, HD]), sb("neg_u", [P, H, HD])
        ab_t, ak_t, rb_t, rk_t = (sb(n, [P, H, P]) for n in ("ab_t", "ak_t", "rb_t", "rk_t"))
        t_m, t_t, x_m = sb("t_m", [P, H, P]), sb("t_t", [P, H, P]), sb("x_m", [P, H, P])
        tmp = y_tile.rearrange("p (h k) -> p h k", h=H)
        rp = pi.rearrange("p (b t) -> p b t", b=4)
        m_c, dpc = sb("m_c", [P, 2, 4, P]), sb("dpc", [P, 2, 4, P])
        s_b = sb("s_b", [P, 4, HD])
        s_bd, s_ad = x_m[:, 0:4, :], sb("s_ad", [P, 4, P])
        gsum, gneg, gvar, groot, grs = (sb(n, [P, H]) for n in ("gsum", "gneg", "gvar", "groot", "grs"))
        cen = tmp
        gsq, on = (x.rearrange("p (h k) -> p h k", h=H) for x in (kf, sg))
        Q = [ctx.enter_context(nc.psum_tensor(f"q{i}", [P, 512], F32)) for i in range(6)]
        ev = {n: sem("r_" + n) for n in (
            "raw_loaded", "pm", "tanh", "lora_mm", "gates", "sq", "ssq_mm", "floor", "root", "cs", "decay", "kf", "feat",
            "bonus", "turned", "turned_sb", "prod_mm", "t_init", "prod_sb", "x_mm", "x_sb", "tx_mm", "tx_sb", "y_mm", "y_sb",
            "gu_mm", "gu_sb", "rm_mm", "rp_sb", "dpc", "m_sb", "s0_mm", "s0_sb", "o_mm", "s1_mm", "s1_sb", "cen", "gsq",
            "gvar", "groot", "on", "on_mm", "y_out", "y_stored", "zeroed",
            "pc0", "dpcs", "rpm", "mask_sb", "mz_mm", "mz_sb", "sn_mm", "sn_sb")}
        sn_out = [sem(f"r_sn_out{i}") for i in range(2)]
        s0_loaded = [sem(f"r_s0_loaded{i}") for i in range(2)]
        v = e.vec

        def vb(name, T, blocks=None):
            at, k = VAT[name]
            return v[:, at:at + k].rearrange("p (b o) -> p b o", o=1).to_broadcast((P, k, T))

        def pm_of(t, q):
            return pm[:, 4 * q:4 * q + 4, 0:t.T]

        def e4(t, q):
            return q[0:t.T, 0:4 * t.T].rearrange("p (h t) -> p h t", h=4)

        def tx_at(t, n):
            return (t.i * 5 + n) * 4

        snew_b = m_c[0:HD, :, :, :].rearrange("p c q t -> p c (q t)").rearrange("p c (b k) -> p c b k", k=HD)
        two = lambda x, r: x[0:HD, :, :].rearrange("p h t -> p (h t)")[:, 512 * r:512 * r + 512].rearrange("p (q k) -> p q k", k=HD)
        rpm = [two(x, r) for x in (ab_t, ak_t, t_m, t_t) for r in range(2)]
        kcm, mz = [two(x_m, r) for r in range(2)], [two(ay, r) for r in range(2)]
        bcm = [dpc[0:HD, r].rearrange("p q t -> p (q t)").rearrange("p (q k) -> p q k", k=HD) for r in range(2)]
        dps, rps = (x[0:HD].rearrange("p (q k) -> p q k", k=HD) for x in (kk, pi))
        pc0 = sb("pc0", [HD, H, NB])[:, :, :]
        s0t = raw[0:HD].rearrange("p r t -> p (r t)")[:, 0:1024].rearrange("p (c q k) -> p c q k", c=2, k=HD)

        with nc.Block() as block:
            @block.sync
            def _(sp):
                def load_w(g):
                    if g >= 2:
                        sp.wait_ge(fw_lo, g - 1)
                    b = FILL_BLOCKS[g]
                    sp.dma_start(wst[:, g % 2], io["w_in"][0, :, b * P:(b + 1) * P].rearrange("(k p) m -> p k m", p=P)).then_inc(fw_loaded[g % 2], 16)

                def load_raw(i):
                    if i:
                        sp.wait_ge(ev["pm"], i)
                    src = e.scratch[B_RW:B_RW + RB].rearrange("b p t -> p b t")
                    if i < TILES:
                        sp.dma_start(raw[:, :, :], src[:, :, i * P:i * P + P + 1]).then_inc(ev["raw_loaded"], 16)
                    else:
                        sp.dma_start(raw[:, :, 0:NB * NS], src[:, :, 1 + SEQ:1 + NT]).then_inc(ev["raw_loaded"], 16)

                def store(g):
                    for c, (at, n) in enumerate(CH):
                        sp.wait_ge(f_free, 2 + 3 * g + c + 1)
                        sp.dma_start(e.scratch[FILL_BLOCKS[g], :, 1 + at:1 + at + n], stage[:, c, 0:n]).then_inc(f_stored[c], 16)

                def store_y(i):
                    sp.wait_ge(ev["y_out"], i + 1)
                    n = P if i < TILES else NB * NS
                    sp.dma_start(e.y_scr[1, :, :, i * P:i * P + n], y_tile[:, 0:4 * n].rearrange("p (b t) -> p b t", b=4)).then_inc(ev["y_stored"], 16)

                def new_out(h):
                    sp.wait_ge(ev["sn_sb"], h + 1)
                    sp.dma_start(e.outs["s_rwkv"][0, :, h].rearrange("b v k -> v b k"), snew_b[:, h % 2]).then_inc(sn_out[h % 2], 16)

                def load_s0(h):
                    sp.dma_start(s0t[:, h % 2], e.s0t_scr.rearrange("k (b h) v -> k h b v", h=H)[:, h]).then_inc(s0_loaded[h % 2], 16)

                load_raw(0)
                n = len(FILL_BLOCKS)
                load_w(0)
                load_w(1)
                for g in range(n):
                    if g + 2 < n:
                        load_w(g + 2)
                    if g % 4 == 1 and g // 4 < TILES:
                        load_raw(g // 4 + 1)
                    if g % 4 == 0 and g:
                        store_y(g // 4 - 1)
                    if g == n - 2:
                        sp.wait_ge(ev["pm"], TILES + 1)
                        load_s0(0)
                        load_s0(1)
                    if g < n - 1:
                        store(g)
                for h in range(2, H):
                    sp.wait_ge(ev["sn_mm"], h - 1)
                    load_s0(h)
                    new_out(h - 2)
                new_out(H - 2)
                new_out(H - 1)
                store(n - 1)
                for r in range(3):
                    sp.wait_ge(f_stored[r], 16 * n)
                store_y(TILES)
                sp.wait_ge(ev["y_stored"], 16 * (TILES + 1))
                for r in range(2):
                    sp.wait_ge(sn_out[r], 16 * (H // 2))

            @block.gpsimd
            def _(pool):
                for z in (ab_t, ak_t, rb_t, rk_t, t_m, t_t, s_ad):
                    pool.memset(z[:, :, :], 0.0).then_inc(ev["zeroed"], 1)

                def lo(g_of, r, count):
                    pool.wait_ge(fw_hi, count)
                    pool.tensor_tensor(wlo[:, r], wst[:, r], whi[:, r].bitcast(F32), ALU.subtract).then_inc(fw_lo, 1)

                lo(0, 0, 1)
                lo(1, 1, 2)

                def body(t):
                    i = t.i
                    fv = t.fv
                    n_lo = [0]

                    def lo_next():
                        if t.prompt or n_lo[0] < 2:
                            lo(None, n_lo[0] % 2, i * 4 + (3 + n_lo[0]))
                        n_lo[0] += 1
                    lo_next()
                    pool.wait_ge(ev["kf"], i + 1)
                    pool.tensor_tensor(fv(bonus), pm_of(t, 0), fv(kf), ALU.mult).then_inc(ev["bonus"], 1)
                    pool.wait_ge(ev["bonus"], i * 2 + 1)
                    pool.tensor_tensor(fv(bonus), fv(bonus), vb("r_k", t.T), ALU.mult).then_inc(ev["bonus"], 1)
                    pool.wait_ge(ev["decay"], i * 2 + 2)
                    if t.prompt:
                        for c in (0, 1):
                            pool.tensor_tensor(dpc[:, c], e.ident.rearrange("p (o t) -> p o t", o=1).to_broadcast((P, 4, P)),
                                               fv(pr)[:, :, C * c + C - 1:C * c + C].to_broadcast((P, 4, P)), ALU.mult).then_inc(ev["dpc"], 1)
                    lo_next()
                    lo_next()
                    lo_next()

                with pool.Fori(0, TILES) as i:
                    body(Tile(e, i, True))
                body(Tile(e, TILES, False))

            @block.scalar
            def _(act):
                def hi(r, count_loaded):
                    act.wait_ge(fw_loaded[r], count_loaded)
                    act.activation(whi[:, r], wst[:, r], ACT.Copy).then_inc(fw_hi, 1)
                hi(0, 16)
                hi(1, 16)
                act.sem_inc(f_free, 2)

                def body(t):
                    i, fv, T = t.i, t.fv, t.T
                    done = [0]

                    def evacuate(stage_name):
                        while done[0] < BEFORE[stage_name] // PIECES:
                            u = done[0]
                            r, (at, n) = (u // 3) % 2, CH[u % 3]
                            if not (t.first and u < 3):
                                act.wait_ge(f_stored[u % 3], (i * 4 + u // 3) * 16)
                            act.wait_ge(f_mm, i * 12 + (u + 1))
                            act.activation(stage[:, u % 3, 0:n], fps[u % 2][:, 0:n], ACT.Copy).then_inc(f_free, 1)
                            if u % 3 == 2 and (t.prompt or u < 6):
                                hi(r, (i * 2 + (u // 6 + 2)) * 16)
                            done[0] += 1

                    act.wait_ge(ev["pm"], i + 1)
                    act.activation(tw[:, 0:T], pm[0:64, 12, 0:T], ACT.Tanh).then_inc(ev["tanh"], 1)
                    evacuate("lora")
                    act.wait_ge(ev["lora_mm"], i + 1)
                    for b in range(4):
                        for q, (dst, name) in enumerate(((sg, "w0"), (av, "a0"))):
                            at = VAT[name][0] + b
                            act.activation(fv(dst)[:, b], Q[q][:, b * T:(b + 1) * T], ACT.Sigmoid,
                                           bias=v[:, at:at + 1]).then_inc(ev["gates"], 1)
                    act.wait_ge(ev["cs"], i + 1)
                    act.activation(pr[:, 0:4 * T], cs[:, 0:4 * T], ACT.Exp, scale=-DEC).then_inc(ev["decay"], 1)
                    act.activation(pi[:, 0:4 * T], cs[:, 0:4 * T], ACT.Exp, scale=DEC).then_inc(ev["decay"], 1)
                    evacuate("ssq")
                    act.wait_ge(ev["floor"], i + 1)
                    act.activation(nr[:, 0:4 * T], nr[:, 0:4 * T], ACT.Sqrt).then_inc(ev["root"], 1)
                    evacuate("turn")
                    for q, (bank, dst) in enumerate(((4, vt), (3, None), (5, bCt), (0, kCt))):
                        act.wait_ge(ev["turned"], i * 4 + (q + 1))
                        d = ay[0:T, :, 0:HD] if dst is None else dst[0:T]
                        act.activation(d, Q[bank][0:T, :].rearrange("p (h k) -> p h k", h=H), ACT.Copy).then_inc(ev["turned_sb"], 1)
                    evacuate("Y")
                    act.wait_ge(ev["y_mm"], i + 1)
                    act.activation(ay[0:T, :, HD:P], Q[1][0:T, :].rearrange("p (h k) -> p h k", h=H), ACT.Copy).then_inc(ev["y_sb"], 1)
                    for q in range(2):
                        act.wait_ge(ev["gu_mm"], i * 2 + (q + 1))
                        src = Q[TXB[q]][0:T, :].rearrange("p (h g k) -> p g h k", h=4, g=2)
                        act.activation(n_g[0:T, 4 * q:4 * q + 4, :], src[:, 0], ACT.Copy, scale=-1.0).then_inc(ev["gu_sb"], 1)
                        act.activation(n_u[0:T, 4 * q:4 * q + 4, :], src[:, 1], ACT.Copy, scale=-1.0).then_inc(ev["gu_sb"], 1)
                    evacuate("O")
                    if not t.prompt:
                        for h in range(H):
                            act.wait_ge(ev["sn_mm"], h + 1)
                            if h >= 2:
                                act.wait_ge(sn_out[h % 2], 16 * (h // 2))
                            act.activation(snew_b[:, h % 2], Q[TXB[h % 2]][0:HD, :].rearrange("p (b k) -> p b k", k=HD), ACT.Copy).then_inc(ev["sn_sb"], 1)
                    act.wait_ge(ev["cen"], i + 1)
                    act.activation(gsq[0:T], cen[0:T], ACT.Square).then_inc(ev["gsq"], 1)
                    act.wait_ge(ev["gvar"], i + 1)
                    act.activation(groot[0:T, :], gvar[0:T, :], ACT.Sqrt, scale=1.0 / HD, bias=e.eps[0:T, 1:2]).then_inc(ev["groot"], 1)
                    evacuate("end")

                t0 = Tile(e, 0, True)
                t0.first = True
                body(t0)
                with act.Fori(1, TILES) as i:
                    t = Tile(e, i, True)
                    t.first = False
                    body(t)
                t = Tile(e, TILES, False)
                t.first = False
                body(t)

            @block.vector
            def _(dve):
                ch_sem = sem("r_vec_chain")
                per_tile = [0]

                def body(t, base):
                    i, fv, T, step = t.i, t.fv, t.T, t.step
                    ch = Chain(dve, ch_sem, base)
                    tt = dve.tensor_tensor
                    dve.wait_ge(ev["raw_loaded"], i * 16 + 16)
                    if t.prompt:
                        cur = raw[:, :, 1:P + 1]
                        ch.after(tt(dif[:, :, :], raw[:, :, 0:P], cur, ALU.subtract))
                    else:
                        cur = raw[:, :, 0:T]
                        c4 = cur.rearrange("p r (b s) -> p r b s", s=NS)
                        d4 = dif[:, :, 0:T].rearrange("p r (b s) -> p r b s", s=NS)
                        ch.after(tt(d4[:, :, :, 1:NS], c4[:, :, :, 0:NS - 1], c4[:, :, :, 1:NS], ALU.subtract))
                        ch.after(tt(d4[:, :, :, 0], e.shiftT, c4[:, :, :, 0], ALU.subtract))
                    ch.wait()
                    ch.after(tt(dif[:, :, 0:T], dif[:, :, 0:T], vb("mu", T), ALU.mult))
                    ch.wait()
                    tt(pm[:, :, 0:T], dif[:, :, 0:T], cur, ALU.add).then_inc(ev["pm"], 1)
                    dve.wait_ge(ev["pm"], i + 1)
                    ch.after(tt(fv(kk0), pm_of(t, 1), vb("k_k", T), ALU.mult))
                    ch.wait()
                    tt(sq[:, 0:4 * T], kk0[:, 0:4 * T], kk0[:, 0:4 * T], ALU.mult).then_inc(ev["sq"], 1)
                    dve.wait_ge(ev["gates"], i * 8 + 8)
                    dve.tensor_tensor_scan(cs[:, 0:4 * T], t.keep, sg[:, 0:4 * T], 0.0, ALU.mult, ALU.add).then_inc(ev["cs"], 1)
                    for b in range(4):
                        at = VAT["k_a"][0] + b
                        ch.after(dve.tensor_scalar(fv(kf)[:, b], fv(av)[:, b], v[:, at:at + 1], e.one_minus_ka[:, b:b + 1], ALU.mult, ALU.add))
                    ch.wait()
                    tt(fv(kf), fv(kf), pm_of(t, 1), ALU.mult).then_inc(ev["kf"], 1)
                    dve.wait_ge(ev["ssq_mm"], i + 1)
                    dve.tensor_scalar(nr[:, 0:4 * T], Q[2][:, 0:4 * T], 1e-24, None, ALU.max).then_inc(ev["floor"], 1)
                    dve.wait_ge(ev["decay"], i * 2 + 2)
                    dve.wait_ge(ev["kf"], i + 1)
                    ch.after(tt(kappa[:, 0:4 * T], kf[:, 0:4 * T], pi[:, 0:4 * T], ALU.mult))
                    ch.after(tt(fv(rho), pm_of(t, 0), fv(pr), ALU.mult))
                    dve.wait_ge(ev["root"], i + 1)
                    ch.after(dve.reciprocal(nr[:, 0:4 * T], nr[:, 0:4 * T]))
                    ch.wait()
                    ch.after(tt(kk[:, 0:4 * T], kk0[:, 0:4 * T], nr[:, 0:4 * T], ALU.mult))
                    ch.wait()
                    ch.after(tt(bb[:, 0:4 * T], kk[:, 0:4 * T], av[:, 0:4 * T], ALU.mult))
                    q4 = lambda x: x[:, 0:4 * T].rearrange("p (q s) -> p q s", s=step)
                    ch.after(tt(q4(alpha)[:, :, 1:step], q4(kk)[:, :, 1:step], q4(pr)[:, :, 0:step - 1], ALU.mult))
                    dve.tensor_copy(q4(alpha)[:, :, 0:1], q4(kk)[:, :, 0:1]).then_inc(ev["feat"], 1)
                    ch.wait()
                    tt(beta[:, 0:4 * T], bb[:, 0:4 * T], pi[:, 0:4 * T], ALU.mult).then_inc(ev["feat"], 1)
                    dve.wait_ge(ev["feat"], i * 4 + 2)
                    pend = q4(pr)[:, :, step - 1:step].to_broadcast((P, 4 * T // step, step))
                    tt(q4(bC), q4(beta), pend, ALU.mult).then_inc(ev["feat"], 1)
                    tt(q4(kC), q4(kappa), pend, ALU.mult).then_inc(ev["feat"], 1)
                    def prod(n, par, lo_, cnt):
                        banks, z = PROD[n]
                        return Q[banks[par]][lo_:lo_ + cnt, 256 * z:256 * z + 256].rearrange("p (h t) -> p h t", h=4)
                    mb = lambda m, lo_, n: m[lo_:lo_ + n, :].rearrange("p (o t) -> p o t", o=1).to_broadcast((n, 4, C))
                    half = lambda x, par: x.rearrange("p (b o) t -> p b o t", o=2)[:, :, par]
                    blk = lambda x, c: x[C * c:C * c + C, :, C * c:C * c + C]
                    if t.first:
                        dve.wait_ge(ev["zeroed"], 7)
                    else:
                        dve.wait_ge(ev["y_stored"], i * 16)
                    for n, (mask, dst) in enumerate(((e.pair_ts, t_m), (e.pair_st, t_t))):
                        if n == 0:
                            dve.wait_ge(ev["prod_mm"], i * 5 + 2)
                        for par in (0, 1):
                            ch.after(tt(half(tmp[0:T], par), prod(n, par, 0, T), mb(mask, 0, T), ALU.mult))
                        if n == 1:
                            for c in t.halves:
                                for par in (0, 1):
                                    ch.after(tt(half(blk(ab_t, c), par), prod(n, par, C * c, C), mb(t.strict, C * c, C), ALU.mult))
                        ch.wait()
                        for c in t.halves:
                            idb = e.ident[C * c:C * c + C, C * c:C * c + C].rearrange("p (o t) -> p o t", o=1).to_broadcast((C, H, C))
                            ins = tt(blk(dst, c), tmp[C * c:C * c + C], idb, ALU.add)
                            if n == 1 and c == t.halves[-1]:
                                ins.then_inc(ev["t_init"], 1)
                            else:
                                ch.after(ins)
                        ch.wait()
                    dve.wait_ge(ev["t_init"], i + 1)
                    for n, (dst, m) in enumerate(((ak_t, t.strict), (rk_t, t.incl), (rb_t, t.incl)), 2):
                        dve.wait_ge(ev["prod_mm"], i * 5 + (4, 5, 5)[n - 2])
                        for c in t.halves:
                            for par in (0, 1):
                                ins = tt(half(blk(dst, c), par), prod(n, par, C * c, C), mb(m, C * c, C), ALU.mult)
                                if c == t.halves[-1] and par:
                                    ins.then_inc(ev["prod_sb"], 1)
                                else:
                                    ch.after(ins)
                    for n in range(t.levels):
                        full = n < 4
                        last = n == t.levels - 1
                        for q in range(2):
                            dve.wait_ge(ev["x_mm"], (i * 5 + n) * 2 + q + 1)
                            tt(x_m[0:T, 4 * q:4 * q + 4, 0:T], e4(t, Q[XB[q]]), e.lv[0:T, n:n + 1, 0:T].to_broadcast((T, 4, T)), ALU.mult).then_inc(ev["x_sb"], 1)
                        for q in range(2):
                            dve.wait_ge(ev["tx_mm"], tx_at(t, n) + 2 * q + 1)
                            tt(t_m[0:T, 4 * q:4 * q + 4, 0:T], t_m[0:T, 4 * q:4 * q + 4, 0:T], e4(t, Q[TXB[q]]), ALU.subtract).then_inc(ev["tx_sb"], 1)
                            dve.wait_ge(ev["tx_mm"], tx_at(t, n) + 2 * q + 2)
                            tt(t_t[0:T, 4 * q:4 * q + 4, 0:T], t_t[0:T, 4 * q:4 * q + 4, 0:T], e4(t, Q[XTB[q]]), ALU.subtract).then_inc(ev["tx_sb"], 1)
                        dve.wait_ge(ev["tx_sb"], tx_at(t, n) + 4)
                    dve.wait_ge(ev["rm_mm"], i * 3 + 1)
                    if t.prompt:
                        tt(rp[:, :, :], Q[4][:, :].rearrange("p (b t) -> p b t", b=4), fv(rho), ALU.add).then_inc(ev["rp_sb"], 1)
                        for c in (0, 1):
                            dve.wait_ge(ev["rm_mm"], i * 3 + (2 + c))
                            ch.after(tt(m_c[:, c], Q[1 + c][:, :].rearrange("p (b t) -> p b t", b=4),
                                        e.ones_bd.rearrange("p (o t) -> p o t", o=1).to_broadcast((P, 4, P)), ALU.mult))
                            ch.wait()
                            dve.wait_ge(ev["dpc"], i * 2 + (c + 1))
                            tt(m_c[:, c], m_c[:, c], dpc[:, c], ALU.add).then_inc(ev["m_sb"], 1)
                        dve.wait_ge(ev["s0_mm"], i + 1)
                        new_s(s_b, s_bd, 3, ev["s0_sb"], ch)
                    else:
                        sample_states(t, ch)
                    dve.wait_ge(ev["o_mm"], i + 1)
                    o = Q[0][0:T, :].rearrange("p (h k) -> p h k", h=H)
                    b8 = lambda x: x[0:T, :].rearrange("p (h o) -> p h o", o=1).to_broadcast((T, H, HD))
                    ch.after(dve.tensor_reduce(gsum[0:T, :], o, AX.X, ALU.add))
                    ch.wait()
                    ch.after(dve.tensor_scalar(gneg[0:T, :], gsum[0:T, :], -1.0 / HD, None, ALU.mult))
                    ch.wait()
                    tt(cen[0:T], o, b8(gneg), ALU.add).then_inc(ev["cen"], 1)
                    if t.prompt:
                        dve.wait_ge(ev["s1_mm"], i + 1)
                        new_s(e.s_a, s_ad, 5, ev["s1_sb"], ch)
                    dve.wait_ge(ev["gsq"], i + 1)
                    dve.tensor_reduce(gvar[0:T, :], gsq[0:T], AX.X, ALU.add).then_inc(ev["gvar"], 1)
                    dve.wait_ge(ev["groot"], i + 1)
                    ch.after(dve.reciprocal(grs[0:T, :], groot[0:T, :]))
                    ch.wait()
                    tt(on[0:T], cen[0:T], b8(grs), ALU.mult).then_inc(ev["on"], 1)
                    ch.after(tt(fv(bt), Q[4][:, 0:4 * T].rearrange("p (b t) -> p b t", b=4), pm_of(t, 2), ALU.mult))
                    dve.wait_ge(ev["on_mm"], i + 1)
                    for b in range(4):
                        gw, gb = VAT["gn_w"][0] + b, VAT["gn_b"][0] + b
                        ch.after(dve.tensor_scalar(fv(yv)[:, b], Q[1][:, b * T:(b + 1) * T], v[:, gw:gw + 1], v[:, gb:gb + 1], ALU.mult, ALU.add))
                    ch.wait()
                    tt(y_tile[:, 0:4 * T], yv[:, 0:4 * T], bt[:, 0:4 * T], ALU.add).then_inc(ev["y_out"], 1)
                    dve.wait_ge(ev["y_out"], i + 1)
                    return ch.n

                def new_s(dst, dst_d, bank, done, ch):
                    src = Q[bank][:, 0:256].rearrange("p (b k) -> p b k", b=4)
                    for par in (0, 1):
                        h0 = slice(HD * par, HD * par + HD)
                        ch.after(dve.tensor_copy(dst_d[h0, :, h0], src[h0]))
                    ch.wait()
                    dve.tensor_copy(dst[:, :, :], src).then_inc(done, 1)

                def sample_states(t, ch):
                    tt = dve.tensor_tensor
                    T = t.T
                    pe_ = pr[:, 0:4 * T].rearrange("p (b q s) -> p b q s", b=4, s=NS)[:, :, :, NS - 1]
                    pc = pc0.rearrange("p (b o) q -> p b o q", o=2)
                    ch.after(dve.tensor_copy(pc[:, :, 0, :], pe_[0:HD]))
                    ch.after(dve.tensor_copy(pc[:, :, 1, :], pe_[HD:P]))
                    r4 = Q[4][0:HD, :].rearrange("p (b o t) -> p b o t", b=4, o=2)
                    rs = rps.rearrange("p (b o) t -> p b o t", o=2)
                    ch.after(tt(rs[:, :, 0], r4[:, :, 0], t.fv(rho)[0:HD], ALU.add))
                    ch.after(tt(rs[:, :, 1], r4[:, :, 1], t.fv(rho)[HD:P], ALU.add))
                    ch.wait()
                    for x in range(NB):
                        ch.after(dve.memset(rpm[x], 0.0))
                    ch.wait()
                    for x in range(NB):
                        dve.tensor_copy(rpm[x][:, :, NS * x:NS * x + NS], rps[:, :, NS * x:NS * x + NS]).then_inc(ev["rpm"], 1)
                    for h in range(H):
                        r = h % 2
                        sel = e.seq_of.rearrange("p (q o) -> p q o", o=1).to_broadcast((T, NB, HD))
                        if h >= 2:
                            dve.wait_ge(ev["sn_mm"], h - 1)
                        tt(bcm[r], sel, bCt[0:T, h:h + 1, :].to_broadcast((T, NB, HD)), ALU.mult).then_inc(ev["mask_sb"], 1)
                        tt(kcm[r], sel, kCt[0:T, h:h + 1, :].to_broadcast((T, NB, HD)), ALU.mult).then_inc(ev["mask_sb"], 1)
                        ch.after(tt(dps, e.ident[0:HD, 0:HD].rearrange("p (o k) -> p o k", o=1).to_broadcast((HD, NB, HD)),
                                    pc0[:, h, :].rearrange("p (q o) -> p q o", o=1).to_broadcast((HD, NB, HD)), ALU.mult))
                        ch.wait()
                        dve.wait_ge(ev["mz_mm"], h + 1)
                        ins = tt(mz[r], Q[1 + r][0:HD, :].rearrange("p (q k) -> p q k", k=HD), dps, ALU.add)
                        ins.then_inc(ev["mz_sb"], 1)
                        dve.wait_ge(ev["mz_sb"], h + 1)

                t0 = Tile(e, 0, True)
                t0.first = True
                k = body(t0, 0)
                with dve.Fori(1, TILES) as i:
                    t = Tile(e, i, True)
                    t.first = False
                    assert body(t, i * k) == k
                t = Tile(e, TILES, False)
                t.first = False
                body(t, TILES * k)

            @block.tensor
            def _(pe):
                def body(t):
                    i, fv, T = t.i, t.fv, t.T
                    issued = [0]

                    def fill(stage_name):
                        while issued[0] < BEFORE[stage_name]:
                            u, part = divmod(issued[0], PIECES)
                            r, (at, n) = (u // 3) % 2, CH[u % 3]
                            if part == 0:
                                if u % 3 == 0:
                                    pe.wait_ge(fw_lo, i * 4 + (u // 3 + 1))
                                pe.wait_ge(f_free, i * 12 + (u + 1))
                            for k in range(2 * part, 2 * part + 2):
                                mm = split_mm(pe, fps[u % 2][:, 0:n], whi[:, r, k], wlo[:, r, k], e.h_hi[:, k, at:at + n],
                                              e.h_lo[:, k, at:at + n], k == 0, k == KT - 1)
                            if part == PIECES - 1:
                                mm.then_inc(f_mm, 1)
                            issued[0] += 1

                    mm_ = pe.matmul

                    def settle(bank):
                        mm_(Q[bank][:, 511:512], e.ident, e.ident[:, 0:1], start=True, stop=True)

                    fill("lora")
                    pe.wait_ge(ev["tanh"], i + 1)
                    pe.wait_ge(ev["pm"], i + 1)
                    for b in range(4):
                        mm_(Q[0][:, b * T:(b + 1) * T], e.lora_w[0:64, b * P:(b + 1) * P], tw[:, 0:T], start=True, stop=True)
                        mm = mm_(Q[1][:, b * T:(b + 1) * T], e.lora_w[64:128, b * P:(b + 1) * P], pm[64:128, 12, 0:T], start=True, stop=True)
                    mm.then_inc(ev["lora_mm"], 1)
                    fill("ssq")
                    pe.wait_ge(ev["sq"], i + 1)
                    mm_(Q[2][:, 0:4 * T], e.ones_bd, sq[:, 0:4 * T], start=True, stop=True).then_inc(ev["ssq_mm"], 1)
                    fill("turn")
                    for q, (bank, src) in enumerate(((4, None), (3, alpha), (5, bC), (0, kC))):
                        if src is not None:
                            pe.wait_ge(ev["feat"], i * 4 + (1, 3, 4)[q - 1])
                        for b in range(4):
                            s = pm[:, 8 + b, 0:T] if src is None else fv(src)[:, b]
                            mm = pe.transpose(Q[bank][0:T, b * P:(b + 1) * P], s, e.ident)
                        mm.then_inc(ev["turned"], 1)
                    for n, (l, r_) in enumerate(((alpha, beta), (beta, alpha), (kappa, alpha), (kappa, rho), (beta, rho))):
                        if n == 2:
                            pe.wait_ge(ev["turned_sb"], i * 4 + 4)
                            settle(3)
                        banks, z = PROD[n]
                        for b in range(4):
                            for par in (0, 1):
                                h0 = HD * par
                                for c in t.halves:
                                    mm = mm_(Q[banks[par]][C * c:C * c + C, (4 * z + b) * C:(4 * z + b + 1) * C], fv(l)[h0:h0 + HD, b, C * c:C * c + C],
                                             fv(r_)[h0:h0 + HD, b, C * c:C * c + C], start=True, stop=True)
                        mm.then_inc(ev["prod_mm"], 1)
                    fill("X0")
                    for n in range(t.levels):
                        fill(f"X{n}")
                        if n == 0:
                            pe.wait_ge(ev["t_init"], i + 1)
                            pe.wait_ge(ev["turned_sb"], i * 4 + 4)
                        else:
                            pe.wait_ge(ev["tx_sb"], tx_at(t, n - 1) + 4)
                        for q in range(2):
                            for h in range(4 * q, 4 * q + 4):
                                mm = mm_(Q[XB[q]][0:T, (h % 4) * T:(h % 4 + 1) * T], ab_t[0:T, h, 0:T], t_m[0:T, h, 0:T], start=True, stop=True)
                            mm.then_inc(ev["x_mm"], 1)
                        fill(f"TX{n}")
                        if n == 0:
                            pe.wait_ge(ev["prod_sb"], i * 3 + 3)
                        for q in range(2):
                            pe.wait_ge(ev["x_sb"], (i * 5 + n) * 2 + q + 1)
                            for h in range(4 * q, 4 * q + 4):
                                mm = mm_(Q[TXB[q]][0:T, (h % 4) * T:(h % 4 + 1) * T], t_t[0:T, h, 0:T], x_m[0:T, h, 0:T], start=True, stop=True)
                            mm.then_inc(ev["tx_mm"], 1)
                            for h in range(4 * q, 4 * q + 4):
                                mm = mm_(Q[XTB[q]][0:T, (h % 4) * T:(h % 4 + 1) * T], x_m[0:T, h, 0:T], t_t[0:T, h, 0:T], start=True, stop=True)
                            mm.then_inc(ev["tx_mm"], 1)
                    fill("Y")
                    for h in range(H):
                        mm = mm_(Q[1][0:T, h * HD:(h + 1) * HD], ak_t[0:T, h, 0:T], vt[0:T, h, :], start=True, stop=True)
                    mm.then_inc(ev["y_mm"], 1)
                    fill("GU")
                    pe.wait_ge(ev["tx_sb"], tx_at(t, t.levels - 1) + 4)
                    pe.wait_ge(ev["y_sb"], i + 1)
                    for q in range(2):
                        for h in range(4 * q, 4 * q + 4):
                            mm = mm_(Q[TXB[q]][0:T, (h % 4) * P:(h % 4 + 1) * P], t_t[0:T, h, 0:T], ay[0:T, h, :], start=True, stop=True)
                        mm.then_inc(ev["gu_mm"], 1)
                    fill("RM")
                    pe.wait_ge(ev["gu_sb"], i * 4 + 4)
                    for h in range(H):
                        if t.prompt:
                            o = Q[4][HD * (h % 2):HD * (h % 2) + HD, (h // 2) * P:(h // 2 + 1) * P]
                        else:
                            o = Q[4][0:HD, h * HD:(h + 1) * HD]
                        mm = mm_(o, n_g[0:T, h, :], rb_t[0:T, h, 0:T], start=True, stop=True)
                    mm.then_inc(ev["rm_mm"], 1)
                    if t.prompt:
                        for c in (0, 1):
                            for b in range(4):
                                mm = mm_(Q[1 + c][:, b * P:(b + 1) * P], n_g[C * c:C * c + C, 2 * b:2 * b + 2, :], bCt[C * c:C * c + C, 2 * b:2 * b + 2, :],
                                         start=True, stop=True)
                            mm.then_inc(ev["rm_mm"], 1)

                    def new_state(c, s_from, bank, done):
                        for b in range(4):
                            for h in (2 * b, 2 * b + 1):
                                o = Q[bank][HD * (h % 2):HD * (h % 2) + HD, b * HD:(b + 1) * HD]
                                rows = slice(C * c, C * c + C)
                                mm_(o, kCt[rows, h, :], vt[rows, h, :], start=True, stop=False, skip_group_check=True)
                                mm_(o, bCt[rows, h, :], n_u[rows, h, :], start=False, stop=False, skip_group_check=True)
                            mm = mm_(Q[bank][:, b * HD:(b + 1) * HD], m_c[:, c, b, :], s_from[:, b, :], start=False, stop=True, skip_group_check=True)
                        mm.then_inc(done, 1)

                    fill("S0")
                    if t.prompt:
                        pe.wait_ge(ev["m_sb"], i * 2 + 1)
                        if not t.first:
                            pe.wait_ge(ev["s1_sb"], i)
                        settle(3)
                        new_state(0, e.s_a, 3, ev["s0_mm"])
                        pe.wait_ge(ev["bonus"], i * 2 + 2)
                        pe.wait_ge(ev["rp_sb"], i + 1)
                        mm_(Q[4][:, 0:4 * T], e.ones_bd, bonus[:, 0:4 * T], start=True, stop=True)
                        fill("O")
                        pe.wait_ge(ev["s0_sb"], i + 1)
                        for b in range(4):
                            for c, s in ((0, s_ad), (1, s_bd)):
                                mm_(Q[0][C * c:C * c + C, b * P:(b + 1) * P], rp[:, b, C * c:C * c + C], s[:, b, :],
                                    start=True, stop=False, skip_group_check=True)
                            for h in (2 * b, 2 * b + 1):
                                o = Q[0][:, h * HD:(h + 1) * HD]
                                mm_(o, rk_t[:, h, :], vt[:, h, :], start=False, stop=False, skip_group_check=True)
                                mm = mm_(o, rb_t[:, h, :], n_u[:, h, :], start=False, stop=True, skip_group_check=True)
                        mm.then_inc(ev["o_mm"], 1)
                        pe.wait_ge(ev["m_sb"], i * 2 + 2)
                        settle(5)
                        new_state(1, s_b, 5, ev["s1_mm"])
                    else:
                        fill("O")
                        pe.wait_ge(ev["rpm"], NB)
                        pe.wait_ge(ev["bonus"], i * 2 + 2)
                        mm_(Q[4][:, 0:4 * T], e.ones_bd, bonus[:, 0:4 * T], start=True, stop=True)
                        for h in range(H):
                            r = h % 2
                            pe.wait_ge(s0_loaded[r], 16 * (h // 2 + 1))
                            o = Q[0][0:T, h * HD:(h + 1) * HD]
                            mm_(o, rk_t[0:T, h, 0:T], vt[0:T, h, :], start=True, stop=False)
                            mm_(o, rb_t[0:T, h, 0:T], n_u[0:T, h, :], start=False, stop=False)
                            for x in range(NB):
                                mm = mm_(o, rpm[x][:, h, :], s0t[:, r, x, :], start=False, stop=x == NB - 1)
                            if h == H - 1:
                                mm.then_inc(ev["o_mm"], 1)
                            pe.wait_ge(ev["mask_sb"], 2 * h + 2)
                            if h >= 2:
                                pe.wait_ge(ev["mz_sb"], h - 1)
                            mm_(Q[1 + r][0:HD, :], n_g[0:T, h, :], bcm[r], start=True, stop=True).then_inc(ev["mz_mm"], 1)
                            if h >= 2:
                                pe.wait_ge(ev["sn_sb"], h - 1)
                            o = Q[TXB[r]][0:HD, :]
                            mm_(o, vt[0:T, h, :], kcm[r], start=True, stop=False, skip_group_check=True)
                            mm_(o, n_u[0:T, h, :], bcm[r], start=False, stop=False, skip_group_check=True)
                            pe.wait_ge(ev["mz_sb"], h + 1)
                            for x in range(NB):
                                mm = mm_(o[:, x * HD:(x + 1) * HD], s0t[:, r, x, :], mz[r][:, x, :], start=False, stop=True, skip_group_check=True)
                            mm.then_inc(ev["sn_mm"], 1)
                    fill("ON")
                    pe.wait_ge(ev["on"], i + 1)
                    for b in range(4):
                        mm = pe.transpose(Q[1][:, b * T:(b + 1) * T], on[0:T, 2 * b:2 * b + 2, :].rearrange("p h k -> p (h k)"), e.ident[0:T, 0:T])
                    mm.then_inc(ev["on_mm"], 1)
                    fill("end")

                t0 = Tile(e, 0, True)
                t0.first = True
                body(t0)
                with pe.Fori(1, TILES) as i:
                    t = Tile(e, i, True)
                    t.first = False
                    body(t)
                t = Tile(e, TILES, False)
                t.first = False
                body(t)


def phase_pool(nc, io, e):
    EX = BUF + SEQ
    ES_ = BUF + NS
    with ExitStack() as ctx:
        sem = lambda n: ctx.enter_context(nc.semaphore(n))
        sb = lambda n, s, d=F32: ctx.enter_context(nc.sbuf_tensor(n, s, d))
        ux, usx = sb("pool_ext", [P, WB, EX])[:, :, :], sb("pool_ext_s", [P, WB, NB, ES_])[:, :, :, :]
        u5, cut = sb("s5_u_raw", [P, WB, NT]), sb("s5_u_cut", [P, WB, L5, J5])
        fresh = sb("pool_fresh", [P, WB, NB * NS])
        old = sb("pool_old", [NB * BUF, W])
        pw = sb("pool_weights", [P, WB, P])
        sums = [sb(f"pool_sum{i}", [P, WB, EX]) for i in range(2)]
        ssums = [sb(f"pool_ssum{i}", [P, WB, NB, ES_]) for i in range(2)]
        inv = sb("pool_inv", [P, WB, BUF])
        pooled = sb("pooled", [P, WB, NT])
        y_pl = sb("y_pl", [P, WB, NT])
        tail = sb("shift_tail", [P, RB, 1 + NB * NS])
        tail9 = sb("shift_cols", [P, RB, 1 + NB])
        shift_rows = sb("shift_rows_new", [1 + NB, RB * P])
        tail_p, tail_s = sb("pool_tail", [P, WB, BUF]), sb("pool_tail_s", [P, WB, NB * BUF])
        rows_p, rows_s = sb("pool_rows", [BUF, W]), sb("pool_rows_s", [NB * BUF, W])
        st_rows = sb("rwkv_rows", [HD, H, HD])
        ps = [ctx.enter_context(nc.psum_tensor(f"pool_ps{i}", [P, 512], F32)) for i in range(8)]
        loaded, cut_done, stored = sem("pl_loaded"), sem("s5_cut"), sem("pl_stored")
        u5_loaded = sem("s5_u_loaded")
        flip, flip_sb, tails, done, mm_done, chain = [sem(n) for n in ("pl_flip", "pl_flip_sb", "pl_tails", "pooled_done", "pl_mm", "pl_chain")]
        flip2, rows_done, scaled = sem("pl_flip2"), sem("pl_rows"), sem("pl_scaled")
        scr = lambda b0, k, a, b: e.scratch[b0:b0 + k, :, a:b].rearrange("b p t -> p b t")
        with nc.Block() as block:
            @block.sync
            def _(sp):
                sp.dma_start(u5[:, :, :], scr(B_S5X, WB, 1, 1 + NT)).then_inc(u5_loaded, 16)
                sp.dma_start(ux[:, :, BUF:EX], scr(B_PLX, WB, 1, 1 + SEQ)).then_inc(loaded, 16)
                sp.dma_start(fresh[:, :, :], scr(B_PLX, WB, 1 + SEQ, 1 + NT)).then_inc(loaded, 16)
                sp.dma_start(old[:, :], io["state_pool"][0].rearrange("b t w -> (b t) w")).then_inc(loaded, 16)
                sp.dma_start(pw[:, :, :], io["pool_w"][0].rearrange("g c d -> c g d")).then_inc(loaded, 16)
                sp.dma_start(tail[:, :, :], scr(B_RW, RB, SEQ, 1 + NT)).then_inc(loaded, 16)
                sp.wait_ge(cut_done, WB)
                sp.dma_start(e.u5_scr, cut[:, :, :, :]).then_inc(stored, 16)
                sp.wait_ge(rows_done, 7)
                sp.dma_start(e.outs["p_shift"][0], shift_rows[0:1, :]).then_inc(stored, 16)
                sp.dma_start(e.outs["s_shift"][0], shift_rows[1:1 + NB, :]).then_inc(stored, 16)
                sp.dma_start(e.outs["p_pool"][0, 0], rows_p[:, :]).then_inc(stored, 16)
                sp.dma_start(e.outs["s_pool"][0].rearrange("b t w -> (b t) w"), rows_s[:, :]).then_inc(stored, 16)
                sp.dma_start(e.outs["p_rwkv"][0, 0].rearrange("h v k -> v h k"), st_rows[:, :, :]).then_inc(stored, 16)
                sp.wait_ge(scaled, 3 * WB)
                sp.dma_start(e.y_scr[2], y_pl[:, :, :]).then_inc(stored, 16)
                sp.wait_ge(stored, 16 * 7)

            @block.gpsimd
            def _(pool):
                pool.wait_ge(u5_loaded, 16)
                for b in range(WB):
                    pool.tensor_copy(cut[:, b], u5[:, b, :].rearrange("p (j s) -> p s j", s=L5)).then_inc(cut_done, 1)

            @block.tensor
            def _(pe):
                pe.wait_ge(loaded, 16 * 5)
                for b in range(WB):
                    mm = pe.transpose(ps[0][:, b * NB * BUF:(b + 1) * NB * BUF], old[:, b * P:(b + 1) * P], e.ident[0:NB * BUF, 0:NB * BUF])
                mm.then_inc(flip, 1)
                for b in range(WB):
                    mm = pe.transpose(ps[1][0:HD, b * P:(b + 1) * P], e.s_a[:, b, :], e.ident)
                mm.then_inc(flip2, 1)
                pe.wait_ge(tails, 3)
                for r in range(RB):
                    mm = pe.transpose(ps[2 + r // 4][0:1 + NB, (r % 4) * P:(r % 4 + 1) * P], tail9[:, r, :], e.ident)
                mm.then_inc(flip2, 1)
                for b in range(WB):
                    mm = pe.transpose(ps[6][0:BUF, b * P:(b + 1) * P], tail_p[:, b, :], e.ident)
                for b in range(WB):
                    mm = pe.transpose(ps[7][0:NB * BUF, b * P:(b + 1) * P], tail_s[:, b, :], e.ident)
                mm.then_inc(flip2, 1)
                for g in range(WB):
                    pe.wait_ge(done, g + 1)
                    for c, (at, n) in enumerate(CH):
                        q = g * 3 + c
                        if q == 0:
                            pe.wait_ge(rows_done, 7)
                        if q >= 8:
                            pe.wait_ge(scaled, q - 7)
                        pe.matmul(ps[q % 8][:, 0:n], pw[:, g, :], pooled[:, g, at:at + n], start=True, stop=True).then_inc(mm_done, 1)

            @block.scalar
            def _(act):
                act.wait_ge(flip2, 1)
                act.activation(st_rows[:, :, :], ps[1][0:HD, :].rearrange("v (h k) -> v h k", k=HD), ACT.Copy).then_inc(rows_done, 1)
                act.wait_ge(flip2, 3)
                for q in range(4):
                    n = min(4, RB - 4 * q) * P
                    act.activation(shift_rows[:, q * 512:q * 512 + n], ps[2 + q][0:1 + NB, 0:n], ACT.Copy).then_inc(rows_done, 1)
                act.activation(rows_p[:, :], ps[6][0:BUF, :], ACT.Copy).then_inc(rows_done, 1)
                act.activation(rows_s[:, :], ps[7][0:NB * BUF, :], ACT.Copy).then_inc(rows_done, 1)
                for g in range(WB):
                    at_s = VAT["pool_scale"][0] + g
                    for c, (at, n) in enumerate(CH):
                        q = g * 3 + c
                        act.wait_ge(mm_done, q + 1)
                        act.activation(y_pl[:, g, at:at + n], ps[q % 8][:, 0:n], ACT.Copy, scale=e.vec[:, at_s:at_s + 1]).then_inc(scaled, 1)

            @block.vector
            def _(dve):
                ch = Chain(dve, chain)
                tt = dve.tensor_tensor
                ch.after(dve.memset(ux[:, :, 0:BUF], 0.0))
                for g, w in enumerate(WIN):
                    ch.after(dve.memset(inv[:, g, :], 1.0 / w))
                ch.wait()
                for pos in range(BUF):
                    g0 = [g for g, w in enumerate(WIN) if w > pos + 1][0]
                    ch.after(dve.memset(inv[:, g0:WB, pos:pos + 1], 1.0 / (pos + 1)))
                dve.wait_ge(loaded, 16 * 5)
                dve.tensor_copy(tail9[:, :, :], tail[:, :, 0:1 + NB * NS:NS]).then_inc(tails, 1)
                dve.tensor_copy(tail_p[:, :, :], ux[:, :, SEQ:EX]).then_inc(tails, 1)
                dve.wait_ge(flip, 1)
                ch.after(dve.tensor_copy(usx[:, :, :, 0:BUF], ps[0][:, 0:WB * NB * BUF].rearrange("p (w b t) -> p w b t", w=WB, b=NB)))
                ch.after(dve.tensor_copy(usx[:, :, :, BUF:ES_], fresh[:, :, :].rearrange("p w (b t) -> p w b t", b=NB)))
                ch.wait()
                dve.tensor_copy(tail_s[:, :, :].rearrange("p w (b t) -> p w b t", b=NB), usx[:, :, :, NS:ES_]).then_inc(tails, 1)
                src, ssrc = ux, usx
                for g, w in enumerate(WIN):
                    d, lo = w // 2, w - 1
                    dst, sdst = sums[g % 2], ssums[g % 2]
                    ch.after(tt(dst[:, g:WB, lo:EX], src[:, g:WB, lo:EX], src[:, g:WB, lo - d:EX - d], ALU.add))
                    ch.after(tt(sdst[:, g:WB, :, lo:ES_], ssrc[:, g:WB, :, lo:ES_], ssrc[:, g:WB, :, lo - d:ES_ - d], ALU.add))
                    ch.wait()
                    ch.after(tt(pooled[:, g, 0:BUF], dst[:, g, BUF:2 * BUF], inv[:, g, :], ALU.mult))
                    ch.wait()
                    ch.after(tt(pooled[:, g, 0:BUF], pooled[:, g, 0:BUF], ux[:, g, BUF:2 * BUF], ALU.subtract))
                    ch.after(dve.scalar_tensor_tensor(out=pooled[:, g, BUF:SEQ], in0=dst[:, g, 2 * BUF:EX], scalar=1.0 / w,
                                                      in1=ux[:, g, 2 * BUF:EX], op0=ALU.mult, op1=ALU.subtract))
                    ch.after(dve.scalar_tensor_tensor(out=pooled[:, g, SEQ:NT].rearrange("p (b t) -> p b t", b=NB), in0=sdst[:, g, :, BUF:ES_],
                                                      scalar=1.0 / w, in1=usx[:, g, :, BUF:ES_], op0=ALU.mult, op1=ALU.subtract))
                    ch.wait()
                    dve.sem_inc(done, 1)
                    src, ssrc = dst, sdst


def phase_s5_tables(nc, io, e):
    L = L5
    with ExitStack() as ctx:
        sem = lambda n: ctx.enter_context(nc.semaphore(n))
        sb = lambda n, s, d=F32: ctx.enter_context(nc.sbuf_tensor(n, s, d))
        small = lambda n: sb(n, [P, G])[:, :]
        lam = sb("lam_rows", [G, 2, P])
        lam_t = sb("lam_t", [P, 2, G])
        dt, ldt, mag, m2, th, kf, r1, sh, si, co, ar, ai, den, u1, u2, u3, cor, coi = (small("t5_" + n) for n in (
            "dt", "ldt", "mag", "m2", "th", "k", "r", "sh", "si", "co", "ar", "ai", "den", "u1", "u2", "u3", "cor", "coi"))
        kint = sb("t5_kint", [P, G], mybir.dt.int32)[:, :]
        pw = sb("t5_pow", [P, 2, L + 1, G])
        wv = sb("t5_unit", [P, 2, 10, G])
        braw = sb("b_raw", [P, 2, G, GC])
        bt = sb("b_bar", [P, 2, G, GC])
        crow = sb("c_rows", [P, 2, 4, P])
        cst = sb("c_st", [P, 2, G, GC])
        ebuf, tmp = sb("e_buf", [P, G, L, GC]), sb("t5_tmp", [P, 3 * G * GC])
        kt = ebuf[0:GC].rearrange("p g s c -> p g (s c)")
        h0rows = sb("h0_rows", [P, 2, 2, P])
        ps = [ctx.enter_context(nc.psum_tensor(f"t5_ps{i}", [P, 512], F32)) for i in range(8)]
        loaded, chain, flip, lam_sb, etab, eflip, es_sb, dtab, kmm, k_sb, toep = [sem("t5s_" + n) for n in (
            "loaded", "chain", "flip", "lam_sb", "etab", "eflip", "es_sb", "dtab", "kmm", "k_sb", "toep")]
        acts, unit, tz, ptab, cflip, c_sb, hflip = [sem("t5s_" + n) for n in ("acts", "unit", "tz", "ptab", "cflip", "c_sb", "hflip")]
        es2_sb = sem("t5s_es2")
        with nc.Block() as block:
            @block.sync
            def _(sp):
                n = 0
                def ld(dst, src):
                    sp.dma_start(dst, src).then_inc(loaded, 16)
                for half in range(2):
                    hs = slice(HD * half, HD * half + HD)
                    ld(lam[:, 0, hs], io["s5_lam_re"][0])
                    ld(lam[:, 1, hs], io["s5_lam_im"][0])
                    for k in range(2):
                        re = half == k
                        ld(braw[hs, k], io["s5_b_re" if re else "s5_b_im"][0].rearrange("g n c -> n g c"))
                        ld(crow[:, k, :, hs], io["s5_c_re" if re else "s5_c_im"][0].rearrange("g c n -> (g c) n").rearrange("(q p) n -> p q n", p=P))
                        ld(h0rows[:, k, :, hs], io["state_s5_re" if re else "state_s5_im"][0].rearrange("b g n -> (b g) n").rearrange("(q p) n -> p q n", p=P))
                ld(ldt, io["s5_log_dt"].to_broadcast((P, G)))
                for s in range(L):
                    sp.dma_start(e.u5[GC * s:GC * s + GC].rearrange("c (b q) j -> c b q j", b=WB),
                                 e.u5_scr.rearrange("(q c) b s j -> s c b q j", c=GC)[s]).then_inc(e.u5_sem, 16)
                sp.wait_ge(k_sb, 8)
                sp.wait_ge(tz, 1)
                for s in range(L):
                    sp.dma_start(e.toep[GC * s:GC * s + GC, :, GC * s:P], kt[:, :, 0:P - GC * s]).then_inc(toep, 16)
                sp.wait_ge(toep, 16 * L)
                sp.wait_ge(e.u5_sem, 16 * L)

            @block.scalar
            def _(act):
                act.wait_ge(loaded, 16 * 17)
                act.wait_ge(lam_sb, 1)
                act.activation(si, r1, ACT.Sin).then_inc(acts, 1)
                act.activation(sh, r1, ACT.Sin, scale=0.5).then_inc(acts, 1)
                for q in range(8):
                    act.wait_ge(eflip, q + 1)
                    act.activation(e.es[:, 0, 4 * q:4 * q + 4, :], ps[q % 4][:, :].rearrange("p (g n) -> p g n", g=4), ACT.Copy).then_inc(es_sb, 1)
                    act.wait_ge(es_sb, q + 1)
                    act.activation(e.es[:, 1, 4 * q:4 * q + 4, 0:HD], e.es[:, 0, 4 * q:4 * q + 4, HD:P], ACT.Copy, scale=-1.0).then_inc(es2_sb, 1)
                    act.activation(e.es[:, 1, 4 * q:4 * q + 4, HD:P], e.es[:, 0, 4 * q:4 * q + 4, 0:HD], ACT.Copy).then_inc(es2_sb, 1)
                for q in range(8):
                    act.wait_ge(kmm, q + 1)
                    act.activation(kt[:, 4 * q:4 * q + 4, :], ps[4 + q % 4][0:GC, :].rearrange("p (g n) -> p g n", g=4), ACT.Copy).then_inc(k_sb, 1)

            @block.tensor
            def _(pe):
                pe.wait_ge(loaded, 16 * 17)
                for q in range(2):
                    mm = pe.transpose(ps[0][:, q * G:(q + 1) * G], lam[:, q, :], e.ident[0:G, 0:G])
                mm.then_inc(flip, 1)
                for k in range(2):
                    for q in range(4):
                        mm = pe.transpose(ps[1 + k][:, q * P:(q + 1) * P], crow[:, k, q, :], e.ident)
                    mm.then_inc(cflip, 1)
                for k in range(2):
                    for q in range(2):
                        mm = pe.transpose(ps[3][:, (2 * k + q) * P:(2 * k + q + 1) * P], h0rows[:, k, q, :], e.ident)
                mm.then_inc(hflip, 1)
                pe.wait_ge(etab, 1)
                for q in range(8):
                    if q >= 4:
                        pe.wait_ge(es_sb, q - 3)
                    for g in range(4):
                        mm = pe.transpose(ps[q % 4][:, g * P:(g + 1) * P], ebuf[:, 4 * q + g, :, :].rearrange("p s c -> p (s c)"), e.ident)
                    mm.then_inc(eflip, 1)
                pe.wait_ge(dtab, 1)
                for q in range(8):
                    if q >= 4:
                        pe.wait_ge(k_sb, q - 3)
                    for g in range(4):
                        mm = pe.matmul(ps[4 + q % 4][0:GC, g * P:(g + 1) * P], bt[:, 0, 4 * q + g, :],
                                       e.dtab[:, 4 * q + g, 0:L, :].rearrange("p t c -> p (t c)"), start=True, stop=True)
                    mm.then_inc(kmm, 1)

            @block.gpsimd
            def _(pool):
                pool.memset(e.toep[:, :, :], 0.0).then_inc(tz, 1)
                ch = Chain(pool, ptab)
                ch.after(pool.memset(e.rot[:, 0, :, 0:1], 1.0))
                ch.after(pool.memset(e.rot[:, 1, :, 0:1], 0.0))
                pool.wait_ge(unit, 1)
                ta, tb = e.hprev[:, :, 0:HD], e.hprev[:, :, HD:P]
                m = 1
                for q in range(7):
                    w = [wv[:, z, 3 + q, :].rearrange("p (g o) -> p g o", o=1).to_broadcast((P, G, m)) for z in range(2)]
                    tr, ti = e.rot[:, 0, :, 0:m], e.rot[:, 1, :, 0:m]
                    for z, (a, b, op) in enumerate(((0, 1, ALU.subtract), (1, 0, ALU.add))):
                        ch.wait()
                        ch.after(pool.tensor_tensor(ta[:, :, 0:m], tr, w[a], ALU.mult))
                        ch.after(pool.tensor_tensor(tb[:, :, 0:m], ti, w[b], ALU.mult))
                        ch.wait()
                        ch.after(pool.tensor_tensor(e.rot[:, z, :, m:2 * m], ta[:, :, 0:m], tb[:, :, 0:m], op))
                    m *= 2
                ch.wait()

            @block.vector
            def _(dve):
                ch = Chain(dve, chain)
                tt, ts = dve.tensor_tensor, dve.tensor_scalar

                def op(ins):
                    ch.after(ins)
                    ch.wait()
                dve.wait_ge(flip, 1)
                op(dve.tensor_copy(lam_t[:, :, :].rearrange("p q g -> p (q g)"), ps[0][:, 0:2 * G]))
                lr, li = lam_t[:, 0, :], lam_t[:, 1, :]
                dve.wait_ge(cflip, 2)
                ch.after(dve.tensor_copy(cst[:, 0].rearrange("p g c -> p (g c)"), ps[1][:, :]))
                ch.after(dve.tensor_copy(cst[:, 1].rearrange("p g c -> p (g c)"), ps[2][:, :]))
                ch.wait()
                op(ts(cst[HD:P, 0], cst[HD:P, 0], -1.0, None, ALU.mult))
                dve.wait_ge(hflip, 1)
                h4 = ps[3][:, :].rearrange("p (k b g) -> p k b g", k=2, g=G)
                op(dve.tensor_copy(e.h0[:, :, :, :], h4))
                op(ts(e.h0[0:HD, 1], e.h0[0:HD, 1], -1.0, None, ALU.mult))

                def exp(dst, x):
                    op(ts(kf, x, 1.0 / LN2, -126.0, ALU.mult, ALU.max))
                    op(ts(kf, kf, 127.0, MAGIC, ALU.min, ALU.add))
                    op(ts(kf, kf, -MAGIC, None, ALU.add))
                    op(dve.scalar_tensor_tensor(out=u2, in0=kf, scalar=-LN2_PARTS[0], in1=x, op0=ALU.mult, op1=ALU.add))
                    op(dve.scalar_tensor_tensor(out=u2, in0=kf, scalar=-LN2_PARTS[1], in1=u2, op0=ALU.mult, op1=ALU.add))
                    op(ts(u2, u2, -0.35, 0.35, ALU.max, ALU.min))
                    op(ts(dst, u2, 1.0 / EXP_FACT[-1], None, ALU.mult))
                    for f in EXP_FACT[-2::-1]:
                        op(dve.scalar_tensor_tensor(out=dst, in0=dst, scalar=1.0 / f, in1=u2, op0=ALU.add, op1=ALU.mult))
                    op(ts(kf, kf, 127.0, 2.0 ** 23, ALU.add, ALU.mult))
                    op(dve.tensor_copy(kint, kf))
                    op(dve.scalar_tensor_tensor(out=dst, in0=dst, scalar=1.0, in1=kint.bitcast(F32), op0=ALU.add, op1=ALU.mult))

                dve.wait_ge(loaded, 16 * 17)
                exp(dt, ldt)
                op(tt(u1, lr, dt, ALU.mult))
                exp(mag, u1)
                op(tt(th, li, dt, ALU.mult))
                op(ts(kf, th, 1.0 / (2 * np.pi), MAGIC, ALU.mult, ALU.add))
                op(ts(kf, kf, -MAGIC, None, ALU.add))
                op(dve.scalar_tensor_tensor(out=r1, in0=kf, scalar=-TURN[0], in1=th, op0=ALU.mult, op1=ALU.add))
                op(dve.scalar_tensor_tensor(out=r1, in0=kf, scalar=-TURN[1], in1=r1, op0=ALU.mult, op1=ALU.add))
                op(dve.scalar_tensor_tensor(out=r1, in0=kf, scalar=-TURN[2], in1=r1, op0=ALU.mult, op1=ALU.add))
                op(ts(r1, r1, -PI_IN, PI_IN, ALU.max, ALU.min))
                dve.sem_inc(lam_sb, 1)
                dve.wait_ge(acts, 2)
                op(tt(co, sh, sh, ALU.mult))
                op(ts(co, co, -2.0, 1.0, ALU.mult, ALU.add))
                op(tt(ar, mag, co, ALU.mult))
                op(tt(ai, mag, si, ALU.mult))
                ch.after(dve.tensor_copy(wv[:, 0, 0, :], co))
                op(dve.tensor_copy(wv[:, 1, 0, :], si))
                for q in range(9):
                    a, b = wv[:, 0, q, :], wv[:, 1, q, :]
                    ch.after(tt(u1, a, a, ALU.mult))
                    ch.after(tt(u2, b, b, ALU.mult))
                    ch.after(tt(u3, a, b, ALU.mult))
                    ch.wait()
                    ch.after(tt(wv[:, 0, q + 1, :], u1, u2, ALU.subtract))
                    op(ts(wv[:, 1, q + 1, :], u3, 2.0, None, ALU.mult))
                    if q >= 2:
                        a, b = wv[:, 0, q + 1, :], wv[:, 1, q + 1, :]
                        ch.after(tt(u1, a, a, ALU.mult))
                        op(tt(u2, b, b, ALU.mult))
                        op(tt(u3, u1, u2, ALU.add))
                        op(ts(u3, u3, -0.5, 1.5, ALU.mult, ALU.add))
                        ch.after(tt(a, a, u3, ALU.mult))
                        op(tt(b, b, u3, ALU.mult))
                dve.sem_inc(unit, 1)
                op(tt(m2, mag, mag, ALU.mult))
                op(tt(m2, m2, m2, ALU.mult))
                op(tt(e.mag8, m2, m2, ALU.mult))
                ch.after(dve.memset(pw[:, 0, 0, :], 1.0))
                ch.after(dve.memset(pw[:, 1, 0, :], 0.0))
                ch.after(dve.tensor_copy(pw[:, 0, 1, :], ar))
                op(dve.tensor_copy(pw[:, 1, 1, :], ai))
                t3 = lambda k, m: tmp[:, k * 256:k * 256 + m * G].rearrange("p (s g) -> p s g", s=m)
                m = 1
                while m < L:
                    w = [pw[:, z, m:m + 1, :].to_broadcast((P, m, G)) for z in range(2)]
                    x, y = pw[:, 0, 1:m + 1, :], pw[:, 1, 1:m + 1, :]
                    for z, (a, b, o) in enumerate(((0, 1, ALU.subtract), (1, 0, ALU.add))):
                        ch.after(tt(t3(0, m), x, w[a], ALU.mult))
                        op(tt(t3(1, m), y, w[b], ALU.mult))
                        op(tt(pw[:, z, m + 1:2 * m + 1, :], t3(0, m), t3(1, m), o))
                    m *= 2
                ch.after(tt(u1, lr, lr, ALU.mult))
                op(tt(u2, li, li, ALU.mult))
                op(tt(den, u1, u2, ALU.add))
                ch.after(dve.reciprocal(den, den))
                op(ts(ar, ar, -1.0, None, ALU.add))
                for dst, (x, y, o) in ((cor, (lr, li, ALU.add)), (coi, (li, lr, ALU.subtract))):
                    a_, b_ = (ar, ai)
                    ch.after(tt(u1, a_ if o == ALU.add else b_, lr, ALU.mult))
                    op(tt(u2, b_ if o == ALU.add else a_, li, ALU.mult))
                    op(tt(u3, u1, u2, o))
                    op(tt(dst, u3, den, ALU.mult))
                dve.wait_ge(loaded, 16 * 17)
                op(ts(braw[0:HD, 1], braw[0:HD, 1], -1.0, None, ALU.mult))
                gb = lambda x: x.rearrange("p (g o) -> p g o", o=1).to_broadcast((P, G, GC))
                ta, tb = (tmp[:, k * 512:(k + 1) * 512].rearrange("p (g c) -> p g c", g=G) for k in range(2))
                for z, o in enumerate((ALU.add, ALU.subtract)):
                    ch.after(tt(ta, braw[:, z], gb(cor), ALU.mult))
                    op(tt(tb, braw[:, 1 - z], gb(coi), ALU.mult))
                    op(tt(bt[:, z], ta, tb, o))

                def table(dst, x, power, count, o):
                    tq = tmp[:, :].rearrange("p (s g c) -> p s g c", s=3, g=G)
                    for s0 in range(0, count, 3):
                        some = range(s0, min(s0 + 3, count))
                        for s in some:
                            pb = [gb(pw[:, z, power(s), :]) for z in range(2)]
                            ch.after(tt(dst[:, :, s, :], x[:, 0], pb[0], ALU.mult))
                            ch.after(tt(tq[:, s - s0], x[:, 1], pb[1], ALU.mult))
                        ch.wait()
                        for s in some:
                            ch.after(tt(dst[:, :, s, :], dst[:, :, s, :], tq[:, s - s0], o))
                        ch.wait()

                table(ebuf, bt, lambda s: L - 1 - s, L, ALU.add)
                dve.sem_inc(etab, 1)
                table(e.dtab, cst, lambda s: s, L + 1, ALU.subtract)
                dve.sem_inc(dtab, 1)
                op(dve.tensor_copy(e.a8[:, :, :], pw[:, :, L, :]))


def phase_s5(nc, io, e):
    NG = 3
    batches = [list(range(a, min(a + NG, G))) for a in range(0, G, NG)]
    with ExitStack() as ctx:
        sem = lambda n: ctx.enter_context(nc.semaphore(n))
        sb = lambda n, s, d=F32: ctx.enter_context(nc.sbuf_tensor(n, s, d))
        gsc = sb("s5_scan", [P, G, JP])
        xs = sb("s5_x_sample", [P, G, NB])
        t_a, t_b = sb("s5_ta", [P, 2, NG, JP]), sb("s5_tb", [P, 2, NG, JP])
        fin, snew = sb("s5_fin", [P, G]), sb("s5_snew", [P, NB, G])
        fa, fb = sb("s5_fa", [P, NB, G]), sb("s5_fb", [P, NB, G])
        perm = sb("s5_perm", [P, P])
        fin_rows, s_rows = sb("s5_fin_rows", [G, P]), sb("s5_s_rows", [P, 2, P])
        ycut = sb("s5_ycut", [P, G, J5])
        ps = [ctx.enter_context(nc.psum_tensor(f"s5_ps{i}", [P, 512], F32)) for i in range(8)]
        x_mm, x_used, gin, scan, i_mm, hdone, y_mm, y_sb, chain, permd, y_st, fins, finflip, fin_sb, out_st = [sem("s5_" + n) for n in (
            "x_mm", "x_used", "gin", "scan", "i_mm", "hdone", "y_mm", "y_sb", "chain", "permd", "y_st", "fins", "finflip", "fin_sb", "out_st")]
        hz = sem("s5_hz")
        with nc.Block() as block:
            @block.gpsimd
            def _(pool):
                ch = Chain(pool, permd)
                ch.after(pool.memset(perm[:, :], 0.0))
                ch.wait()
                ch.after(pool.affine_select(out=perm[:, :], in_=perm[:, :], compare_op=ALU.not_equal, fill=1.0, base=HD,
                                            pattern=[[-1, P]], channel_multiplier=1))
                ch.wait()
                ch.after(pool.affine_select(out=perm[:, :], in_=perm[:, :], compare_op=ALU.not_equal, fill=-1.0, base=-HD,
                                            pattern=[[-1, P]], channel_multiplier=1))
                ch.wait()

            @block.tensor
            def _(pe):
                def turn(n):
                    gs = batches[n]
                    if n == 0:
                        pe.wait_ge(permd, 3)
                    pe.wait_ge(scan, gs[-1] + 1)
                    if n >= 2:
                        pe.wait_ge(hdone, n - 1)
                    pe.matmul(ps[4 + n % 2][:, 0:len(gs) * JP], perm[:, :], gsc[:, gs[0]:gs[-1] + 1, :].rearrange("p g j -> p (g j)"),
                              start=True, stop=True).then_inc(i_mm, 1)

                for n, gs in enumerate(batches):
                    if n >= 2:
                        pe.wait_ge(x_used, n - 1)
                    for z in range(2):
                        for q, g in enumerate(gs):
                            mm = pe.matmul(ps[2 * (n % 2) + z][:, q * J5:(q + 1) * J5], e.es[:, z, g, :], e.u5[:, g, :], start=True, stop=True)
                    mm.then_inc(x_mm, 1)
                    if n >= 1:
                        turn(n - 1)
                turn(len(batches) - 1)
                pe.wait_ge(fins, 2)
                pe.transpose(ps[0][0:G, 0:P], fin[:, :], e.ident).then_inc(finflip, 1)
                for q in range(2):
                    mm = pe.transpose(ps[1][:, q * P:(q + 1) * P], snew[:, 4 * q:4 * q + 4, :].rearrange("p b g -> p (b g)"), e.ident)
                mm.then_inc(finflip, 1)
                for n, gs in enumerate(batches):
                    if n >= 2:
                        pe.wait_ge(y_sb, n - 1)
                    if n == 0:
                        pe.wait_ge(hz, 2)
                    pe.wait_ge(hdone, n + 1)
                    for q, g in enumerate(gs):
                        o = ps[6 + n % 2][:, q * J5:(q + 1) * J5]
                        pe.matmul(o, e.toep[:, g, :], e.u5[:, g, :], start=True, stop=False)
                        mm = pe.matmul(o, e.dtab[:, g, 1:L5 + 1, :].rearrange("p t c -> p (t c)"), e.hprev[:, g, :], start=False, stop=True)
                    mm.then_inc(y_mm, 1)

            @block.vector
            def _(dve):
                ch = Chain(dve, chain)
                tt = dve.tensor_tensor
                dve.memset(e.hprev[:, :, 0:1], 0.0).then_inc(hz, 1)
                dve.tensor_copy(e.hprev[:, :, JP:J5].rearrange("p g b -> p b g"), e.h0[:, 0]).then_inc(hz, 1)

                def rotate_back(n):
                    gs = batches[n]
                    gr, k = slice(gs[0], gs[-1] + 1), len(gs)
                    dve.wait_ge(i_mm, n + 1)
                    ig = ps[4 + n % 2][:, 0:k * JP].rearrange("p (g j) -> p g j", g=k)
                    ch.after(tt(t_a[:, 1, 0:k, :], gsc[:, gr, :], e.rot[:, 0, gr, :], ALU.mult))
                    ch.after(tt(t_b[:, 1, 0:k, :], ig, e.rot[:, 1, gr, :], ALU.mult))
                    ch.wait()
                    ch.after(tt(fin[:, gr], t_a[:, 1, 0:k, JP - 1], t_b[:, 1, 0:k, JP - 1], ALU.add))
                    ch.after(tt(e.hprev[:, gr, 1:JP], t_a[:, 1, 0:k, 0:JP - 1], t_b[:, 1, 0:k, 0:JP - 1], ALU.add))
                    ch.wait()
                    dve.sem_inc(hdone, 1)

                for n, gs in enumerate(batches):
                    gr, k = slice(gs[0], gs[-1] + 1), len(gs)
                    dve.wait_ge(x_mm, n + 1)
                    x, ix = (ps[2 * (n % 2) + z][:, 0:k * J5].rearrange("p (g j) -> p g j", g=k) for z in range(2))
                    ch.after(tt(t_a[:, 0, 0:k, :], x[:, :, 0:JP], e.rot[:, 0, gr, :], ALU.mult))
                    ch.after(tt(t_b[:, 0, 0:k, :], ix[:, :, 0:JP], e.rot[:, 1, gr, :], ALU.mult))
                    ch.after(dve.tensor_copy(xs[:, gr, :], x[:, :, JP:J5]))
                    ch.wait()
                    dve.sem_inc(x_used, 1)
                    ch.after(tt(t_a[:, 0, 0:k, :], t_a[:, 0, 0:k, :], t_b[:, 0, 0:k, :], ALU.subtract))
                    ch.wait()
                    for q, g in enumerate(gs):
                        dve.tensor_tensor_scan(gsc[:, g, :], e.mag8[:, g:g + 1].to_broadcast((P, JP)), t_a[:, 0, q, :], 0.0,
                                               ALU.mult, ALU.add).then_inc(scan, 1)
                    dve.wait_ge(scan, gs[-1] + 1)
                    if n >= 1:
                        rotate_back(n - 1)
                rotate_back(len(batches) - 1)
                ab = [e.a8[:, z:z + 1, :].to_broadcast((P, NB, G)) for z in range(2)]
                ch.after(tt(fa[:, :, :], e.h0[:, 0], ab[0], ALU.mult))
                ch.after(tt(fb[:, :, :], e.h0[:, 1], ab[1], ALU.mult))
                ch.wait()
                ch.after(tt(fa[:, :, :], fa[:, :, :], fb[:, :, :], ALU.add))
                ch.wait()
                ch.after(tt(snew[:, :, :], fa[:, :, :], xs[:, :, :].rearrange("p g b -> p b g"), ALU.add))
                ch.wait()
                dve.sem_inc(fins, 2)

            @block.scalar
            def _(act):
                act.wait_ge(finflip, 2)
                act.activation(fin_rows[:, :], ps[0][0:G, 0:P], ACT.Copy).then_inc(fin_sb, 1)
                act.activation(s_rows[:, :, :], ps[1][:, 0:2 * P].rearrange("p (q n) -> p q n", q=2), ACT.Copy).then_inc(fin_sb, 1)
                for n, gs in enumerate(batches):
                    k = len(gs)
                    act.wait_ge(y_mm, n + 1)
                    act.activation(ycut[:, gs[0]:gs[-1] + 1, :], ps[6 + n % 2][:, 0:k * J5].rearrange("p (g j) -> p g j", g=k), ACT.Copy).then_inc(y_sb, 1)

            @block.sync
            def _(sp):
                sp.wait_ge(fin_sb, 2)
                for z, n in enumerate(("re", "im")):
                    zs = slice(HD * z, HD * z + HD)
                    sp.dma_start(e.outs["p_s5_" + n][0, 0], fin_rows[:, zs]).then_inc(out_st, 16)
                    sp.dma_start(e.outs["s_s5_" + n][0].rearrange("b g n -> (b g) n").rearrange("(q p) n -> p q n", p=P), s_rows[:, :, zs]).then_inc(out_st, 16)
                sp.wait_ge(y_sb, len(batches))
                sp.dma_start(e.y5_scr, ycut[:, :, :]).then_inc(y_st, 16)
                sp.wait_ge(y_st, 16)
                sp.wait_ge(out_st, 64)


def phase_glu(nc, io, e):
    with ExitStack() as ctx:
        sem = lambda n: ctx.enter_context(nc.semaphore(n))
        sb = lambda n, s, d=F32: ctx.enter_context(nc.sbuf_tensor(n, s, d))
        yc, u = sb("glu_yc", [P, WB, L5, J5]), sb("glu_u", [P, WB, NT])
        act_y, gate = sb("glu_act", [P, WB, NT]), sb("glu_gate", [P, 2, CH[0][1]])
        w = sb("glu_w", [P, WB, W])
        y_s5 = sb("y_s5", [P, WB, NT])
        y_stored = sem("glu_stored")
        ps = [ctx.enter_context(nc.psum_tensor(f"glu_ps{i}", [P, 512], F32)) for i in range(4)]
        loaded, u_loaded, w_loaded, pre, gelu, mm_done, sig, out = [sem("glu_" + n) for n in ("loaded", "u_loaded", "w_loaded", "pre", "gelu", "mm", "sig", "out")]
        with nc.Block() as block:
            @block.sync
            def _(sp):
                sp.dma_start(u[:, :, :], e.scratch[B_S5X:B_S5X + WB, :, 1:1 + NT].rearrange("b p t -> p b t")).then_inc(u_loaded, 16)
                for q in range(8):
                    sp.dma_start(yc[GC * q:GC * q + GC], e.y5_scr.rearrange("(t c) (b q) j -> q c b t j", c=GC, q=8)[q]).then_inc(loaded, 16)
                sp.dma_start(w[:, :, :], io["s5_w_glu"][0].rearrange("(k p) m -> p k m", p=P)).then_inc(w_loaded, 16)
                sp.wait_ge(out, 3 * WB)
                sp.dma_start(e.y_scr[0], y_s5[:, :, :]).then_inc(y_stored, 16)
                sp.wait_ge(y_stored, 16)

            @block.vector
            def _(dve):
                dve.wait_ge(u_loaded, 16)
                dve.wait_ge(loaded, 16 * 8)
                for b in range(WB):
                    at = VAT["s5_d"][0] + b
                    dve.scalar_tensor_tensor(out=u[:, b, :].rearrange("p (j t) -> p j t", t=L5), in0=u[:, b, :].rearrange("p (j t) -> p j t", t=L5),
                                             scalar=e.vec[:, at:at + 1], in1=yc[:, b].rearrange("p t j -> p j t"),
                                             op0=ALU.mult, op1=ALU.add).then_inc(pre, 1)
                for m in range(WB):
                    for c, (at, n) in enumerate(CH):
                        q = m * 3 + c
                        dve.wait_ge(sig, q + 1)
                        dve.tensor_tensor(y_s5[:, m, at:at + n], act_y[:, m, at:at + n], gate[:, q % 2, 0:n], ALU.mult).then_inc(out, 1)

            @block.scalar
            def _(act):
                for b in range(WB):
                    act.wait_ge(pre, b + 1)
                    act.activation(act_y[:, b, :], u[:, b, :], ACT.Gelu_apprx_tanh).then_inc(gelu, 1)
                for m in range(WB):
                    for c, (at, n) in enumerate(CH):
                        q = m * 3 + c
                        act.wait_ge(mm_done, q + 1)
                        if q >= 2:
                            act.wait_ge(out, q - 1)
                        act.activation(gate[:, q % 2, 0:n], ps[q % 4][:, 0:n], ACT.Sigmoid).then_inc(sig, 1)

            @block.tensor
            def _(pe):
                pe.wait_ge(w_loaded, 16)
                pe.wait_ge(gelu, WB)
                for m in range(WB):
                    for c, (at, n) in enumerate(CH):
                        q = m * 3 + c
                        if q >= 4:
                            pe.wait_ge(sig, q - 3)
                        for k in range(WB):
                            mm = pe.matmul(ps[q % 4][:, 0:n], w[:, k, m * P:(m + 1) * P], act_y[:, k, at:at + n], start=k == 0, stop=k == WB - 1)
                        mm.then_inc(mm_done, 1)


def phase_up(nc, io, e):
    zs = (B_S5Z, B_RWZ, B_PLZ)
    w_up = [io[n] for n in ("w_up_s5", "w_up_rwkv", "w_up_pool")]
    NB3 = 3
    with ExitStack() as ctx:
        sem = lambda n: ctx.enter_context(nc.semaphore(n))
        yh = ctx.enter_context(nc.sbuf_tensor("up_y_hi", [P, NB3, WB, NT], F32R))
        yl = ctx.enter_context(nc.sbuf_tensor("up_y_lo", [P, NB3, WB, NT], F32R))
        with ExitStack() as c1:
            sb = lambda n, s, d=F32: c1.enter_context(nc.sbuf_tensor(n, s, d))
            y, z = sb("up_y", [P, 2, NT]), sb("up_z", [P, 2, NT])
            loaded = [sem(f"up_loaded{i}") for i in range(2)]
            silu, prod, hi, lo = sem("up_silu"), sem("up_prod"), sem("up_yhi"), sem("up_ylo")
            units = [(br, b) for br in (1, 2, 0) for b in range(WB)]
            with nc.Block() as block:
                @block.sync
                def _(sp):
                    for u, (br, b) in enumerate(units):
                        if u >= 2:
                            sp.wait_ge(lo, u - 1)
                        sp.dma_start(y[:, u % 2], e.y_scr[br, :, b, :]).then_inc(loaded[u % 2], 16)
                        sp.dma_start(z[:, u % 2], e.scratch[zs[br] + b, :, 1:1 + NT]).then_inc(loaded[u % 2], 16)

                @block.scalar
                def _(act):
                    def high(u):
                        br, b = units[u]
                        act.wait_ge(prod, u + 1)
                        act.activation(yh[:, br, b], y[:, u % 2], ACT.Copy).then_inc(hi, 1)
                    for u in range(len(units)):
                        act.wait_ge(loaded[u % 2], 32 * (u // 2 + 1))
                        act.activation(z[:, u % 2], z[:, u % 2], ACT.Silu).then_inc(silu, 1)
                        if u:
                            high(u - 1)
                    high(len(units) - 1)

                @block.vector
                def _(dve):
                    def low(u):
                        br, b = units[u]
                        dve.wait_ge(hi, u + 1)
                        dve.tensor_tensor(yl[:, br, b], y[:, u % 2], yh[:, br, b].bitcast(F32), ALU.subtract).then_inc(lo, 1)
                    for u in range(len(units)):
                        dve.wait_ge(silu, u + 1)
                        dve.tensor_tensor(y[:, u % 2], y[:, u % 2], z[:, u % 2], ALU.mult).then_inc(prod, 1)
                        if u:
                            low(u - 1)
                    low(len(units) - 1)

        sb = lambda n, s, d=F32: ctx.enter_context(nc.sbuf_tensor(n, s, d))
        wst, whi, wlo = sb("up_w", [P, 2, WB, P]), sb("up_w_hi", [P, 2, WB, P], F32R), sb("up_w_lo", [P, 2, WB, P], F32R)
        gate = sb("up_gate", [P, 2, NT])
        gu = sb("up_gu", [P, 2, CH[0][1]])
        acc = sb("up_acc", [P, NT])
        ps = [ctx.enter_context(nc.psum_tensor(f"up_ps{i}", [P, 512], F32)) for i in range(6)]
        w_loaded = [sem(f"upw_loaded{i}") for i in range(2)]
        g_loaded = [sem(f"upg_loaded{i}") for i in range(2)]
        w_hi, w_lo, mm_done, sig, gated, summed, m_hi, m_lo = [sem("up_" + n) for n in ("w_hi", "w_lo", "mm", "sig", "gated", "summed", "m_hi", "m_lo")]
        UN = 2 * NB3
        with nc.Block() as block:
            @block.sync
            def _(sp):
                def load(i, u, first):
                    m, br = i * 2 + u // 3, u % 3
                    if not (first and u < 2):
                        sp.wait_ge(w_lo, i * UN + (u - 1))
                    sp.dma_start(wst[:, u % 2], w_up[br][0].rearrange("(k p) (m n) -> m p k n", p=P, n=P)[m]).then_inc(w_loaded[u % 2], 16)
                    if not (first and u < 2):
                        sp.wait_ge(gated, i * (3 * UN) + 3 * (u - 1))
                    sp.dma_start(gate[:, u % 2], e.scratch[B_GATE + br * KT:B_GATE + (br + 1) * KT][m, :, 1:1 + NT]).then_inc(g_loaded[u % 2], 16)
                for u in range(UN):
                    load(0, u, True)
                with sp.Fori(1, KT // 2) as i:
                    for u in range(UN):
                        load(i, u, False)

            @block.scalar
            def _(act):
                def body(i, first):
                    for u in range(UN):
                        act.wait_ge(w_loaded[u % 2], i * (16 * 3) + 16 * (u // 2 + 1))
                        if not (first and u < 2):
                            act.wait_ge(mm_done, i * (3 * UN) + 3 * (u - 1))
                        act.activation(whi[:, u % 2], wst[:, u % 2], ACT.Copy).then_inc(w_hi, 1)
                        act.wait_ge(g_loaded[u % 2], i * (16 * 3) + 16 * (u // 2 + 1))
                        act.activation(gate[:, u % 2], gate[:, u % 2], ACT.Sigmoid).then_inc(sig, 1)
                        if u in (0, 3) and not (first and u == 0):
                            merged_hi(i, u)

                def merged_hi(i, u):
                    act.wait_ge(summed, i * (3 * UN) + 3 * u)
                    act.activation(e.m_hi[:, i * 2 + (u // 3 - 1)], acc[:, :], ACT.Copy).then_inc(m_hi, 1)
                body(0, True)
                with act.Fori(1, KT // 2) as i:
                    body(i, False)
                merged_hi(KT // 2, 0)

            @block.gpsimd
            def _(pool):
                def merged_lo(i, u):
                    pool.wait_ge(m_hi, i * 2 + u // 3)
                    pool.tensor_tensor(e.m_lo[:, i * 2 + (u // 3 - 1)], acc[:, :], e.m_hi[:, i * 2 + (u // 3 - 1)].bitcast(F32), ALU.subtract).then_inc(m_lo, 1)

                def body(i, first):
                    for u in range(UN):
                        pool.wait_ge(w_hi, i * UN + (u + 1))
                        if not (first and u < 2):
                            pool.wait_ge(mm_done, i * (3 * UN) + 3 * (u - 1))
                        pool.tensor_tensor(wlo[:, u % 2], wst[:, u % 2], whi[:, u % 2].bitcast(F32), ALU.subtract).then_inc(w_lo, 1)
                        if u in (0, 3) and not (first and u == 0):
                            merged_lo(i, u)
                body(0, True)
                with pool.Fori(1, KT // 2) as i:
                    body(i, False)
                merged_lo(KT // 2, 0)
                pool.wait_ge(m_lo, KT)

            @block.tensor
            def _(pe):
                def body(i, first):
                    for u in range(UN):
                        br = u % 3
                        pe.wait_ge(w_lo, i * UN + (u + 1))
                        for c, (at, n) in enumerate(CH):
                            q = 3 * u + c
                            if not (first and q < 6):
                                pe.wait_ge(gated, i * (3 * UN) + (q - 5))
                            for k in range(WB):
                                mm = split_mm(pe, ps[q % 6][:, 0:n], whi[:, u % 2, k], wlo[:, u % 2, k], yh[:, br, k, at:at + n],
                                              yl[:, br, k, at:at + n], k == 0, k == WB - 1)
                            mm.then_inc(mm_done, 1)
                body(0, True)
                with pe.Fori(1, KT // 2) as i:
                    body(i, False)

            @block.vector
            def _(dve):
                def body(i, first):
                    for u in range(UN):
                        dve.wait_ge(sig, i * UN + (u + 1))
                        if u in (0, 3) and not (first and u == 0):
                            dve.wait_ge(m_lo, i * 2 + u // 3)
                        for c, (at, n) in enumerate(CH):
                            q = 3 * u + c
                            dve.wait_ge(mm_done, i * (3 * UN) + (q + 1))
                            dst = acc[:, at:at + n] if u % 3 == 0 else gu[:, q % 2, 0:n]
                            dve.tensor_tensor(dst, ps[q % 6][:, 0:n], gate[:, u % 2, at:at + n], ALU.mult).then_inc(gated, 1)
                            dve.wait_ge(gated, i * (3 * UN) + (q + 1))
                            if u % 3 == 0:
                                dve.sem_inc(summed, 1)
                            else:
                                dve.tensor_tensor(acc[:, at:at + n], acc[:, at:at + n], dst, ALU.add).then_inc(summed, 1)
                                dve.wait_ge(summed, i * (3 * UN) + (q + 1))
                body(0, True)
                with dve.Fori(1, KT // 2) as i:
                    body(i, False)


def phase_out(nc, io, e):
    with ExitStack() as ctx:
        sem = lambda n: ctx.enter_context(nc.semaphore(n))
        sb = lambda n, s, d=F32: ctx.enter_context(nc.sbuf_tensor(n, s, d))
        wst = sb("wo", [P, 2, D])
        whi, wlo = sb("wo_hi", [P, KT, D], F32R), sb("wo_lo", [P, KT, D], F32R)
        gpost = sb("gpost_row", [P, D])
        xt, yt = sb("x_res", [P, 2, D]), sb("y_out_tile", [P, 2, D])
        junk = sb("out_junk", [P, 512])
        ss, s1, root, rstd = sb("o_ss", [P, 2, 9]), sb("o_s1", [P, 9]), sb("o_root", [P, 9]), sb("o_rstd", [P, 9])
        ps = [ctx.enter_context(nc.psum_tensor(f"out_ps{i}", [P, 512], F32)) for i in range(8)]
        w_loaded = [sem(f"wo_loaded{i}") for i in range(2)]
        x_loaded = [sem(f"xr_loaded{i}") for i in range(2)]
        y_stored = [sem(f"yo_stored{i}") for i in range(2)]
        g_loaded, w_hi, w_lo, mm_done, sq, s1_done, root_done, rs, normed, summed = [sem("o_" + n) for n in (
            "g_loaded", "w_hi", "w_lo", "mm", "sq", "s1_done", "root_done", "rs", "normed", "summed")]
        tiles = [(t * P, P if t < TILES else NB * NS) for t in range(TILES + 1)]
        with nc.Block() as block:
            @block.sync
            def _(sp):
                def rows(name, t, n):
                    a = io[name] if name[0] == "x" else e.outs[name]
                    return a[0, t * P:t * P + n, :] if t < TILES else a.rearrange("b t d -> (b t) d")

                def load_x(t):
                    n = tiles[t][1]
                    sp.dma_start(xt[0:n, t % 2], rows("x_prompt" if t < TILES else "x_sample", t, n)).then_inc(x_loaded[t % 2], 16)
                for k in range(KT):
                    if k >= 2:
                        sp.wait_ge(w_lo, k - 1)
                    sp.dma_start(wst[:, k % 2], io["w_o"][0, k * P:(k + 1) * P, :]).then_inc(w_loaded[k % 2], 16)
                sp.dma_start(gpost[:, :], io["norm_post"].to_broadcast((P, D))).then_inc(g_loaded, 16)
                load_x(0)
                load_x(1)
                for t, (at, n) in enumerate(tiles):
                    sp.wait_ge(summed, t + 1)
                    sp.dma_start(rows("y_prompt" if t < TILES else "y_sample", t, n), yt[0:n, t % 2]).then_inc(y_stored[t % 2], 16)
                    if t + 2 < len(tiles):
                        load_x(t + 2)
                sp.wait_ge(y_stored[0], 16 * 5)
                sp.wait_ge(y_stored[1], 16 * 4)

            @block.gpsimd
            def _(pool):
                for k in range(KT):
                    pool.wait_ge(w_hi, k + 1)
                    pool.tensor_tensor(wlo[:, k], wst[:, k % 2], whi[:, k].bitcast(F32), ALU.subtract).then_inc(w_lo, 1)

            @block.tensor
            def _(pe):
                for t, (at, n) in enumerate(tiles):
                    if t >= 4:
                        pe.wait_ge(normed, 2 * (t - 3))
                    for k in range(KT):
                        if t == 0:
                            pe.wait_ge(w_lo, k + 1)
                        for h in range(2):
                            d = slice(512 * h, 512 * h + 512)
                            mm = split_mm(pe, ps[2 * (t % 4) + h][0:n, :], e.m_hi[:, k, at:at + n], e.m_lo[:, k, at:at + n],
                                          whi[:, k, d], wlo[:, k, d], k == 0, k == KT - 1)
                    mm.then_inc(mm_done, 1)

            @block.scalar
            def _(act):
                for k in range(KT):
                    act.wait_ge(w_loaded[k % 2], 16 * (k // 2 + 1))
                    act.activation(whi[:, k], wst[:, k % 2], ACT.Copy).then_inc(w_hi, 1)
                for t, (at, n) in enumerate(tiles):
                    act.wait_ge(mm_done, t + 1)
                    for h in range(2):
                        if t or h:
                            act.wait_ge(sq, 2 * t + h)
                        act.activation(junk[0:n, :], ps[2 * (t % 4) + h][0:n, :], ACT.Square, accum_out=ss[0:n, h, t:t + 1]).then_inc(sq, 1)
                    act.wait_ge(s1_done, t + 1)
                    act.activation(root[0:n, t:t + 1], s1[0:n, t:t + 1], ACT.Sqrt, scale=1.0 / D, bias=e.eps[0:n, 0:1]).then_inc(root_done, 1)

            @block.vector
            def _(dve):
                dve.wait_ge(g_loaded, 16)
                for t, (at, n) in enumerate(tiles):
                    dve.wait_ge(sq, 2 * t + 2)
                    dve.tensor_tensor(s1[0:n, t:t + 1], ss[0:n, 0, t:t + 1], ss[0:n, 1, t:t + 1], ALU.add).then_inc(s1_done, 1)
                    dve.wait_ge(root_done, t + 1)
                    dve.reciprocal(rstd[0:n, t:t + 1], root[0:n, t:t + 1]).then_inc(rs, 1)
                    dve.wait_ge(rs, t + 1)
                    if t >= 2:
                        dve.wait_ge(y_stored[t % 2], 16 * (t // 2))
                    for h in range(2):
                        d = slice(512 * h, 512 * h + 512)
                        dve.scalar_tensor_tensor(out=yt[0:n, t % 2, d], in0=ps[2 * (t % 4) + h][0:n, :], scalar=rstd[0:n, t:t + 1],
                                                 in1=gpost[0:n, d], op0=ALU.mult, op1=ALU.mult).then_inc(normed, 1)
                    dve.wait_ge(x_loaded[t % 2], 16 * (t // 2 + 1))
                    dve.wait_ge(normed, 2 * t + 2)
                    dve.tensor_tensor(yt[0:n, t % 2], yt[0:n, t % 2], xt[0:n, t % 2], ALU.add).then_inc(summed, 1)


def build(nc, io, outs):
    e = Env()
    e.outs = outs
    dram = lambda n, s: nc.dram_tensor(n, s, F32).ap()
    e.scratch = dram("projected", (NIN, P, NT + 1))
    e.y_scr = dram("y_branches", (3, P, WB, NT))
    e.s0t_scr = dram("s0_turned", (HD, NB * H, HD))
    e.u5_scr = dram("s5_u_chunks", (P, WB, L5, J5))
    e.y5_scr = dram("s5_y_chunks", (P, G, J5))
    with ExitStack() as ctx:
        sb = lambda n, s, d=F32: ctx.enter_context(nc.sbuf_tensor(n, s, d))
        e.ident = sb("ident", [P, P])[:, :]
        e.ident_b = sb("ident_b", [P, P])
        e.vec = sb("vec", [P, NVEC])
        e.eps = sb("eps", [P, 2])
        e.s_a = sb("s_a", [P, 4, HD])
        with ExitStack() as rctx:
            sb = lambda n, s, d=F32: rctx.enter_context(nc.sbuf_tensor(n, s, d))
            e.ones_bd = sb("ones_bd", [P, P])[:, :]
            e.lv = sb("level_masks", [P, 5, P])[:, :, :]
            e.up_strict = sb("up_strict", [P, C])[:, :]
            e.up_incl = sb("up_incl", [P, C])[:, :]
            e.pair_ts = sb("pair_ts", [P, C])[:, :]
            e.pair_st = sb("pair_st", [P, C])[:, :]
            e.s_strict = sb("s_strict", [NB * NS, C])[:, :]
            e.s_incl = sb("s_incl", [NB * NS, C])[:, :]
            e.keep_p = sb("keep_p", [P, WB * P])[:, :]
            e.keep_s = sb("keep_s", [P, WB * NB * NS])[:, :]
            e.seq_of = sb("seq_of", [NB * NS, NB])[:, :]
            e.one_minus_ka = sb("one_minus_ka", [P, 4])
            e.shiftT = sb("shiftT", [P, RB, NB])[:, :, :]
            e.lora_w = sb("lora_w", [P, W])
            phase_setup(nc, io, e)
            e.h_hi = sb("h_hi", [P, KT, NT], F32R)
            e.h_lo = sb("h_lo", [P, KT, NT], F32R)
            phase_norm(nc, io, e)
            phase_project(nc, io, e)
            phase_states(nc, io, e)
            with nc.cleanup_on_exit():
                phase_rwkv(nc, io, e)
        phase_pool(nc, io, e)
        with ExitStack() as sctx:
            sb = lambda n, s, d=F32: sctx.enter_context(nc.sbuf_tensor(n, s, d))
            e.es = sb("s5_es", [P, 2, G, P])
            e.dtab = sb("s5_dtab", [P, G, L5 + 1, GC])
            e.toep = sb("s5_toep", [P, G, P])
            e.rot = sb("s5_rot", [P, 2, G, JP])
            e.u5 = sb("s5_u", [P, G, J5])
            e.hprev = sb("s5_hprev", [P, G, J5])
            e.mag8 = sb("s5_mag8", [P, G])[:, :]
            e.h0 = sb("s5_h0", [P, 2, NB, G])
            e.a8 = sb("s5_a8", [P, 2, G])
            e.u5_sem = sctx.enter_context(nc.semaphore("u5_chunks_loaded"))
            phase_s5_tables(nc, io, e)
            phase_s5(nc, io, e)
        phase_glu(nc, io, e)
        sb = lambda n, s, d=F32: ctx.enter_context(nc.sbuf_tensor(n, s, d))
        e.m_hi = sb("merged_hi", [P, KT, NT], F32R)
        e.m_lo = sb("merged_lo", [P, KT, NT], F32R)
        phase_up(nc, io, e)
        phase_out(nc, io, e)


_INS = (
    "x_prompt",
    "x_sample",
    "state_s5_re",
    "state_s5_im",
    "state_rwkv",
    "state_shift",
    "state_pool",
    "norm_pre",
    "norm_post",
    "w_in",
    "s5_lam_re",
    "s5_lam_im",
    "s5_log_dt",
    "s5_b_re",
    "s5_b_im",
    "s5_c_re",
    "s5_c_im",
    "s5_d",
    "s5_w_glu",
    "rwkv_mu",
    "rwkv_w0",
    "rwkv_w_w2",
    "rwkv_a0",
    "rwkv_w_a2",
    "rwkv_k_k",
    "rwkv_k_a",
    "rwkv_r_k",
    "rwkv_gn_w",
    "rwkv_gn_b",
    "pool_w",
    "pool_scale",
    "w_up_s5",
    "w_up_rwkv",
    "w_up_pool",
    "w_o",
)
_OUTS = (
    ("y_prompt", (1, 1024, 1024)),
    ("y_sample", (8, 8, 1024)),
    ("p_s5_re", (1, 1, 32, 64)),
    ("p_s5_im", (1, 1, 32, 64)),
    ("p_rwkv", (1, 1, 8, 64, 64)),
    ("p_shift", (1, 1, 1664)),
    ("p_pool", (1, 1, 15, 512)),
    ("s_s5_re", (1, 8, 32, 64)),
    ("s_s5_im", (1, 8, 32, 64)),
    ("s_rwkv", (1, 8, 8, 64, 64)),
    ("s_shift", (1, 8, 1664)),
    ("s_pool", (1, 8, 15, 512)),
)


def kernel(**inputs):
    import numpy as _np
    import concourse.bacc as _bacc
    from concourse import mybir as _mybir
    from concourse.bass_utils import run_bass_kernel_spmd as _run

    nc = _bacc.Bacc("TRN2", target_bir_lowering=False, num_devices=1)
    arrays, io, outs = {}, {}, {}
    for name in _INS:
        a = _np.ascontiguousarray(inputs[name])
        arrays[f"in_{name}_dram"] = a
        io[name] = nc.dram_tensor(f"in_{name}_dram", a.shape, _mybir.dt.from_np(a.dtype), kind="ExternalInput").ap()
    for name, shape in _OUTS:
        outs[name] = nc.dram_tensor(f"out_{name}_dram", shape, _mybir.dt.float32, kind="ExternalOutput").ap()
    build(nc, io, outs)
    r = _run(nc, [arrays], core_ids=[0])
    return tuple(r.results[0][f"out_{name}_dram"] for name, _ in _OUTS)
```

```python
from contextlib import ExitStack

import numpy as np

import concourse.bass as bass
from concourse import mybir

ALU = mybir.AluOpType
ACT = mybir.ActivationFunctionType
AX = mybir.AxisListType
F32 = mybir.dt.float32
F32R = mybir.dt.float32r

P = 128
D = 1024
KT = D // P
SEQ = 1024
NB, NS = 8, 8
NT = SEQ + NB * NS
W = 512
WB = W // P
H, HD = 8, 64
C = 64
RB = 13
G, GC = 32, 16
L5 = 8
J5 = NT // L5
JP = SEQ // L5
WIN = (2, 4, 8, 16)
BUF = 15
TILES = SEQ // P
NIN = 57
B_S5X, B_S5Z, B_RW, B_RWZ, B_PLX, B_PLZ, B_GATE = 0, 4, 8, 21, 25, 29, 33
CH = [(0, 384), (384, 384), (768, 320)]
NORM_EPS, GN_EPS = 1e-6, 64e-5
DEC = 0.6065306597126334

MAGIC = 1.5 * 2.0 ** 23
_C2 = float(np.float32(np.round((2 * np.pi - 6.28125) * 2.0 ** 20) / 2.0 ** 20))
TURN = (6.28125, _C2, 2 * np.pi - 6.28125 - _C2)
PI_IN = 3.1415925
LN2 = float(np.log(2.0))
LN2_PARTS = (0.693359375, LN2 - 0.693359375)
EXP_FACT = (1.0, 2.0, 6.0, 24.0, 120.0, 720.0, 5040.0)

VECS = [("mu", 13), ("w0", 4), ("a0", 4), ("k_k", 4), ("k_a", 4), ("r_k", 4), ("gn_w", 4), ("gn_b", 4),
        ("pool_scale", 4), ("s5_d", 4)]
VAT, _n = {}, 0
for _name, _k in VECS:
    VAT[_name] = (_n, _k)
    _n += _k
NVEC = _n


class Chain:

    def __init__(self, eng, sem, base=0):
        self.eng, self.sem, self.base, self.n = eng, sem, base, 0

    def after(self, ins):
        ins.then_inc(self.sem, 1)
        self.n += 1

    def wait(self, back=0):
        self.eng.wait_ge(self.sem, self.base + (self.n - back))


class Env:
    pass


def phase_start(nc, io, e):
    with nc.semaphore("ident_made") as made, nc.semaphore("eps_made") as eps, nc.Block() as block:
        @block.sync
        def _(sp):
            for t in range(3):
                sp.dma_start(e.xt[:, t, :], io["x_prompt"][0, t * P:(t + 1) * P, :]).then_inc(e.x_loaded[t], 16)
            sp.dma_start(e.gpre_row[:, :], io["norm_pre"].to_broadcast((P, D))).then_inc(e.g_loaded, 16)

        @block.gpsimd
        def _(pool):
            pool.memset(e.ident, 0.0).then_inc(made, 1)
            pool.wait_ge(made, 1)
            pool.affine_select(out=e.ident, in_=e.ident, compare_op=ALU.not_equal, fill=1.0, base=0, pattern=[[-1, P]],
                               channel_multiplier=1).then_inc(made, 1)
            pool.wait_ge(made, 2)

        @block.vector
        def _(dve):
            dve.memset(e.eps[:, 0:1], NORM_EPS).then_inc(eps, 1)
            dve.memset(e.eps[:, 1:2], GN_EPS).then_inc(eps, 1)
            dve.wait_ge(eps, 2)


class Setup:

    def __init__(self, nc, io, e, ctx):
        sem = lambda n: ctx.enter_context(nc.semaphore(n))
        self.io, self.e = io, e
        self.rows = ctx.enter_context(nc.sbuf_tensor("vec_rows", [NVEC, P], F32))
        self.shift = ctx.enter_context(nc.sbuf_tensor("shift_rows", [NB, RB * P], F32))
        self.ps = ctx.enter_context(nc.psum_tensor("setup_ps", [P, 512], F32))
        self.ps2 = ctx.enter_context(nc.psum_tensor("setup_ps2", [P, 512], F32))
        self.loaded, self.masks, self.flipped, self.made = sem("setup_loaded"), sem("setup_masks"), sem("setup_flipped"), sem("setup_made")

    def sync(self, sp):
        io, e, rows, shift, loaded = self.io, self.e, self.rows, self.shift, self.loaded
        vsrc = {"mu": io["rwkv_mu"], "w0": io["rwkv_w0"], "a0": io["rwkv_a0"], "k_k": io["rwkv_k_k"],
                "k_a": io["rwkv_k_a"], "r_k": io["rwkv_r_k"].rearrange("l h n -> l (h n)"), "gn_w": io["rwkv_gn_w"],
                "gn_b": io["rwkv_gn_b"], "pool_scale": io["pool_scale"], "s5_d": io["s5_d"]}
        for name, (at, k) in VAT.items():
            sp.dma_start(rows[at:at + k, :], vsrc[name][0].rearrange("(b p) -> b p", p=P)).then_inc(loaded, 16)
        sp.dma_start(shift[:, :], io["state_shift"][0]).then_inc(loaded, 16)
        sp.dma_start(e.lora_w[0:64, :], io["rwkv_w_w2"][0]).then_inc(loaded, 16)
        sp.dma_start(e.lora_w[64:128, :], io["rwkv_w_a2"][0]).then_inc(loaded, 16)

    def gpsimd(self, pool):
        e, masks = self.e, self.masks
        ch = Chain(pool, masks)

        def select(out, base, pattern, mult, fill=0.0, op=ALU.is_ge):
            ch.wait()
            ch.after(pool.affine_select(out=out, in_=out, compare_op=op, fill=fill, base=base,
                                        pattern=pattern, channel_multiplier=mult))

        for t, v in ((e.ones_bd, 1.0), (e.lv, 0.0), (e.up_strict, 1.0), (e.up_incl, 1.0),
                     (e.pair_st, 0.0), (e.s_strict, 1.0), (e.s_incl, 1.0),
                     (e.keep_p, 1.0), (e.keep_s, 1.0), (e.seq_of, 1.0)):
            ch.after(pool.memset(t, v))
        ch.wait()
        bd = e.ones_bd.rearrange("p (q r) -> p q r", r=HD)
        select(bd, 0, [[-HD, 2], [0, HD]], 1)
        select(bd, HD - 1, [[HD, 2], [0, HD]], -1)
        for n in range(5):
            b = 2 << n
            v = e.lv[:, n, :].rearrange("p (q h r) -> p q h r", h=2, r=b)[:, :, 0, :]
            ch.wait()
            ch.after(pool.memset(v, 1.0))
            select(v, -b, [[-2 * b, P // (2 * b)], [0, b]], 1)
            select(v, 2 * b - 1, [[2 * b, P // (2 * b)], [0, b]], -1)
        for h0 in (0, C):
            select(e.up_strict[h0:h0 + C, :], -1, [[1, C]], -1)
            select(e.up_incl[h0:h0 + C, :], 0, [[1, C]], -1)
            select(e.pair_st[h0:h0 + C, :].rearrange("p (q h) -> p q h", h=2)[:, :, 1], 0, [[-2, C // 2]], 1, -1.0, ALU.not_equal)
        for m, off in ((e.s_strict, -1), (e.s_incl, 0)):
            v = m.rearrange("p (q r) -> p q r", r=NS)
            select(v, off, [[NS, NB], [1, NS]], -1)
            select(v, 0, [[-NS, NB], [0, NS]], 1)
            select(v, NS - 1, [[NS, NB], [0, NS]], -1)
        select(e.seq_of, 0, [[-NS, NB]], 1)
        select(e.seq_of, NS - 1, [[NS, NB]], -1)
        ch.wait()
        ch.after(pool.memset(e.keep_p.rearrange("p (q r) -> p q r", r=C)[:, :, 0:1], 0.0))
        ch.after(pool.memset(e.keep_s.rearrange("p (q r) -> p q r", r=NS)[:, :, 0:1], 0.0))
        ch.wait()

    def tensor(self, pe):
        e, rows, shift, ps, ps2, loaded, flipped = self.e, self.rows, self.shift, self.ps, self.ps2, self.loaded, self.flipped
        n_loads = len(VECS) + 3
        pe.wait_ge(loaded, 16 * n_loads)
        pe.transpose(ps[:, 0:NVEC], rows[:, :], e.ident[0:NVEC, 0:NVEC]).then_inc(flipped, 1)
        for b in range(RB):
            pe.transpose(ps2[:, b * NB:(b + 1) * NB], shift[:, b * P:(b + 1) * P],
                         e.ident[0:NB, 0:NB]).then_inc(flipped, 1)

    def vector(self, dve):
        e, ps, ps2, flipped, made = self.e, self.ps, self.ps2, self.flipped, self.made
        ch = Chain(dve, made)
        dve.wait_ge(flipped, 1 + RB)
        ch.after(dve.tensor_copy(e.vec[:, :], ps[:, 0:NVEC]))
        ch.after(dve.tensor_copy(e.shiftT.rearrange("p r b -> p (r b)"), ps2[:, 0:RB * NB]))
        ch.wait()
        at = VAT["k_a"][0]
        ch.after(dve.tensor_scalar(e.one_minus_ka[:, :], e.vec[:, at:at + 4], -1.0, 1.0, ALU.mult, ALU.add))
        ch.wait()


def phase_norm(nc, io, e):
    with ExitStack() as ctx:
        sem = lambda n: ctx.enter_context(nc.semaphore(n))
        sb = lambda n, s, d=F32: ctx.enter_context(nc.sbuf_tensor(n, s, d))
        xt, gpre_row, x_loaded, g_loaded = e.xt, e.gpre_row, e.x_loaded, e.g_loaded
        xn = sb("xn", [P, 2, D])
        junk = sb("junk", [P, D])
        ssum, root, rstd = sb("ssum", [P, 9]), sb("root", [P, 9]), sb("rstd", [P, 9])
        ps = [ctx.enter_context(nc.psum_tensor(f"hT{i}", [P, 512], F32)) for i in range(4)]
        sq_done, root_done, rs_done, xn_done, flipped, hi_done, lo_done = [sem(n) for n in (
            "sq_done", "root_done", "rs_done", "xn_done", "h_flipped", "hi_done", "lo_done")]
        tiles = [(t * P, P if t < TILES else NB * NS) for t in range(TILES + 1)]
        setup = Setup(nc, io, e, ctx)
        with nc.Block() as block:
            @block.sync
            def _(sp):
                for t, (at, n) in list(enumerate(tiles))[3:]:
                    sp.wait_ge(xn_done, t - 2)
                    sp.wait_ge(sq_done, t - 2)
                    src = io["x_prompt"][0, at:at + n, :] if t < TILES else io["x_sample"].rearrange("b t d -> (b t) d")
                    sp.dma_start(xt[0:n, t % 3, :], src).then_inc(x_loaded[t % 3], 16)
                    if t == 4:
                        for r in range(RW):
                            load_w(sp, io, e, r)
                setup.sync(sp)

            @block.scalar
            def _(act):
                def hi(t):
                    at, n = tiles[t]
                    act.wait_ge(flipped, t + 1)
                    for q in range(2):
                        v = ps[2 * (t % 2) + q][:, :].rearrange("p (k t) -> p k t", k=4)[:, :, 0:n]
                        act.activation(e.h_hi[:, 4 * q:4 * q + 4, at:at + n], v, ACT.Copy).then_inc(hi_done, 1)
                for t, (at, n) in enumerate(tiles):
                    act.wait_ge(x_loaded[t % 3], 16 * (t // 3 + 1))
                    if t:
                        act.wait_ge(sq_done, t)
                    act.activation(junk[0:n, :], xt[0:n, t % 3, :], ACT.Square, accum_out=ssum[0:n, t:t + 1]).then_inc(sq_done, 1)
                    act.wait_ge(sq_done, t + 1)
                    act.activation(root[0:n, t:t + 1], ssum[0:n, t:t + 1], ACT.Sqrt, scale=1.0 / D, bias=e.eps[0:n, 0:1]).then_inc(root_done, 1)
                    if t:
                        hi(t - 1)
                    if t >= 6:
                        r = t - 6
                        act.wait_ge(e.w_loaded[r], 16)
                        act.activation(e.whi[:, r], e.wst[:, r], ACT.Copy).then_inc(e.w_hi, 1)
                hi(len(tiles) - 1)

            @block.gpsimd
            def _(pool):
                setup.gpsimd(pool)
                for r in range(RW):
                    pool.wait_ge(e.w_hi, r + 1)
                    pool.tensor_tensor(e.wlo[:, r], e.wst[:, r], e.whi[:, r].bitcast(F32), ALU.subtract).then_inc(e.w_lo, 1)

            @block.vector
            def _(dve):
                def lo(t):
                    at, n = tiles[t]
                    for q in range(2):
                        dve.wait_ge(hi_done, 2 * t + q + 1)
                        v = ps[2 * (t % 2) + q][:, :].rearrange("p (k t) -> p k t", k=4)[:, :, 0:n]
                        dve.tensor_tensor(e.h_lo[:, 4 * q:4 * q + 4, at:at + n], v,
                                          e.h_hi[:, 4 * q:4 * q + 4, at:at + n].bitcast(F32), ALU.subtract).then_inc(lo_done, 1)
                dve.wait_ge(g_loaded, 16)
                for t, (at, n) in enumerate(tiles):
                    dve.wait_ge(root_done, t + 1)
                    dve.reciprocal(rstd[0:n, t:t + 1], root[0:n, t:t + 1]).then_inc(rs_done, 1)
                    dve.wait_ge(rs_done, t + 1)
                    if t >= 2:
                        dve.wait_ge(flipped, t - 1)
                    dve.scalar_tensor_tensor(out=xn[0:n, t % 2, :], in0=xt[0:n, t % 3, :], scalar=rstd[0:n, t:t + 1],
                                             in1=gpre_row[0:n, :], op0=ALU.mult, op1=ALU.mult).then_inc(xn_done, 1)
                    if t:
                        lo(t - 1)
                lo(len(tiles) - 1)
                setup.vector(dve)

            @block.tensor
            def _(pe):
                for t, (at, n) in enumerate(tiles):
                    pe.wait_ge(xn_done, t + 1)
                    if t >= 2:
                        pe.wait_ge(lo_done, 2 * (t - 1))
                    for k in range(KT):
                        mm = pe.transpose(ps[2 * (t % 2) + k // 4][:, (k % 4) * P:(k % 4) * P + n],
                                          xn[0:n, t % 2, k * P:(k + 1) * P], e.ident[0:n, 0:n])
                    mm.then_inc(flipped, 1)
                setup.tensor(pe)


FIRST_BLOCKS = [B_RW + b for b in range(RB)] + [B_S5X + b for b in range(4)] + [B_PLX + b for b in range(4)]
RW = 3


def load_w(sp, io, e, n):
    b = FIRST_BLOCKS[n]
    sp.dma_start(e.wst[:, n % RW], io["w_in"][0, :, b * P:(b + 1) * P].rearrange("(k p) m -> p k m", p=P)).then_inc(e.w_loaded[n % RW], 16)


def split_mm(pe, out, whi, wlo, xhi, xlo, first, last):
    pe.matmul(out, whi, xhi, start=first, stop=False)
    pe.matmul(out, whi, xlo, start=False, stop=False)
    return pe.matmul(out, wlo, xhi, start=False, stop=last)


def phase_project(nc, io, e):
    nq = NB * H // 2
    blocks, R = FIRST_BLOCKS, RW
    n_it = len(blocks) // R
    with ExitStack() as ctx:
        sem = lambda n: ctx.enter_context(nc.semaphore(n))
        sb = lambda n, s, d=F32: ctx.enter_context(nc.sbuf_tensor(n, s, d))
        wst, whi, wlo, w_loaded, hi_done, lo_done = e.wst, e.whi, e.wlo, e.w_loaded, e.w_hi, e.w_lo
        out = sb("proj_out", [P, R, NT + 1])
        ps = [ctx.enter_context(nc.psum_tensor(f"proj_ps{i}", [P, 512], F32)) for i in range(R)]
        stored = [sem(f"p_stored{i}") for i in range(R)]
        mm_done, ev_done, zero = [sem(n) for n in ("p_mm", "p_ev", "p_zero")]
        rows, turned = sb("state_rows", [P, nq, HD]), sb("state_turned", [HD, NB * H, HD])
        st_ps = [ctx.enter_context(nc.psum_tensor(f"st_ps{i}", [P, 512], F32)) for i in range(2)]
        c_ps = [ctx.enter_context(nc.psum_tensor(f"par_ps{i}", [P, 512], F32)) for i in range(2)]
        par, par_stored = MakeParams(nc, io, ctx, st_ps, c_ps), sem("par_stored")
        st_loaded, st_flipped, st_copied, st_stored = sem("st_loaded"), sem("st_flipped"), sem("st_copied"), sem("st_stored")
        def store(sp, n):
            sp.wait_ge(ev_done, 3 * (n + 1))
            sp.dma_start(e.scratch[blocks[n]], out[:, n % R, :]).then_inc(stored[n % R], 16)

        with nc.Block() as block:
            @block.sync
            def _(sp):
                for n, b in enumerate(blocks):
                    if n == R:
                        par.sync(sp)
                        sp.dma_start(rows[:, :, :], io["state_rwkv"].rearrange("l b h v k -> (l b h v) k")
                                     .rearrange("(q p) k -> p q k", p=P)).then_inc(st_loaded, 16)
                    if n == 3 * R:
                        sp.wait_ge(st_copied, nq // 4)
                        sp.dma_start(e.s0t_scr, turned[:, :, :]).then_inc(st_stored, 16)
                    if n == 5 * R:
                        sp.wait_ge(par.made, 1)
                        sp.dma_start(e.par_scr, par.tile[:, :]).then_inc(par_stored, 16)
                    if n >= R:
                        sp.wait_ge(lo_done, n - R + 1)
                        load_w(sp, io, e, n)
                    if n >= R:
                        store(sp, n - R)
                for n in range(len(blocks) - R, len(blocks)):
                    store(sp, n)
                for r in range(R):
                    sp.wait_ge(stored[r], 16 * n_it)
                sp.wait_ge(st_stored, 16)
                sp.wait_ge(par_stored, 16)

            @block.gpsimd
            def _(pool):
                for r in range(R):
                    pool.memset(out[:, r, 0:1], 0.0).then_inc(zero, 1)
                with pool.Fori(1, n_it) as i:
                    for r in range(R):
                        pool.wait_ge(hi_done, i * R + (r + 1))
                        pool.tensor_tensor(wlo[:, r], wst[:, r], whi[:, r].bitcast(F32), ALU.subtract).then_inc(lo_done, 1)

            @block.vector
            def _(dve):
                dve.memset(e.s_a[:, :, :], 0.0)
                par.vector_take(dve)
                for n in range(nq // 4):
                    dve.wait_ge(st_flipped, n + 1)
                    dve.tensor_copy(turned[:, 8 * n:8 * n + 8, :].rearrange("k q v -> k (q v)"), st_ps[n % 2][0:HD, :]).then_inc(st_copied, 1)
                par.vector(dve)

            @block.tensor
            def _(pe):
                def body(i, first):
                    for r in range(R):
                        pe.wait_ge(lo_done, i * R + (r + 1))
                        for c, (at, n) in enumerate(CH):
                            if not (first and r == 0):
                                pe.wait_ge(ev_done, i * (3 * R) + (3 * r + c - 2))
                            for k in range(KT):
                                mm = split_mm(pe, ps[c][:, 0:n], whi[:, r, k], wlo[:, r, k], e.h_hi[:, k, at:at + n],
                                              e.h_lo[:, k, at:at + n], k == 0, k == KT - 1)
                            mm.then_inc(mm_done, 1)
                body(0, True)
                par.tensor(pe, e)
                pe.wait_ge(st_loaded, 16)
                for n in range(nq // 4):
                    if n >= 2:
                        pe.wait_ge(st_copied, n - 1)
                    elif n == 0:
                        pe.wait_ge(par.taken, 4)
                    for q in range(4):
                        mm = pe.transpose(st_ps[n % 2][0:HD, q * P:(q + 1) * P], rows[:, 4 * n + q, :], e.ident)
                    mm.then_inc(st_flipped, 1)
                with pe.Fori(1, n_it) as i:
                    body(i, False)

            @block.scalar
            def _(act):
                def split(i, r):
                    act.wait_ge(w_loaded[r], (i + 1) * 16)
                    act.activation(whi[:, r], wst[:, r], ACT.Copy).then_inc(hi_done, 1)

                def body(i, first=False, last=False):
                    for r in range(R):
                        if not first:
                            act.wait_ge(stored[r], i * 16)
                        for c, (at, n) in enumerate(CH):
                            act.wait_ge(mm_done, i * (3 * R) + (3 * r + c + 1))
                            act.activation(out[:, r, 1 + at:1 + at + n], ps[c][:, 0:n], ACT.Copy).then_inc(ev_done, 1)
                        if not last:
                            split(i + 1, r)
                act.wait_ge(zero, R)
                body(0, first=True)
                par.scalar(act)
                with act.Fori(1, n_it - 1) as i:
                    body(i)
                body(n_it - 1, last=True)


FILL_BLOCKS = ([B_S5Z + b for b in range(4)] + [B_RWZ + b for b in range(4)] + [B_PLZ + b for b in range(4)]
               + [B_GATE + b for b in range(24)])
PIECES = 4
BEFORE = {"lora": 13, "ssq": 18, "turn": 24, "A": 25, "T": 28, "X0": 29, "TX0": 31, "X1": 34, "TX1": 35, "X2": 35, "TX2": 35,
          "X3": 35, "TX3": 35, "X4": 35, "TX4": 35, "Y": 35, "GU": 38, "RM": 39, "S0": 40, "O": 41, "ON": 44, "end": 48}


PROD = [((1, 2), 0), ((3, 5), 0), ((3, 5), 1), ((4, 0), 0)]
XB, TXB, XTB = (1, 2), (3, 5), (4, 0)


class Tile:

    def __init__(self, e, i, prompt):
        self.i, self.prompt = i, prompt
        self.T = P if prompt else NB * NS
        self.halves = (0, 1) if prompt else (0,)
        self.levels = 5 if prompt else 2
        self.strict = e.up_strict if prompt else e.s_strict
        self.incl = e.up_incl if prompt else e.s_incl
        self.keep = e.keep_p if prompt else e.keep_s
        self.step = C if prompt else NS

    def fv(self, t):
        return t[:, 0:4 * self.T].rearrange("p (b t) -> p b t", b=4)


def phase_rwkv(nc, io, e):
    with ExitStack() as ctx:
        sem = lambda n: nc.alloc_semaphore(name=n)
        sb = lambda n, s, d=F32: ctx.enter_context(nc.sbuf_tensor(n, s, d))
        wst, stage = sb("fw", [P, 2, KT, P]), sb("f_out", [P, 3, CH[0][1]])
        whi, wlo = sb("fw_hi", [P, 2, KT, P], F32R), sb("fw_lo", [P, 2, KT, P], F32R)
        fps = [ctx.enter_context(nc.psum_tensor(f"f_ps{i}", [P, 512], F32)) for i in range(2)]
        fw_loaded = [sem(f"fw_loaded{i}") for i in range(2)]
        f_stored = [sem(f"f_stored{i}") for i in range(3)]
        fw_hi, fw_lo, f_mm, f_free = sem("fw_hi"), sem("fw_lo"), sem("f_mm"), sem("f_bank_free")
        raw, dif, pm = sb("raw", [P, RB, P + 1]), sb("dif", [P, RB, P]), sb("pm", [P, RB, P])
        fm = lambda n: sb(n, [P, 4 * P])[:, :]
        tw = sb("tw", [64, P])
        sg, av, cs, pr, pi, kk0, sq, nr, kk, kf, bonus, y_tile = (fm(n) for n in (
            "sg_on", "a_bC", "cs_yv", "decay_prod", "decay_inv", "kk0_b", "sq_alpha_bonus", "norm_kC", "kk", "kf_gsq", "rk_bonus", "y_tile"))
        bb, bC, kC, alpha, bt, yv = kk0, av, nr, sq, sq, cs
        dflat = dif[:, :, :].rearrange("p r t -> p (r t)")
        beta, kappa, rho = (dflat[:, 4 * P * n:4 * P * (n + 1)] for n in range(3))
        ay, vt = sb("alpha_y", [P, H, P]), sb("v_t", [P, H, HD])
        bCt, kCt = sb("bC_t", [P, H, HD]), sb("kC_t", [P, H, HD])
        n_g, n_u = sb("neg_g", [P, H, HD]), sb("neg_u", [P, H, HD])
        ab_t, ak_t, rb_t, rk_t = (sb(n, [P, H, P]) for n in ("ab_t", "ak_t", "rb_t", "rk_t"))
        t_m, t_t, x_m = sb("t_m", [P, H, P]), sb("t_t", [P, H, P]), sb("x_m", [P, H, P])
        tmp = y_tile.rearrange("p (h k) -> p h k", h=H)
        rp = pi.rearrange("p (b t) -> p b t", b=4)
        m_c, dpc = sb("m_c", [P, 2, 4, P]), sb("dpc", [P, 2, 4, P])
        s_b = sb("s_b", [P, 4, HD])
        s_bd, s_ad = x_m[:, 0:4, :], sb("s_ad", [P, 4, P])
        gsum, gneg, gvar, groot, grs = (sb(n, [P, H]) for n in ("gsum", "gneg", "gvar", "groot", "grs"))
        cen = tmp
        gsq, on = (x.rearrange("p (h k) -> p h k", h=H) for x in (kf, sg))
        Q = [ctx.enter_context(nc.psum_tensor(f"q{i}", [P, 512], F32)) for i in range(6)]
        ev = {n: sem("r_" + n) for n in (
            "raw_loaded", "pm", "tanh", "lora_mm", "gates", "sq", "ssq_mm", "floor", "root", "cs", "decay", "kf", "feat",
            "bonus", "turned", "turned_sb", "prod_mm", "t_init", "tm_mm", "tm_sb", "prod_sb", "x_mm", "x_sb", "tx_mm", "tx_sb", "tt_mm", "tt_sb", "y_mm", "y_sb",
            "gu_mm", "gu_sb", "rm_mm", "rp_sb", "dpc", "m_sb", "s0_mm", "s0_sb", "o_mm", "s1_mm", "s1_sb", "cen", "gsq",
            "gvar", "groot", "on", "on_mm", "y_out", "y_stored", "zeroed",
            "rpm", "mask_sb", "mz_mm", "mz_sb", "sn_mm", "sn_sb")}
        sn_out = [sem(f"r_sn_out{i}") for i in range(2)]
        s0_loaded = [sem(f"r_s0_loaded{i}") for i in range(2)]
        v = e.vec

        def vb(name, T, blocks=None):
            at, k = VAT[name]
            return v[:, at:at + k].rearrange("p (b o) -> p b o", o=1).to_broadcast((P, k, T))

        def pm_of(t, q):
            return pm[:, 4 * q:4 * q + 4, 0:t.T]

        def e4(t, q):
            return q[0:t.T, 0:4 * t.T].rearrange("p (h t) -> p h t", h=4)

        def level_at(t, n, q):
            return (t.i * 5 + n) * 2 + (q + 1)

        def turn_at(t, n, q):
            return (t.i * 4 + (n - 1)) * 2 + (q + 1)

        snew_b = m_c[0:HD, :, :, :].rearrange("p c q t -> p c (q t)").rearrange("p c (b k) -> p c b k", k=HD)
        two = lambda x, r: x[0:HD, :, :].rearrange("p h t -> p (h t)")[:, 512 * r:512 * r + 512].rearrange("p (q k) -> p q k", k=HD)
        rpm = [two(x, r) for x in (ab_t, ak_t, t_m, t_t) for r in range(2)]
        kcm, mz = [two(x_m, r) for r in range(2)], [two(ay, r) for r in range(2)]
        bcm = [dpc[0:HD, r].rearrange("p q t -> p (q t)").rearrange("p (q k) -> p q k", k=HD) for r in range(2)]
        dps, rps = (x[0:HD].rearrange("p (q k) -> p q k", k=HD) for x in (kk, pi))
        pc0 = sb("pc0", [HD, H, NB])[:, :, :]
        s0t = raw[0:HD].rearrange("p r t -> p (r t)")[:, 0:1024].rearrange("p (c q k) -> p c q k", c=2, k=HD)

        with nc.Block() as block:
            @block.sync
            def _(sp):
                def load_w(g):
                    if g >= 2:
                        sp.wait_ge(fw_lo, g - 1)
                    b = FILL_BLOCKS[g]
                    sp.dma_start(wst[:, g % 2], io["w_in"][0, :, b * P:(b + 1) * P].rearrange("(k p) m -> p k m", p=P)).then_inc(fw_loaded[g % 2], 16)

                def load_raw(i):
                    if i:
                        sp.wait_ge(ev["pm"], i)
                    src = e.scratch[B_RW:B_RW + RB].rearrange("b p t -> p b t")
                    if i < TILES:
                        sp.dma_start(raw[:, :, :], src[:, :, i * P:i * P + P + 1]).then_inc(ev["raw_loaded"], 16)
                    else:
                        sp.dma_start(raw[:, :, 0:NB * NS], src[:, :, 1 + SEQ:1 + NT]).then_inc(ev["raw_loaded"], 16)

                def store(g):
                    for c, (at, n) in enumerate(CH):
                        sp.wait_ge(f_free, 2 + 3 * g + c + 1)
                        sp.dma_start(e.scratch[FILL_BLOCKS[g], :, 1 + at:1 + at + n], stage[:, c, 0:n]).then_inc(f_stored[c], 16)

                def store_y(i):
                    sp.wait_ge(ev["y_out"], i + 1)
                    n = P if i < TILES else NB * NS
                    sp.dma_start(e.y_scr[1, :, :, i * P:i * P + n], y_tile[:, 0:4 * n].rearrange("p (b t) -> p b t", b=4)).then_inc(ev["y_stored"], 16)

                def new_out(h):
                    sp.wait_ge(ev["sn_sb"], h + 1)
                    sp.dma_start(e.outs["s_rwkv"][0, :, h].rearrange("b v k -> v b k"), snew_b[:, h % 2]).then_inc(sn_out[h % 2], 16)

                def load_s0(h):
                    sp.dma_start(s0t[:, h % 2], e.s0t_scr.rearrange("k (b h) v -> k h b v", h=H)[:, h]).then_inc(s0_loaded[h % 2], 16)

                n = len(FILL_BLOCKS)
                load_w(0)
                load_raw(0)
                load_w(1)
                for g in range(n):
                    if g + 2 < n:
                        load_w(g + 2)
                    if g % 4 == 1 and g // 4 < TILES:
                        load_raw(g // 4 + 1)
                    if g % 4 == 0 and g:
                        store_y(g // 4 - 1)
                    if g == n - 2:
                        sp.wait_ge(ev["pm"], TILES + 1)
                        load_s0(0)
                        load_s0(1)
                    if g < n - 1:
                        store(g)
                for h in range(2, H):
                    sp.wait_ge(ev["sn_mm"], h - 1)
                    load_s0(h)
                    new_out(h - 2)
                new_out(H - 2)
                new_out(H - 1)
                store(n - 1)
                for r in range(3):
                    sp.wait_ge(f_stored[r], 16 * n)
                store_y(TILES)
                sp.wait_ge(ev["y_stored"], 16 * (TILES + 1))
                for r in range(2):
                    sp.wait_ge(sn_out[r], 16 * (H // 2))

            @block.gpsimd
            def _(pool):
                def lo(r, count):
                    pool.wait_ge(fw_hi, count)
                    pool.tensor_tensor(wlo[:, r], wst[:, r], whi[:, r].bitcast(F32), ALU.subtract).then_inc(fw_lo, 1)

                lo(0, 1)
                lo(1, 2)
                for z in (ab_t, ak_t, rb_t, rk_t, t_t, s_ad):
                    pool.memset(z[:, :, :], 0.0).then_inc(ev["zeroed"], 1)

                def body(t):
                    i = t.i
                    fv = t.fv
                    n_lo = [0]

                    def lo_next():
                        if t.prompt or n_lo[0] < 2:
                            lo(n_lo[0] % 2, i * 4 + (3 + n_lo[0]))
                        n_lo[0] += 1
                    lo_next()
                    pool.wait_ge(ev["kf"], i + 1)
                    pool.tensor_tensor(fv(bonus), pm_of(t, 0), fv(kf), ALU.mult).then_inc(ev["bonus"], 1)
                    pool.wait_ge(ev["bonus"], i * 2 + 1)
                    pool.tensor_tensor(fv(bonus), fv(bonus), vb("r_k", t.T), ALU.mult).then_inc(ev["bonus"], 1)
                    pool.wait_ge(ev["decay"], i * 2 + 2)
                    if t.prompt:
                        for c in (0, 1):
                            pool.tensor_tensor(dpc[:, c], e.ident.rearrange("p (o t) -> p o t", o=1).to_broadcast((P, 4, P)),
                                               fv(pr)[:, :, C * c + C - 1:C * c + C].to_broadcast((P, 4, P)), ALU.mult).then_inc(ev["dpc"], 1)
                    lo_next()
                    lo_next()
                    lo_next()

                with pool.Fori(0, TILES) as i:
                    body(Tile(e, i, True))
                body(Tile(e, TILES, False))

            @block.scalar
            def _(act):
                def hi(r, count_loaded):
                    act.wait_ge(fw_loaded[r], count_loaded)
                    act.activation(whi[:, r], wst[:, r], ACT.Copy).then_inc(fw_hi, 1)
                hi(0, 16)
                hi(1, 16)
                act.sem_inc(f_free, 2)

                def body(t):
                    i, fv, T = t.i, t.fv, t.T
                    done = [0]

                    def evacuate(stage_name):
                        while done[0] < BEFORE[stage_name] // PIECES:
                            u = done[0]
                            r, (at, n) = (u // 3) % 2, CH[u % 3]
                            if not (t.first and u < 3):
                                act.wait_ge(f_stored[u % 3], (i * 4 + u // 3) * 16)
                            act.wait_ge(f_mm, i * 12 + (u + 1))
                            act.activation(stage[:, u % 3, 0:n], fps[u % 2][:, 0:n], ACT.Copy).then_inc(f_free, 1)
                            if u % 3 == 2 and (t.prompt or u < 6):
                                hi(r, (i * 2 + (u // 6 + 2)) * 16)
                            done[0] += 1

                    act.wait_ge(ev["pm"], i + 1)
                    act.activation(tw[:, 0:T], pm[0:64, 12, 0:T], ACT.Tanh).then_inc(ev["tanh"], 1)
                    evacuate("lora")
                    act.wait_ge(ev["lora_mm"], i + 1)
                    for b in range(4):
                        for q, (dst, name) in enumerate(((sg, "w0"), (av, "a0"))):
                            at = VAT[name][0] + b
                            act.activation(fv(dst)[:, b], Q[q][:, b * T:(b + 1) * T], ACT.Sigmoid,
                                           bias=v[:, at:at + 1]).then_inc(ev["gates"], 1)
                    act.wait_ge(ev["cs"], i + 1)
                    act.activation(pr[:, 0:4 * T], cs[:, 0:4 * T], ACT.Exp, scale=-DEC).then_inc(ev["decay"], 1)
                    act.activation(pi[:, 0:4 * T], cs[:, 0:4 * T], ACT.Exp, scale=DEC).then_inc(ev["decay"], 1)
                    evacuate("ssq")
                    act.wait_ge(ev["floor"], i + 1)
                    act.activation(nr[:, 0:4 * T], nr[:, 0:4 * T], ACT.Sqrt).then_inc(ev["root"], 1)
                    evacuate("turn")
                    for q, (bank, dst) in enumerate(((4, vt), (3, None), (5, bCt), (0, kCt))):
                        act.wait_ge(ev["turned"], i * 4 + (q + 1))
                        d = ay[0:T, :, 0:HD] if dst is None else dst[0:T]
                        act.activation(d, Q[bank][0:T, :].rearrange("p (h k) -> p h k", h=H), ACT.Copy).then_inc(ev["turned_sb"], 1)
                    evacuate("T")
                    for q in range(2):
                        act.wait_ge(ev["tm_mm"], i * 2 + (q + 1))
                        act.activation(t_m[0:T, 4 * q:4 * q + 4, 0:T], e4(t, Q[XB[q]]), ACT.Copy).then_inc(ev["tm_sb"], 1)
                    for n in range(1, t.levels):
                        evacuate(f"X{n}")
                        for q in range(2):
                            act.wait_ge(ev["tt_mm"], turn_at(t, n, q))
                            act.activation(t_t[0:T, 4 * q:4 * q + 4, 0:T], e4(t, Q[XTB[q]]), ACT.Copy).then_inc(ev["tt_sb"], 1)
                    evacuate("Y")
                    act.wait_ge(ev["y_mm"], i + 1)
                    act.activation(ay[0:T, :, HD:P], Q[1][0:T, :].rearrange("p (h k) -> p h k", h=H), ACT.Copy).then_inc(ev["y_sb"], 1)
                    for q in range(2):
                        act.wait_ge(ev["gu_mm"], i * 2 + (q + 1))
                        src = Q[TXB[q]][0:T, :].rearrange("p (h g k) -> p g h k", h=4, g=2)
                        act.activation(n_g[0:T, 4 * q:4 * q + 4, :], src[:, 0], ACT.Copy, scale=-1.0).then_inc(ev["gu_sb"], 1)
                        act.activation(n_u[0:T, 4 * q:4 * q + 4, :], src[:, 1], ACT.Copy, scale=-1.0).then_inc(ev["gu_sb"], 1)
                    evacuate("O")
                    if not t.prompt:
                        for h in range(H):
                            act.wait_ge(ev["sn_mm"], h + 1)
                            if h >= 2:
                                act.wait_ge(sn_out[h % 2], 16 * (h // 2))
                            act.activation(snew_b[:, h % 2], Q[TXB[h % 2]][0:HD, :].rearrange("p (b k) -> p b k", k=HD), ACT.Copy).then_inc(ev["sn_sb"], 1)
                    act.wait_ge(ev["cen"], i + 1)
                    act.activation(gsq[0:T], cen[0:T], ACT.Square).then_inc(ev["gsq"], 1)
                    act.wait_ge(ev["gvar"], i + 1)
                    act.activation(groot[0:T, :], gvar[0:T, :], ACT.Sqrt, scale=1.0 / HD, bias=e.eps[0:T, 1:2]).then_inc(ev["groot"], 1)
                    evacuate("end")

                t0 = Tile(e, 0, True)
                t0.first = True
                body(t0)
                with act.Fori(1, TILES) as i:
                    t = Tile(e, i, True)
                    t.first = False
                    body(t)
                t = Tile(e, TILES, False)
                t.first = False
                body(t)

            @block.vector
            def _(dve):
                ch_sem = sem("r_vec_chain")

                def body(t, base):
                    i, fv, T, step = t.i, t.fv, t.T, t.step
                    ch = Chain(dve, ch_sem, base)
                    tt = dve.tensor_tensor
                    dve.wait_ge(ev["raw_loaded"], i * 16 + 16)
                    if t.prompt:
                        cur = raw[:, :, 1:P + 1]
                        ch.after(tt(dif[:, :, :], raw[:, :, 0:P], cur, ALU.subtract))
                    else:
                        cur = raw[:, :, 0:T]
                        c4 = cur.rearrange("p r (b s) -> p r b s", s=NS)
                        d4 = dif[:, :, 0:T].rearrange("p r (b s) -> p r b s", s=NS)
                        ch.after(tt(d4[:, :, :, 1:NS], c4[:, :, :, 0:NS - 1], c4[:, :, :, 1:NS], ALU.subtract))
                        ch.after(tt(d4[:, :, :, 0], e.shiftT, c4[:, :, :, 0], ALU.subtract))
                    ch.wait()
                    ch.after(tt(dif[:, :, 0:T], dif[:, :, 0:T], vb("mu", T), ALU.mult))
                    ch.wait()
                    tt(pm[:, :, 0:T], dif[:, :, 0:T], cur, ALU.add).then_inc(ev["pm"], 1)
                    dve.wait_ge(ev["pm"], i + 1)
                    ch.after(tt(fv(kk0), pm_of(t, 1), vb("k_k", T), ALU.mult))
                    ch.wait()
                    tt(sq[:, 0:4 * T], kk0[:, 0:4 * T], kk0[:, 0:4 * T], ALU.mult).then_inc(ev["sq"], 1)
                    dve.wait_ge(ev["gates"], i * 8 + 8)
                    dve.tensor_tensor_scan(cs[:, 0:4 * T], t.keep, sg[:, 0:4 * T], 0.0, ALU.mult, ALU.add).then_inc(ev["cs"], 1)
                    for b in range(4):
                        at = VAT["k_a"][0] + b
                        ch.after(dve.tensor_scalar(fv(kf)[:, b], fv(av)[:, b], v[:, at:at + 1], e.one_minus_ka[:, b:b + 1], ALU.mult, ALU.add))
                    ch.wait()
                    tt(fv(kf), fv(kf), pm_of(t, 1), ALU.mult).then_inc(ev["kf"], 1)
                    dve.wait_ge(ev["ssq_mm"], i + 1)
                    dve.tensor_scalar(nr[:, 0:4 * T], Q[2][:, 0:4 * T], 1e-24, None, ALU.max).then_inc(ev["floor"], 1)
                    dve.wait_ge(ev["decay"], i * 2 + 2)
                    dve.wait_ge(ev["kf"], i + 1)
                    ch.after(tt(kappa[:, 0:4 * T], kf[:, 0:4 * T], pi[:, 0:4 * T], ALU.mult))
                    ch.after(tt(fv(rho), pm_of(t, 0), fv(pr), ALU.mult))
                    dve.wait_ge(ev["root"], i + 1)
                    ch.after(dve.reciprocal(nr[:, 0:4 * T], nr[:, 0:4 * T]))
                    ch.wait()
                    ch.after(tt(kk[:, 0:4 * T], kk0[:, 0:4 * T], nr[:, 0:4 * T], ALU.mult))
                    ch.wait()
                    ch.after(tt(bb[:, 0:4 * T], kk[:, 0:4 * T], av[:, 0:4 * T], ALU.mult))
                    q4 = lambda x: x[:, 0:4 * T].rearrange("p (q s) -> p q s", s=step)
                    ch.after(tt(q4(alpha)[:, :, 1:step], q4(kk)[:, :, 1:step], q4(pr)[:, :, 0:step - 1], ALU.mult))
                    dve.tensor_copy(q4(alpha)[:, :, 0:1], q4(kk)[:, :, 0:1]).then_inc(ev["feat"], 1)
                    ch.wait()
                    tt(beta[:, 0:4 * T], bb[:, 0:4 * T], pi[:, 0:4 * T], ALU.mult).then_inc(ev["feat"], 1)
                    dve.wait_ge(ev["feat"], i * 4 + 2)
                    pend = q4(pr)[:, :, step - 1:step].to_broadcast((P, 4 * T // step, step))
                    tt(q4(bC), q4(beta), pend, ALU.mult).then_inc(ev["feat"], 1)
                    tt(q4(kC), q4(kappa), pend, ALU.mult).then_inc(ev["feat"], 1)
                    def prod(n, par, lo_, cnt):
                        banks, z = PROD[n]
                        return Q[banks[par]][lo_:lo_ + cnt, 256 * z:256 * z + 256].rearrange("p (h t) -> p h t", h=4)
                    mb = lambda m, lo_, n: m[lo_:lo_ + n, :].rearrange("p (o t) -> p o t", o=1).to_broadcast((n, 4, C))
                    half = lambda x, par: x.rearrange("p (b o) t -> p b o t", o=2)[:, :, par]
                    blk = lambda x, c: x[C * c:C * c + C, :, C * c:C * c + C]
                    if t.first:
                        dve.wait_ge(ev["zeroed"], 6)
                    else:
                        dve.wait_ge(ev["y_stored"], i * 16)
                    dve.wait_ge(ev["prod_mm"], i * 4 + 1)
                    for par in (0, 1):
                        ch.after(tt(half(tmp[0:T], par), prod(0, par, 0, T), mb(e.pair_st, 0, T), ALU.mult))
                    for c in t.halves:
                        for par in (0, 1):
                            ch.after(tt(half(blk(ab_t, c), par), prod(0, par, C * c, C), mb(t.strict, C * c, C), ALU.mult))
                    ch.wait()
                    for c in t.halves:
                        idb = e.ident[C * c:C * c + C, C * c:C * c + C].rearrange("p (o t) -> p o t", o=1).to_broadcast((C, H, C))
                        tt(blk(t_t, c), tmp[C * c:C * c + C], idb, ALU.add).then_inc(ev["t_init"], 1)
                    for n, (dst, m) in enumerate(((ak_t, t.strict), (rk_t, t.incl), (rb_t, t.incl)), 1):
                        dve.wait_ge(ev["prod_mm"], i * 4 + (3, 3, 4)[n - 1])
                        for c in t.halves:
                            for par in (0, 1):
                                ins = tt(half(blk(dst, c), par), prod(n, par, C * c, C), mb(m, C * c, C), ALU.mult)
                                if c == t.halves[-1] and par:
                                    ins.then_inc(ev["prod_sb"], 1)
                                else:
                                    ch.after(ins)
                    for n in range(t.levels):
                        last = n == t.levels - 1
                        for q in range(2):
                            dve.wait_ge(ev["x_mm"], level_at(t, n, q))
                            tt(x_m[0:T, 4 * q:4 * q + 4, 0:T], e4(t, Q[XB[q]]), e.lv[0:T, n:n + 1, 0:T].to_broadcast((T, 4, T)), ALU.mult).then_inc(ev["x_sb"], 1)
                        for q in range(2):
                            dst, bank = (t_t, XTB[q]) if last else (t_m, TXB[q])
                            dve.wait_ge(ev["tx_mm"], level_at(t, n, q))
                            tt(dst[0:T, 4 * q:4 * q + 4, 0:T], dst[0:T, 4 * q:4 * q + 4, 0:T], e4(t, Q[bank]), ALU.subtract).then_inc(ev["tx_sb"], 1)
                    dve.wait_ge(ev["rm_mm"], i * 3 + 1)
                    if t.prompt:
                        tt(rp[:, :, :], Q[4][:, :].rearrange("p (b t) -> p b t", b=4), fv(rho), ALU.add).then_inc(ev["rp_sb"], 1)
                        for c in (0, 1):
                            dve.wait_ge(ev["rm_mm"], i * 3 + (2 + c))
                            ch.after(tt(m_c[:, c], Q[1 + c][:, :].rearrange("p (b t) -> p b t", b=4),
                                        e.ones_bd.rearrange("p (o t) -> p o t", o=1).to_broadcast((P, 4, P)), ALU.mult))
                            ch.wait()
                            dve.wait_ge(ev["dpc"], i * 2 + (c + 1))
                            tt(m_c[:, c], m_c[:, c], dpc[:, c], ALU.add).then_inc(ev["m_sb"], 1)
                        dve.wait_ge(ev["s0_mm"], i + 1)
                        new_s(s_b, s_bd, 3, ev["s0_sb"], ch)
                    else:
                        sample_states(t, ch)
                    dve.wait_ge(ev["o_mm"], i + 1)
                    o = Q[0][0:T, :].rearrange("p (h k) -> p h k", h=H)
                    b8 = lambda x: x[0:T, :].rearrange("p (h o) -> p h o", o=1).to_broadcast((T, H, HD))
                    ch.after(dve.tensor_reduce(gsum[0:T, :], o, AX.X, ALU.add))
                    ch.wait()
                    ch.after(dve.tensor_scalar(gneg[0:T, :], gsum[0:T, :], -1.0 / HD, None, ALU.mult))
                    ch.wait()
                    tt(cen[0:T], o, b8(gneg), ALU.add).then_inc(ev["cen"], 1)
                    if t.prompt:
                        dve.wait_ge(ev["s1_mm"], i + 1)
                        new_s(e.s_a, s_ad, 5, ev["s1_sb"], ch)
                    dve.wait_ge(ev["gsq"], i + 1)
                    dve.tensor_reduce(gvar[0:T, :], gsq[0:T], AX.X, ALU.add).then_inc(ev["gvar"], 1)
                    dve.wait_ge(ev["groot"], i + 1)
                    ch.after(dve.reciprocal(grs[0:T, :], groot[0:T, :]))
                    ch.wait()
                    tt(on[0:T], cen[0:T], b8(grs), ALU.mult).then_inc(ev["on"], 1)
                    ch.after(tt(fv(bt), Q[4][:, 0:4 * T].rearrange("p (b t) -> p b t", b=4), pm_of(t, 2), ALU.mult))
                    dve.wait_ge(ev["on_mm"], i + 1)
                    for b in range(4):
                        gw, gb = VAT["gn_w"][0] + b, VAT["gn_b"][0] + b
                        ch.after(dve.tensor_scalar(fv(yv)[:, b], Q[1][:, b * T:(b + 1) * T], v[:, gw:gw + 1], v[:, gb:gb + 1], ALU.mult, ALU.add))
                    ch.wait()
                    tt(y_tile[:, 0:4 * T], yv[:, 0:4 * T], bt[:, 0:4 * T], ALU.add).then_inc(ev["y_out"], 1)
                    dve.wait_ge(ev["y_out"], i + 1)
                    return ch.n

                def new_s(dst, dst_d, bank, done, ch):
                    src = Q[bank][:, 0:256].rearrange("p (b k) -> p b k", b=4)
                    for par in (0, 1):
                        h0 = slice(HD * par, HD * par + HD)
                        ch.after(dve.tensor_copy(dst_d[h0, :, h0], src[h0]))
                    ch.wait()
                    dve.tensor_copy(dst[:, :, :], src).then_inc(done, 1)

                def sample_states(t, ch):
                    tt = dve.tensor_tensor
                    T = t.T
                    pe_ = pr[:, 0:4 * T].rearrange("p (b q s) -> p b q s", b=4, s=NS)[:, :, :, NS - 1]
                    pc = pc0.rearrange("p (b o) q -> p b o q", o=2)
                    ch.after(dve.tensor_copy(pc[:, :, 0, :], pe_[0:HD]))
                    ch.after(dve.tensor_copy(pc[:, :, 1, :], pe_[HD:P]))
                    r4 = Q[4][0:HD, :].rearrange("p (b o t) -> p b o t", b=4, o=2)
                    rs = rps.rearrange("p (b o) t -> p b o t", o=2)
                    ch.after(tt(rs[:, :, 0], r4[:, :, 0], t.fv(rho)[0:HD], ALU.add))
                    ch.after(tt(rs[:, :, 1], r4[:, :, 1], t.fv(rho)[HD:P], ALU.add))
                    ch.wait()
                    for x in range(NB):
                        ch.after(dve.memset(rpm[x], 0.0))
                    ch.wait()
                    for x in range(NB):
                        dve.tensor_copy(rpm[x][:, :, NS * x:NS * x + NS], rps[:, :, NS * x:NS * x + NS]).then_inc(ev["rpm"], 1)
                    for h in range(H):
                        r = h % 2
                        sel = e.seq_of.rearrange("p (q o) -> p q o", o=1).to_broadcast((T, NB, HD))
                        if h >= 2:
                            dve.wait_ge(ev["sn_mm"], h - 1)
                        tt(bcm[r], sel, bCt[0:T, h:h + 1, :].to_broadcast((T, NB, HD)), ALU.mult).then_inc(ev["mask_sb"], 1)
                        tt(kcm[r], sel, kCt[0:T, h:h + 1, :].to_broadcast((T, NB, HD)), ALU.mult).then_inc(ev["mask_sb"], 1)
                        ch.after(tt(dps, e.ident[0:HD, 0:HD].rearrange("p (o k) -> p o k", o=1).to_broadcast((HD, NB, HD)),
                                    pc0[:, h, :].rearrange("p (q o) -> p q o", o=1).to_broadcast((HD, NB, HD)), ALU.mult))
                        ch.wait()
                        dve.wait_ge(ev["mz_mm"], h + 1)
                        ins = tt(mz[r], Q[1 + r][0:HD, :].rearrange("p (q k) -> p q k", k=HD), dps, ALU.add)
                        ins.then_inc(ev["mz_sb"], 1)
                        dve.wait_ge(ev["mz_sb"], h + 1)

                t0 = Tile(e, 0, True)
                t0.first = True
                k = body(t0, 0)
                with dve.Fori(1, TILES) as i:
                    t = Tile(e, i, True)
                    t.first = False
                    assert body(t, i * k) == k
                t = Tile(e, TILES, False)
                t.first = False
                body(t, TILES * k)

            @block.tensor
            def _(pe):
                def body(t):
                    i, fv, T = t.i, t.fv, t.T
                    issued = [0]

                    def fill(stage_name):
                        while issued[0] < BEFORE[stage_name]:
                            u, part = divmod(issued[0], PIECES)
                            r, (at, n) = (u // 3) % 2, CH[u % 3]
                            if part == 0:
                                if u % 3 == 0:
                                    pe.wait_ge(fw_lo, i * 4 + (u // 3 + 1))
                                pe.wait_ge(f_free, i * 12 + (u + 1))
                            for k in range(2 * part, 2 * part + 2):
                                mm = split_mm(pe, fps[u % 2][:, 0:n], whi[:, r, k], wlo[:, r, k], e.h_hi[:, k, at:at + n],
                                              e.h_lo[:, k, at:at + n], k == 0, k == KT - 1)
                            if part == PIECES - 1:
                                mm.then_inc(f_mm, 1)
                            issued[0] += 1

                    mm_ = pe.matmul

                    def settle(bank):
                        mm_(Q[bank][:, 511:512], e.ident, e.ident[:, 0:1], start=True, stop=True)

                    fill("lora")
                    pe.wait_ge(ev["tanh"], i + 1)
                    pe.wait_ge(ev["pm"], i + 1)
                    for b in range(4):
                        mm_(Q[0][:, b * T:(b + 1) * T], e.lora_w[0:64, b * P:(b + 1) * P], tw[:, 0:T], start=True, stop=True)
                        mm = mm_(Q[1][:, b * T:(b + 1) * T], e.lora_w[64:128, b * P:(b + 1) * P], pm[64:128, 12, 0:T], start=True, stop=True)
                    mm.then_inc(ev["lora_mm"], 1)
                    fill("ssq")
                    pe.wait_ge(ev["sq"], i + 1)
                    mm_(Q[2][:, 0:4 * T], e.ones_bd, sq[:, 0:4 * T], start=True, stop=True).then_inc(ev["ssq_mm"], 1)
                    fill("turn")
                    for q, (bank, src) in enumerate(((4, None), (3, alpha), (5, bC), (0, kC))):
                        if q == 2:
                            fill("A")
                        if src is not None:
                            pe.wait_ge(ev["feat"], i * 4 + (1, 3, 4)[q - 1])
                        for b in range(4):
                            s = pm[:, 8 + b, 0:T] if src is None else fv(src)[:, b]
                            mm = pe.transpose(Q[bank][0:T, b * P:(b + 1) * P], s, e.ident)
                        mm.then_inc(ev["turned"], 1)
                    for n, (l, r_) in enumerate(((beta, alpha), (kappa, alpha), (kappa, rho), (beta, rho))):
                        if n == 1:
                            pe.wait_ge(ev["turned_sb"], i * 4 + 4)
                            settle(3)
                        banks, z = PROD[n]
                        for b in range(4):
                            for par in (0, 1):
                                h0 = HD * par
                                for c in t.halves:
                                    mm = mm_(Q[banks[par]][C * c:C * c + C, (4 * z + b) * C:(4 * z + b + 1) * C], fv(l)[h0:h0 + HD, b, C * c:C * c + C],
                                             fv(r_)[h0:h0 + HD, b, C * c:C * c + C], start=True, stop=True)
                        mm.then_inc(ev["prod_mm"], 1)
                    fill("T")
                    pe.wait_ge(ev["t_init"], i * 2 + 2 if t.prompt else 2 * TILES + 1)
                    for q in range(2):
                        for h in range(4 * q, 4 * q + 4):
                            mm = pe.transpose(Q[XB[q]][0:T, (h % 4) * T:(h % 4 + 1) * T], t_t[0:T, h, 0:T], e.ident[0:T, 0:T])
                        mm.then_inc(ev["tm_mm"], 1)
                    for n in range(t.levels):
                        fill(f"X{n}")
                        last = n == t.levels - 1
                        if n == 0:
                            pe.wait_ge(ev["turned_sb"], i * 4 + 4)
                        for q in range(2):
                            heads = range(4 * q, 4 * q + 4)
                            if n:
                                pe.wait_ge(ev["tx_sb"], level_at(t, n - 1, q))
                            else:
                                pe.wait_ge(ev["tm_sb"], i * 2 + (q + 1))
                            for h in heads:
                                mm = mm_(Q[XB[q]][0:T, (h % 4) * T:(h % 4 + 1) * T], ab_t[0:T, h, 0:T], t_m[0:T, h, 0:T], start=True, stop=True)
                            mm.then_inc(ev["x_mm"], 1)
                            if n:
                                if n == 1:
                                    pe.wait_ge(ev["prod_sb"], i * 3 + 3)
                                else:
                                    pe.wait_ge(ev["tt_sb"], turn_at(t, n - 1, q))
                                for h in heads:
                                    mm = pe.transpose(Q[XTB[q]][0:T, (h % 4) * T:(h % 4 + 1) * T], t_m[0:T, h, 0:T], e.ident[0:T, 0:T])
                                mm.then_inc(ev["tt_mm"], 1)
                        fill(f"TX{n}")
                        if n == 0:
                            pe.wait_ge(ev["prod_sb"], i * 3 + 3)
                        for q in range(2):
                            pe.wait_ge(ev["x_sb"], level_at(t, n, q))
                            if n:
                                pe.wait_ge(ev["tt_sb"], turn_at(t, n, q))
                            for h in range(4 * q, 4 * q + 4):
                                o = Q[(XTB if last else TXB)[q]][0:T, (h % 4) * T:(h % 4 + 1) * T]
                                l, r_ = (x_m, t_t) if last else (t_t, x_m)
                                mm = mm_(o, l[0:T, h, 0:T], r_[0:T, h, 0:T], start=True, stop=True)
                            mm.then_inc(ev["tx_mm"], 1)
                    fill("Y")
                    for h in range(H):
                        mm = mm_(Q[1][0:T, h * HD:(h + 1) * HD], ak_t[0:T, h, 0:T], vt[0:T, h, :], start=True, stop=True)
                    mm.then_inc(ev["y_mm"], 1)
                    fill("GU")
                    pe.wait_ge(ev["tx_sb"], level_at(t, t.levels - 1, 1))
                    pe.wait_ge(ev["y_sb"], i + 1)
                    for q in range(2):
                        for h in range(4 * q, 4 * q + 4):
                            mm = mm_(Q[TXB[q]][0:T, (h % 4) * P:(h % 4 + 1) * P], t_t[0:T, h, 0:T], ay[0:T, h, :], start=True, stop=True)
                        mm.then_inc(ev["gu_mm"], 1)
                    fill("RM")
                    pe.wait_ge(ev["gu_sb"], i * 4 + 4)
                    for h in range(H):
                        if t.prompt:
                            o = Q[4][HD * (h % 2):HD * (h % 2) + HD, (h // 2) * P:(h // 2 + 1) * P]
                        else:
                            o = Q[4][0:HD, h * HD:(h + 1) * HD]
                        mm = mm_(o, n_g[0:T, h, :], rb_t[0:T, h, 0:T], start=True, stop=True)
                    mm.then_inc(ev["rm_mm"], 1)
                    if t.prompt:
                        for c in (0, 1):
                            for b in range(4):
                                mm = mm_(Q[1 + c][:, b * P:(b + 1) * P], n_g[C * c:C * c + C, 2 * b:2 * b + 2, :], bCt[C * c:C * c + C, 2 * b:2 * b + 2, :],
                                         start=True, stop=True)
                            mm.then_inc(ev["rm_mm"], 1)

                    def new_state(c, s_from, bank, done):
                        for b in range(4):
                            for h in (2 * b, 2 * b + 1):
                                o = Q[bank][HD * (h % 2):HD * (h % 2) + HD, b * HD:(b + 1) * HD]
                                rows = slice(C * c, C * c + C)
                                mm_(o, kCt[rows, h, :], vt[rows, h, :], start=True, stop=False, skip_group_check=True)
                                mm_(o, bCt[rows, h, :], n_u[rows, h, :], start=False, stop=False, skip_group_check=True)
                            mm = mm_(Q[bank][:, b * HD:(b + 1) * HD], m_c[:, c, b, :], s_from[:, b, :], start=False, stop=True, skip_group_check=True)
                        mm.then_inc(done, 1)

                    fill("S0")
                    if t.prompt:
                        pe.wait_ge(ev["m_sb"], i * 2 + 1)
                        if not t.first:
                            pe.wait_ge(ev["s1_sb"], i)
                        settle(3)
                        new_state(0, e.s_a, 3, ev["s0_mm"])
                        pe.wait_ge(ev["bonus"], i * 2 + 2)
                        pe.wait_ge(ev["rp_sb"], i + 1)
                        mm_(Q[4][:, 0:4 * T], e.ones_bd, bonus[:, 0:4 * T], start=True, stop=True)
                        fill("O")
                        pe.wait_ge(ev["s0_sb"], i + 1)
                        for b in range(4):
                            for c, s in ((0, s_ad), (1, s_bd)):
                                mm_(Q[0][C * c:C * c + C, b * P:(b + 1) * P], rp[:, b, C * c:C * c + C], s[:, b, :],
                                    start=True, stop=False, skip_group_check=True)
                            for h in (2 * b, 2 * b + 1):
                                o = Q[0][:, h * HD:(h + 1) * HD]
                                mm_(o, rk_t[:, h, :], vt[:, h, :], start=False, stop=False, skip_group_check=True)
                                mm = mm_(o, rb_t[:, h, :], n_u[:, h, :], start=False, stop=True, skip_group_check=True)
                        mm.then_inc(ev["o_mm"], 1)
                        pe.wait_ge(ev["m_sb"], i * 2 + 2)
                        settle(5)
                        new_state(1, s_b, 5, ev["s1_mm"])
                    else:
                        fill("O")
                        pe.wait_ge(ev["rpm"], NB)
                        pe.wait_ge(ev["bonus"], i * 2 + 2)
                        mm_(Q[4][:, 0:4 * T], e.ones_bd, bonus[:, 0:4 * T], start=True, stop=True)
                        for h in range(H):
                            r = h % 2
                            pe.wait_ge(s0_loaded[r], 16 * (h // 2 + 1))
                            o = Q[0][0:T, h * HD:(h + 1) * HD]
                            mm_(o, rk_t[0:T, h, 0:T], vt[0:T, h, :], start=True, stop=False)
                            mm_(o, rb_t[0:T, h, 0:T], n_u[0:T, h, :], start=False, stop=False)
                            for x in range(NB):
                                mm = mm_(o, rpm[x][:, h, :], s0t[:, r, x, :], start=False, stop=x == NB - 1)
                            if h == H - 1:
                                mm.then_inc(ev["o_mm"], 1)
                            pe.wait_ge(ev["mask_sb"], 2 * h + 2)
                            if h >= 2:
                                pe.wait_ge(ev["mz_sb"], h - 1)
                            mm_(Q[1 + r][0:HD, :], n_g[0:T, h, :], bcm[r], start=True, stop=True).then_inc(ev["mz_mm"], 1)
                            if h >= 2:
                                pe.wait_ge(ev["sn_sb"], h - 1)
                            o = Q[TXB[r]][0:HD, :]
                            mm_(o, vt[0:T, h, :], kcm[r], start=True, stop=False, skip_group_check=True)
                            mm_(o, n_u[0:T, h, :], bcm[r], start=False, stop=False, skip_group_check=True)
                            pe.wait_ge(ev["mz_sb"], h + 1)
                            for x in range(NB):
                                mm = mm_(o[:, x * HD:(x + 1) * HD], s0t[:, r, x, :], mz[r][:, x, :], start=False, stop=True, skip_group_check=True)
                            mm.then_inc(ev["sn_mm"], 1)
                    fill("ON")
                    pe.wait_ge(ev["on"], i + 1)
                    for b in range(4):
                        mm = pe.transpose(Q[1][:, b * T:(b + 1) * T], on[0:T, 2 * b:2 * b + 2, :].rearrange("p h k -> p (h k)"), e.ident[0:T, 0:T])
                    mm.then_inc(ev["on_mm"], 1)
                    fill("end")

                t0 = Tile(e, 0, True)
                t0.first = True
                body(t0)
                with pe.Fori(1, TILES) as i:
                    t = Tile(e, i, True)
                    t.first = False
                    body(t)
                t = Tile(e, TILES, False)
                t.first = False
                body(t)


def phase_pool(nc, io, e):
    EX = BUF + SEQ
    ES_ = BUF + NS
    with ExitStack() as ctx:
        sem = lambda n: ctx.enter_context(nc.semaphore(n))
        sb = lambda n, s, d=F32: ctx.enter_context(nc.sbuf_tensor(n, s, d))
        ux, usx = sb("pool_ext", [P, WB, EX])[:, :, :], sb("pool_ext_s", [P, WB, NB, ES_])[:, :, :, :]
        u5, cut = sb("s5_u_raw", [P, WB, NT]), sb("s5_u_cut", [P, WB, L5, J5])
        fresh = sb("pool_fresh", [P, WB, NB * NS])
        old = sb("pool_old", [NB * BUF, W])
        pw = sb("pool_weights", [P, WB, P])
        sums = [sb(f"pool_sum{i}", [P, WB, EX]) for i in range(2)]
        ssums = [sb(f"pool_ssum{i}", [P, WB, NB, ES_]) for i in range(2)]
        inv = sb("pool_inv", [P, WB, BUF])
        pooled = sb("pooled", [P, WB, NT])
        y_pl, z_pl = sb("y_pl", [P, WB, NT]), sb("z_pl", [P, WB, NT])
        z_loaded, z_silu = sem("pl_z_loaded"), sem("pl_z_silu")
        tail = sb("shift_tail", [P, RB, 1 + NB * NS])
        tail9 = sb("shift_cols", [P, RB, 1 + NB])
        shift_rows = sb("shift_rows_new", [1 + NB, RB * P])
        tail_p, tail_s = sb("pool_tail", [P, WB, BUF]), sb("pool_tail_s", [P, WB, NB * BUF])
        rows_p, rows_s = sb("pool_rows", [BUF, W]), sb("pool_rows_s", [NB * BUF, W])
        st_rows = sb("rwkv_rows", [HD, H, HD])
        ps = [ctx.enter_context(nc.psum_tensor(f"pool_ps{i}", [P, 512], F32)) for i in range(8)]
        loaded, cut_done, stored = sem("pl_loaded"), sem("s5_cut"), sem("pl_stored")
        u5_loaded = sem("s5_u_loaded")
        par_loaded, toep_zeroed = sem("s5_par_loaded"), sem("s5_toep_zeroed")
        flip, tails, done, mm_done, chain = [sem(n) for n in ("pl_flip", "pl_tails", "pooled_done", "pl_mm", "pl_chain")]
        flip2, rows_done, scaled = sem("pl_flip2"), sem("pl_rows"), sem("pl_scaled")
        scr = lambda b0, k, a, b: e.scratch[b0:b0 + k, :, a:b].rearrange("b p t -> p b t")
        with nc.Block() as block:
            @block.sync
            def _(sp):
                sp.dma_start(ux[:, :, BUF:EX], scr(B_PLX, WB, 1, 1 + SEQ)).then_inc(loaded, 16)
                sp.dma_start(fresh[:, :, :], scr(B_PLX, WB, 1 + SEQ, 1 + NT)).then_inc(loaded, 16)
                sp.dma_start(old[:, :], io["state_pool"][0].rearrange("b t w -> (b t) w")).then_inc(loaded, 16)
                sp.dma_start(pw[:, :, :], io["pool_w"][0].rearrange("g c d -> c g d")).then_inc(loaded, 16)
                sp.dma_start(tail[:, :, :], scr(B_RW, RB, SEQ, 1 + NT)).then_inc(loaded, 16)
                sp.dma_start(u5[:, :, :], scr(B_S5X, WB, 1, 1 + NT)).then_inc(u5_loaded, 16)
                sp.dma_start(z_pl[:, :, :], scr(B_PLZ, WB, 1, 1 + NT)).then_inc(z_loaded, 16)
                sp.dma_start(e.par_tile[:, :], e.par_scr).then_inc(par_loaded, 16)
                sp.wait_ge(cut_done, WB)
                sp.dma_start(e.u5_scr, cut[:, :, :, :]).then_inc(stored, 16)
                sp.wait_ge(rows_done, 7)
                sp.dma_start(e.outs["p_shift"][0], shift_rows[0:1, :]).then_inc(stored, 16)
                sp.dma_start(e.outs["s_shift"][0], shift_rows[1:1 + NB, :]).then_inc(stored, 16)
                sp.dma_start(e.outs["p_pool"][0, 0], rows_p[:, :]).then_inc(stored, 16)
                sp.dma_start(e.outs["s_pool"][0].rearrange("b t w -> (b t) w"), rows_s[:, :]).then_inc(stored, 16)
                sp.dma_start(e.outs["p_rwkv"][0, 0].rearrange("h v k -> v h k"), st_rows[:, :, :]).then_inc(stored, 16)
                sp.wait_ge(scaled, 3 * WB)
                sp.dma_start(e.y_scr[2], y_pl[:, :, :]).then_inc(stored, 16)
                sp.wait_ge(par_loaded, 16)
                sp.wait_ge(stored, 16 * 7)

            @block.gpsimd
            def _(pool):
                pool.memset(e.toep[:, :, :], 0.0).then_inc(toep_zeroed, 1)
                pool.wait_ge(u5_loaded, 16)
                for b in range(WB):
                    pool.tensor_copy(cut[:, b], u5[:, b, :].rearrange("p (j s) -> p s j", s=L5)).then_inc(cut_done, 1)
                pool.wait_ge(toep_zeroed, 1)

            @block.tensor
            def _(pe):
                pe.wait_ge(loaded, 16 * 5)
                for b in range(WB):
                    mm = pe.transpose(ps[0][:, b * NB * BUF:(b + 1) * NB * BUF], old[:, b * P:(b + 1) * P], e.ident[0:NB * BUF, 0:NB * BUF])
                mm.then_inc(flip, 1)
                for b in range(WB):
                    mm = pe.transpose(ps[1][0:HD, b * P:(b + 1) * P], e.s_a[:, b, :], e.ident)
                mm.then_inc(flip2, 1)
                pe.wait_ge(tails, 3)
                for r in range(RB):
                    mm = pe.transpose(ps[2 + r // 4][0:1 + NB, (r % 4) * P:(r % 4 + 1) * P], tail9[:, r, :], e.ident)
                mm.then_inc(flip2, 1)
                for b in range(WB):
                    mm = pe.transpose(ps[6][0:BUF, b * P:(b + 1) * P], tail_p[:, b, :], e.ident)
                for b in range(WB):
                    mm = pe.transpose(ps[7][0:NB * BUF, b * P:(b + 1) * P], tail_s[:, b, :], e.ident)
                mm.then_inc(flip2, 1)
                for g in range(WB):
                    pe.wait_ge(done, g + 1)
                    for c, (at, n) in enumerate(CH):
                        q = g * 3 + c
                        if q == 0:
                            pe.wait_ge(rows_done, 7)
                        if q >= 8:
                            pe.wait_ge(scaled, q - 7)
                        pe.matmul(ps[q % 8][:, 0:n], pw[:, g, :], pooled[:, g, at:at + n], start=True, stop=True).then_inc(mm_done, 1)

            @block.scalar
            def _(act):
                act.wait_ge(flip2, 1)
                act.activation(st_rows[:, :, :], ps[1][0:HD, :].rearrange("v (h k) -> v h k", k=HD), ACT.Copy).then_inc(rows_done, 1)
                act.wait_ge(flip2, 3)
                for q in range(4):
                    n = min(4, RB - 4 * q) * P
                    act.activation(shift_rows[:, q * 512:q * 512 + n], ps[2 + q][0:1 + NB, 0:n], ACT.Copy).then_inc(rows_done, 1)
                act.activation(rows_p[:, :], ps[6][0:BUF, :], ACT.Copy).then_inc(rows_done, 1)
                act.activation(rows_s[:, :], ps[7][0:NB * BUF, :], ACT.Copy).then_inc(rows_done, 1)
                act.wait_ge(z_loaded, 16)
                for g in range(WB):
                    act.activation(z_pl[:, g, :], z_pl[:, g, :], ACT.Silu).then_inc(z_silu, 1)

            @block.vector
            def _(dve):
                ch = Chain(dve, chain)
                tt = dve.tensor_tensor
                ch.after(dve.memset(ux[:, :, 0:BUF], 0.0))
                for g, w in enumerate(WIN):
                    ch.after(dve.memset(inv[:, g, :], 1.0 / w))
                ch.wait()
                for pos in range(BUF):
                    g0 = [g for g, w in enumerate(WIN) if w > pos + 1][0]
                    ch.after(dve.memset(inv[:, g0:WB, pos:pos + 1], 1.0 / (pos + 1)))
                dve.wait_ge(loaded, 16 * 5)
                dve.tensor_copy(tail9[:, :, :], tail[:, :, 0:1 + NB * NS:NS]).then_inc(tails, 1)
                dve.tensor_copy(tail_p[:, :, :], ux[:, :, SEQ:EX]).then_inc(tails, 1)
                dve.wait_ge(flip, 1)
                ch.after(dve.tensor_copy(usx[:, :, :, 0:BUF], ps[0][:, 0:WB * NB * BUF].rearrange("p (w b t) -> p w b t", w=WB, b=NB)))
                ch.after(dve.tensor_copy(usx[:, :, :, BUF:ES_], fresh[:, :, :].rearrange("p w (b t) -> p w b t", b=NB)))
                ch.wait()
                dve.tensor_copy(tail_s[:, :, :].rearrange("p w (b t) -> p w b t", b=NB), usx[:, :, :, NS:ES_]).then_inc(tails, 1)

                def scale(g):
                    at_s = VAT["pool_scale"][0] + g
                    dve.wait_ge(z_silu, g + 1)
                    for c, (at, n) in enumerate(CH):
                        dve.wait_ge(mm_done, 3 * g + c + 1)
                        dve.scalar_tensor_tensor(out=y_pl[:, g, at:at + n], in0=ps[(3 * g + c) % 8][:, 0:n], scalar=e.vec[:, at_s:at_s + 1],
                                                 in1=z_pl[:, g, at:at + n], op0=ALU.mult, op1=ALU.mult).then_inc(scaled, 1)

                src, ssrc = ux, usx
                for g, w in enumerate(WIN):
                    d, lo = w // 2, w - 1
                    dst, sdst = sums[g % 2], ssums[g % 2]
                    ch.after(tt(dst[:, g:WB, lo:EX], src[:, g:WB, lo:EX], src[:, g:WB, lo - d:EX - d], ALU.add))
                    ch.after(tt(sdst[:, g:WB, :, lo:ES_], ssrc[:, g:WB, :, lo:ES_], ssrc[:, g:WB, :, lo - d:ES_ - d], ALU.add))
                    ch.wait()
                    ch.after(tt(pooled[:, g, 0:BUF], dst[:, g, BUF:2 * BUF], inv[:, g, :], ALU.mult))
                    ch.wait()
                    ch.after(tt(pooled[:, g, 0:BUF], pooled[:, g, 0:BUF], ux[:, g, BUF:2 * BUF], ALU.subtract))
                    ch.after(dve.scalar_tensor_tensor(out=pooled[:, g, BUF:SEQ], in0=dst[:, g, 2 * BUF:EX], scalar=1.0 / w,
                                                      in1=ux[:, g, 2 * BUF:EX], op0=ALU.mult, op1=ALU.subtract))
                    ch.after(dve.scalar_tensor_tensor(out=pooled[:, g, SEQ:NT].rearrange("p (b t) -> p b t", b=NB), in0=sdst[:, g, :, BUF:ES_],
                                                      scalar=1.0 / w, in1=usx[:, g, :, BUF:ES_], op0=ALU.mult, op1=ALU.subtract))
                    ch.wait()
                    dve.sem_inc(done, 1)
                    if g:
                        scale(g - 1)
                    src, ssrc = dst, sdst
                scale(WB - 1)


class S5Params:

    PARTS = (("pw", 2 * (L5 + 1) * G), ("wv", 2 * 10 * G), ("bt", 2 * G * GC), ("cst", 2 * G * GC), ("h0", 2 * NB * G), ("mag8", G))
    SIZE = sum(n for _, n in PARTS)

    def __init__(self, tile):
        at = 0
        for name, n in self.PARTS:
            v = tile[:, at:at + n]
            at += n
            if name == "pw":
                self.pw = v.rearrange("p (z s g) -> p z s g", z=2, g=G)
            elif name == "wv":
                self.wv = v.rearrange("p (z s g) -> p z s g", z=2, g=G)
            elif name == "bt":
                self.bt = v.rearrange("p (z g c) -> p z g c", z=2, c=GC)
            elif name == "cst":
                self.cst = v.rearrange("p (z g c) -> p z g c", z=2, c=GC)
            elif name == "h0":
                self.h0 = v.rearrange("p (z b g) -> p z b g", z=2, g=G)
            else:
                self.mag8 = v


class MakeParams:

    LOADS = 17

    def __init__(self, nc, io, ctx, ps, c_ps):
        sem = lambda n: ctx.enter_context(nc.semaphore(n))
        sb = lambda n, s, d=F32: ctx.enter_context(nc.sbuf_tensor(n, s, d))
        self.io, self.ps, self.c_ps = io, ps, c_ps
        self.tile = sb("par_tile", [P, S5Params.SIZE])
        self.v = S5Params(self.tile)
        self.lam = sb("lam_rows", [G, 2, P])
        self.lam_t = sb("lam_t", [P, 2, G])
        self.braw = sb("b_raw", [P, 2, G, GC])
        self.crow = sb("c_rows", [P, 2, 4, P])
        self.h0rows = sb("h0_rows", [P, 2, 2, P])
        self.tmp = sb("par_tmp", [P, 2 * G * GC])
        self.small = {n: sb("par_" + n, [P, G])[:, :] for n in (
            "dt", "ldt", "mag", "m2", "th", "k", "r", "sh", "si", "co", "ar", "ai", "den", "u1", "u2", "u3", "cor", "coi")}
        self.kint = sb("par_kint", [P, G], mybir.dt.int32)[:, :]
        self.loaded, self.flipped, self.taken, self.angle, self.sines, self.chain, self.made = [sem("par_" + n) for n in (
            "loaded", "flipped", "taken", "angle", "sines", "chain", "made")]

    def sync(self, sp):
        io = self.io

        def ld(dst, src):
            sp.dma_start(dst, src).then_inc(self.loaded, 16)
        for half in range(2):
            hs = slice(HD * half, HD * half + HD)
            ld(self.lam[:, 0, hs], io["s5_lam_re"][0])
            ld(self.lam[:, 1, hs], io["s5_lam_im"][0])
            for k in range(2):
                re = half == k
                ld(self.braw[hs, k], io["s5_b_re" if re else "s5_b_im"][0].rearrange("g n c -> n g c"))
                ld(self.crow[:, k, :, hs], io["s5_c_re" if re else "s5_c_im"][0].rearrange("g c n -> (g c) n").rearrange("(q p) n -> p q n", p=P))
                ld(self.h0rows[:, k, :, hs], io["state_s5_re" if re else "state_s5_im"][0].rearrange("b g n -> (b g) n").rearrange("(q p) n -> p q n", p=P))
        ld(self.small["ldt"], io["s5_log_dt"].to_broadcast((P, G)))

    def tensor(self, pe, e):
        pe.wait_ge(self.loaded, 16 * self.LOADS)
        for q in range(2):
            pe.transpose(self.ps[0][:, q * G:(q + 1) * G], self.lam[:, q, :], e.ident[0:G, 0:G])
        for k in range(2):
            for q in range(4):
                pe.transpose(self.c_ps[k][:, q * P:(q + 1) * P], self.crow[:, k, q, :], e.ident)
        for k in range(2):
            for q in range(2):
                mm = pe.transpose(self.ps[1][:, (2 * k + q) * P:(2 * k + q + 1) * P], self.h0rows[:, k, q, :], e.ident)
        mm.then_inc(self.flipped, 1)

    def scalar(self, act):
        act.wait_ge(self.angle, 1)
        act.activation(self.small["si"], self.small["r"], ACT.Sin).then_inc(self.sines, 1)
        act.activation(self.small["sh"], self.small["r"], ACT.Sin, scale=0.5).then_inc(self.sines, 1)

    def vector_take(self, dve):
        v = self.v
        dve.wait_ge(self.flipped, 1)
        dve.tensor_copy(self.lam_t[:, :, :].rearrange("p q g -> p (q g)"), self.ps[0][:, 0:2 * G]).then_inc(self.taken, 1)
        for z in range(2):
            dve.tensor_copy(v.cst[:, z].rearrange("p g c -> p (g c)"), self.c_ps[z][:, :]).then_inc(self.taken, 1)
        dve.tensor_copy(v.h0, self.ps[1][:, :].rearrange("p (k b g) -> p k b g", k=2, g=G)).then_inc(self.taken, 1)

    def vector(self, dve):
        ch = Chain(dve, self.chain)
        tt, ts = dve.tensor_tensor, dve.tensor_scalar
        dt, ldt, mag, m2, th, kf, r1, sh, si, co, ar, ai, den, u1, u2, u3, cor, coi = self.small.values()
        v, kint, tmp, L = self.v, self.kint, self.tmp, L5
        pw, wv, bt, cst, braw = v.pw, v.wv, v.bt, v.cst, self.braw
        lr, li = self.lam_t[:, 0, :], self.lam_t[:, 1, :]

        def op(ins):
            ch.after(ins)
            ch.wait()

        dve.wait_ge(self.taken, 4)
        op(ts(cst[HD:P, 0], cst[HD:P, 0], -1.0, None, ALU.mult))
        op(ts(v.h0[0:HD, 1], v.h0[0:HD, 1], -1.0, None, ALU.mult))

        def exp(dst, x):
            op(ts(kf, x, 1.0 / LN2, -126.0, ALU.mult, ALU.max))
            op(ts(kf, kf, 127.0, MAGIC, ALU.min, ALU.add))
            op(ts(kf, kf, -MAGIC, None, ALU.add))
            op(dve.scalar_tensor_tensor(out=u2, in0=kf, scalar=-LN2_PARTS[0], in1=x, op0=ALU.mult, op1=ALU.add))
            op(dve.scalar_tensor_tensor(out=u2, in0=kf, scalar=-LN2_PARTS[1], in1=u2, op0=ALU.mult, op1=ALU.add))
            op(ts(u2, u2, -0.35, 0.35, ALU.max, ALU.min))
            op(ts(dst, u2, 1.0 / EXP_FACT[-1], None, ALU.mult))
            for f in EXP_FACT[-2::-1]:
                op(dve.scalar_tensor_tensor(out=dst, in0=dst, scalar=1.0 / f, in1=u2, op0=ALU.add, op1=ALU.mult))
            op(ts(kf, kf, 127.0, 2.0 ** 23, ALU.add, ALU.mult))
            op(dve.tensor_copy(kint, kf))
            op(dve.scalar_tensor_tensor(out=dst, in0=dst, scalar=1.0, in1=kint.bitcast(F32), op0=ALU.add, op1=ALU.mult))

        exp(dt, ldt)
        op(tt(u1, lr, dt, ALU.mult))
        exp(mag, u1)
        op(tt(th, li, dt, ALU.mult))
        op(ts(kf, th, 1.0 / (2 * np.pi), MAGIC, ALU.mult, ALU.add))
        op(ts(kf, kf, -MAGIC, None, ALU.add))
        op(dve.scalar_tensor_tensor(out=r1, in0=kf, scalar=-TURN[0], in1=th, op0=ALU.mult, op1=ALU.add))
        op(dve.scalar_tensor_tensor(out=r1, in0=kf, scalar=-TURN[1], in1=r1, op0=ALU.mult, op1=ALU.add))
        op(dve.scalar_tensor_tensor(out=r1, in0=kf, scalar=-TURN[2], in1=r1, op0=ALU.mult, op1=ALU.add))
        op(ts(r1, r1, -PI_IN, PI_IN, ALU.max, ALU.min))
        dve.sem_inc(self.angle, 1)
        dve.wait_ge(self.sines, 2)
        op(tt(co, sh, sh, ALU.mult))
        op(ts(co, co, -2.0, 1.0, ALU.mult, ALU.add))
        op(tt(ar, mag, co, ALU.mult))
        op(tt(ai, mag, si, ALU.mult))
        ch.after(dve.tensor_copy(wv[:, 0, 0, :], co))
        op(dve.tensor_copy(wv[:, 1, 0, :], si))
        for q in range(9):
            a, b = wv[:, 0, q, :], wv[:, 1, q, :]
            ch.after(tt(u1, a, a, ALU.mult))
            ch.after(tt(u2, b, b, ALU.mult))
            ch.after(tt(u3, a, b, ALU.mult))
            ch.wait()
            ch.after(tt(wv[:, 0, q + 1, :], u1, u2, ALU.subtract))
            op(ts(wv[:, 1, q + 1, :], u3, 2.0, None, ALU.mult))
            if q >= 2:
                a, b = wv[:, 0, q + 1, :], wv[:, 1, q + 1, :]
                ch.after(tt(u1, a, a, ALU.mult))
                op(tt(u2, b, b, ALU.mult))
                op(tt(u3, u1, u2, ALU.add))
                op(ts(u3, u3, -0.5, 1.5, ALU.mult, ALU.add))
                ch.after(tt(a, a, u3, ALU.mult))
                op(tt(b, b, u3, ALU.mult))
        op(tt(m2, mag, mag, ALU.mult))
        op(tt(m2, m2, m2, ALU.mult))
        op(tt(v.mag8, m2, m2, ALU.mult))
        ch.after(dve.memset(pw[:, 0, 0, :], 1.0))
        ch.after(dve.memset(pw[:, 1, 0, :], 0.0))
        ch.after(dve.tensor_copy(pw[:, 0, 1, :], ar))
        op(dve.tensor_copy(pw[:, 1, 1, :], ai))
        t3 = lambda k, m: tmp[:, k * 256:k * 256 + m * G].rearrange("p (s g) -> p s g", s=m)
        m = 1
        while m < L:
            w = [pw[:, z, m:m + 1, :].to_broadcast((P, m, G)) for z in range(2)]
            x, y = pw[:, 0, 1:m + 1, :], pw[:, 1, 1:m + 1, :]
            for z, (a, b, o) in enumerate(((0, 1, ALU.subtract), (1, 0, ALU.add))):
                ch.after(tt(t3(0, m), x, w[a], ALU.mult))
                op(tt(t3(1, m), y, w[b], ALU.mult))
                op(tt(pw[:, z, m + 1:2 * m + 1, :], t3(0, m), t3(1, m), o))
            m *= 2
        ch.after(tt(u1, lr, lr, ALU.mult))
        op(tt(u2, li, li, ALU.mult))
        op(tt(den, u1, u2, ALU.add))
        ch.after(dve.reciprocal(den, den))
        op(ts(ar, ar, -1.0, None, ALU.add))
        for dst, (x, y, o) in ((cor, (lr, li, ALU.add)), (coi, (li, lr, ALU.subtract))):
            a_, b_ = (ar, ai)
            ch.after(tt(u1, a_ if o == ALU.add else b_, lr, ALU.mult))
            op(tt(u2, b_ if o == ALU.add else a_, li, ALU.mult))
            op(tt(u3, u1, u2, o))
            op(tt(dst, u3, den, ALU.mult))
        op(ts(braw[0:HD, 1], braw[0:HD, 1], -1.0, None, ALU.mult))
        gb = lambda x: x.rearrange("p (g o) -> p g o", o=1).to_broadcast((P, G, GC))
        ta, tb = (tmp[:, k * 512:(k + 1) * 512].rearrange("p (g c) -> p g c", g=G) for k in range(2))
        for z, o in enumerate((ALU.add, ALU.subtract)):
            ch.after(tt(ta, braw[:, z], gb(cor), ALU.mult))
            op(tt(tb, braw[:, 1 - z], gb(coi), ALU.mult))
            op(tt(bt[:, z], ta, tb, o))
        dve.sem_inc(self.made, 1)


def phase_s5_tables(nc, io, e):
    L = L5
    with ExitStack() as ctx:
        sem = lambda n: ctx.enter_context(nc.semaphore(n))
        sb = lambda n, s, d=F32: ctx.enter_context(nc.sbuf_tensor(n, s, d))
        v = e.par
        ebuf, tmp = sb("e_buf", [P, G, L, GC]), sb("t5_tmp", [P, 3 * G * GC])
        kt = sb("k_t", [GC, G, P])
        half = [sb(f"rot_tmp{z}", [P, G, JP // 2]) for z in range(2)]
        ps = [ctx.enter_context(nc.psum_tensor(f"t5_ps{i}", [P, 512], F32)) for i in range(8)]
        chain, etab, eflip, es_sb, dtab, kmm, k_sb, toep = [sem("t5s_" + n) for n in (
            "chain", "etab", "eflip", "es_sb", "dtab", "kmm", "k_sb", "toep")]
        ptab, es2_sb, rot_half = [sem("t5s_" + n) for n in ("ptab", "es2", "rot_half")]
        skip = sb("s5_skip", [GC, G])
        skip_diag = tmp[0:GC, 0:G * GC].rearrange("p (g c) -> p g c", g=G)
        skip_loaded, skip_in = sem("t5s_skip_loaded"), sem("t5s_skip_in")
        gb = lambda x, m=GC: x.rearrange("p (g o) -> p g o", o=1).to_broadcast((P, G, m))
        with nc.Block() as block:
            @block.sync
            def _(sp):
                for s in range(L):
                    sp.dma_start(e.u5[GC * s:GC * s + GC].rearrange("c (b q) j -> c b q j", b=WB),
                                 e.u5_scr.rearrange("(q c) b s j -> s c b q j", c=GC)[s]).then_inc(e.u5_sem, 16)
                sp.dma_start(skip[:, :], io["s5_d"][0].rearrange("(g c) -> c g", c=GC), allow_slow_non_contiguous=True).then_inc(skip_loaded, 16)
                sp.wait_ge(skip_in, 2)
                for s in range(L):
                    sp.dma_start(e.toep[GC * s:GC * s + GC, :, GC * s:P], kt[:, :, 0:P - GC * s]).then_inc(toep, 16)
                sp.wait_ge(toep, 16 * L)
                sp.wait_ge(e.u5_sem, 16 * L)

            @block.scalar
            def _(act):
                for q in range(8):
                    act.wait_ge(kmm, q + 1)
                    act.activation(kt[:, 4 * q:4 * q + 4, :], ps[4 + q % 4][0:GC, :].rearrange("p (g n) -> p g n", g=4), ACT.Copy).then_inc(k_sb, 1)
                for q in range(8):
                    act.wait_ge(eflip, q + 1)
                    act.activation(e.es[:, 0, 4 * q:4 * q + 4, :], ps[q % 4][:, :].rearrange("p (g n) -> p g n", g=4), ACT.Copy).then_inc(es_sb, 1)
                    act.wait_ge(es_sb, q + 1)
                    act.activation(e.es[:, 1, 4 * q:4 * q + 4, 0:HD], e.es[:, 0, 4 * q:4 * q + 4, HD:P], ACT.Copy, scale=-1.0).then_inc(es2_sb, 1)
                    act.activation(e.es[:, 1, 4 * q:4 * q + 4, HD:P], e.es[:, 0, 4 * q:4 * q + 4, 0:HD], ACT.Copy).then_inc(es2_sb, 1)

            @block.tensor
            def _(pe):
                pe.wait_ge(dtab, 1)
                for q in range(8):
                    if q >= 4:
                        pe.wait_ge(k_sb, q - 3)
                    for g in range(4):
                        mm = pe.matmul(ps[4 + q % 4][0:GC, g * P:(g + 1) * P], v.bt[:, 0, 4 * q + g, :],
                                       e.dtab[:, 4 * q + g, 0:L, :].rearrange("p t c -> p (t c)"), start=True, stop=True)
                    mm.then_inc(kmm, 1)
                pe.wait_ge(etab, 1)
                for q in range(8):
                    if q >= 4:
                        pe.wait_ge(es_sb, q - 3)
                    for g in range(4):
                        mm = pe.transpose(ps[q % 4][:, g * P:(g + 1) * P], ebuf[:, 4 * q + g, :, :].rearrange("p s c -> p (s c)"), e.ident)
                    mm.then_inc(eflip, 1)

            def double(eng, ch, z, q, ta, tb):
                m = 1 << q
                a, b, op = ((0, 1, ALU.subtract), (1, 0, ALU.add))[z]
                ch.wait()
                ch.after(eng.tensor_tensor(ta[:, :, 0:m], e.rot[:, 0, :, 0:m], gb(v.wv[:, a, 3 + q, :], m), ALU.mult))
                ch.after(eng.tensor_tensor(tb[:, :, 0:m], e.rot[:, 1, :, 0:m], gb(v.wv[:, b, 3 + q, :], m), ALU.mult))
                ch.wait()
                ch.after(eng.tensor_tensor(e.rot[:, z, :, m:2 * m], ta[:, :, 0:m], tb[:, :, 0:m], op))

            @block.gpsimd
            def _(pool):
                ch = Chain(pool, ptab)
                ch.after(pool.memset(e.rot[:, 0, :, 0:1], 1.0))
                ch.after(pool.memset(e.rot[:, 1, :, 0:1], 0.0))
                for q in range(6):
                    for z in range(2):
                        double(pool, ch, z, q, e.hprev[:, :, 0:HD], e.hprev[:, :, HD:P])
                ch.wait()
                pool.sem_inc(rot_half, 1)
                double(pool, ch, 1, 6, e.hprev[:, :, 0:HD], e.hprev[:, :, HD:P])
                ch.wait()

            @block.vector
            def _(dve):
                ch = Chain(dve, chain)
                tt = dve.tensor_tensor

                def table(dst, x, power, count, o):
                    tq = tmp[:, :].rearrange("p (s g c) -> p s g c", s=3, g=G)
                    for s0 in range(0, count, 3):
                        some = range(s0, min(s0 + 3, count))
                        for s in some:
                            pb = [gb(v.pw[:, z, power(s), :]) for z in range(2)]
                            ch.after(tt(dst[:, :, s, :], x[:, 0], pb[0], ALU.mult))
                            ch.after(tt(tq[:, s - s0], x[:, 1], pb[1], ALU.mult))
                        ch.wait()
                        for s in some:
                            ch.after(tt(dst[:, :, s, :], dst[:, :, s, :], tq[:, s - s0], o))
                        ch.wait()

                table(e.dtab, v.cst, lambda s: s, L + 1, ALU.subtract)
                dve.sem_inc(dtab, 1)
                table(ebuf, v.bt, lambda s: L - 1 - s, L, ALU.add)
                dve.sem_inc(etab, 1)
                dve.wait_ge(skip_loaded, 16)
                tt(skip_diag[:, :, :], e.ident[0:GC, 0:GC].rearrange("p (o c) -> p o c", o=1).to_broadcast((GC, G, GC)),
                   skip[:, :].rearrange("p (g o) -> p g o", o=1).to_broadcast((GC, G, GC)), ALU.mult).then_inc(skip_in, 1)
                dve.wait_ge(k_sb, 8)
                dve.wait_ge(skip_in, 1)
                tt(kt[:, :, 0:GC], kt[:, :, 0:GC], skip_diag, ALU.add).then_inc(skip_in, 1)
                dve.wait_ge(rot_half, 1)
                double(dve, ch, 0, 6, half[0], half[1])
                ch.wait()


def phase_s5(nc, io, e):
    NG = 3
    batches = [list(range(a, min(a + NG, G))) for a in range(0, G, NG)]
    with ExitStack() as ctx:
        sem = lambda n: ctx.enter_context(nc.semaphore(n))
        sb = lambda n, s, d=F32: ctx.enter_context(nc.sbuf_tensor(n, s, d))
        gsc = sb("s5_scan", [P, G, JP])
        xs = sb("s5_x_sample", [P, G, NB])
        t_a, t_b = sb("s5_ta", [P, 3, NG, JP]), sb("s5_tb", [P, 2, NG, JP])
        back = sem("s5_back")
        fin, snew = sb("s5_fin", [P, G]), sb("s5_snew", [P, NB, G])
        fa, fb = sb("s5_fa", [P, NB, G]), sb("s5_fb", [P, NB, G])
        perm = sb("s5_perm", [P, P])
        fin_rows, s_rows = sb("s5_fin_rows", [G, P]), sb("s5_s_rows", [P, 2, P])
        ycut = sb("s5_ycut", [P, G, J5])
        ps = [ctx.enter_context(nc.psum_tensor(f"s5_ps{i}", [P, 512], F32)) for i in range(8)]
        x_mm, x_used, scan, i_mm, hdone, y_mm, y_sb, chain, permd, y_st, fins, finflip, fin_sb, out_st = [sem("s5_" + n) for n in (
            "x_mm", "x_used", "scan", "i_mm", "hdone", "y_mm", "y_sb", "chain", "permd", "y_st", "fins", "finflip", "fin_sb", "out_st")]
        hz = sem("s5_hz")
        with nc.Block() as block:
            @block.gpsimd
            def _(pool):
                ch = Chain(pool, permd)
                ch.after(pool.memset(perm[:, :], 0.0))
                ch.wait()
                ch.after(pool.affine_select(out=perm[:, :], in_=perm[:, :], compare_op=ALU.not_equal, fill=1.0, base=HD,
                                            pattern=[[-1, P]], channel_multiplier=1))
                ch.wait()
                ch.after(pool.affine_select(out=perm[:, :], in_=perm[:, :], compare_op=ALU.not_equal, fill=-1.0, base=-HD,
                                            pattern=[[-1, P]], channel_multiplier=1))
                ch.wait()
                for n, gs in enumerate(batches):
                    gr, k = slice(gs[0], gs[-1] + 1), len(gs)
                    pool.wait_ge(scan, gs[-1] + 1)
                    if n >= 2:
                        pool.wait_ge(hdone, n - 1)
                    pool.tensor_tensor(t_a[:, 1 + n % 2, 0:k, :], gsc[:, gr, :], e.rot[:, 0, gr, :], ALU.mult).then_inc(back, 1)

            @block.tensor
            def _(pe):
                def turn(n):
                    gs = batches[n]
                    if n == 0:
                        pe.wait_ge(permd, 3)
                    pe.wait_ge(scan, gs[-1] + 1)
                    if n >= 2:
                        pe.wait_ge(hdone, n - 1)
                    pe.matmul(ps[4 + n % 2][:, 0:len(gs) * JP], perm[:, :], gsc[:, gs[0]:gs[-1] + 1, :].rearrange("p g j -> p (g j)"),
                              start=True, stop=True).then_inc(i_mm, 1)

                def outputs(n):
                    if n >= 2:
                        pe.wait_ge(y_sb, n - 1)
                    if n == 0:
                        pe.wait_ge(hz, 2)
                    for q, g in enumerate(batches[n]):
                        o = ps[6 + n % 2][:, q * J5:(q + 1) * J5]
                        pe.matmul(o, e.toep[:, g, :], e.u5[:, g, :], start=True, stop=False)
                        if q == 0:
                            pe.wait_ge(hdone, n + 1)
                        mm = pe.matmul(o, e.dtab[:, g, 1:L5 + 1, :].rearrange("p t c -> p (t c)"), e.hprev[:, g, :], start=False, stop=True)
                    mm.then_inc(y_mm, 1)

                for n, gs in enumerate(batches):
                    if n >= 2:
                        pe.wait_ge(x_used, n - 1)
                    for z in range(2):
                        for q, g in enumerate(gs):
                            mm = pe.matmul(ps[2 * (n % 2) + z][:, q * J5:(q + 1) * J5], e.es[:, z, g, :], e.u5[:, g, :], start=True, stop=True)
                    mm.then_inc(x_mm, 1)
                    if n >= 1:
                        turn(n - 1)
                    if n >= 2:
                        outputs(n - 2)
                turn(len(batches) - 1)
                outputs(len(batches) - 2)
                outputs(len(batches) - 1)
                pe.wait_ge(fins, 2)
                pe.transpose(ps[0][0:G, 0:P], fin[:, :], e.ident).then_inc(finflip, 1)
                for q in range(2):
                    mm = pe.transpose(ps[1][:, q * P:(q + 1) * P], snew[:, 4 * q:4 * q + 4, :].rearrange("p b g -> p (b g)"), e.ident)
                mm.then_inc(finflip, 1)

            @block.vector
            def _(dve):
                ch = Chain(dve, chain)
                tt = dve.tensor_tensor
                dve.memset(e.hprev[:, :, 0:1], 0.0).then_inc(hz, 1)
                dve.tensor_copy(e.hprev[:, :, JP:J5].rearrange("p g b -> p b g"), e.par.h0[:, 0]).then_inc(hz, 1)

                def rotate_back(n):
                    gs = batches[n]
                    gr, k = slice(gs[0], gs[-1] + 1), len(gs)
                    dve.wait_ge(i_mm, n + 1)
                    ig = ps[4 + n % 2][:, 0:k * JP].rearrange("p (g j) -> p g j", g=k)
                    ta = t_a[:, 1 + n % 2]
                    ch.after(tt(t_b[:, 1, 0:k, :], ig, e.rot[:, 1, gr, :], ALU.mult))
                    ch.wait()
                    dve.wait_ge(back, n + 1)
                    ch.after(tt(fin[:, gr], ta[:, 0:k, JP - 1], t_b[:, 1, 0:k, JP - 1], ALU.add))
                    ch.after(tt(e.hprev[:, gr, 1:JP], ta[:, 0:k, 0:JP - 1], t_b[:, 1, 0:k, 0:JP - 1], ALU.add))
                    ch.wait()
                    dve.sem_inc(hdone, 1)

                for n, gs in enumerate(batches):
                    gr, k = slice(gs[0], gs[-1] + 1), len(gs)
                    dve.wait_ge(x_mm, n + 1)
                    x, ix = (ps[2 * (n % 2) + z][:, 0:k * J5].rearrange("p (g j) -> p g j", g=k) for z in range(2))
                    ch.after(tt(t_a[:, 0, 0:k, :], x[:, :, 0:JP], e.rot[:, 0, gr, :], ALU.mult))
                    ch.after(tt(t_b[:, 0, 0:k, :], ix[:, :, 0:JP], e.rot[:, 1, gr, :], ALU.mult))
                    ch.after(dve.tensor_copy(xs[:, gr, :], x[:, :, JP:J5]))
                    ch.wait()
                    dve.sem_inc(x_used, 1)
                    ch.after(tt(t_a[:, 0, 0:k, :], t_a[:, 0, 0:k, :], t_b[:, 0, 0:k, :], ALU.subtract))
                    ch.wait()
                    for q, g in enumerate(gs):
                        dve.tensor_tensor_scan(gsc[:, g, :], e.par.mag8[:, g:g + 1].to_broadcast((P, JP)), t_a[:, 0, q, :], 0.0,
                                               ALU.mult, ALU.add).then_inc(scan, 1)
                    dve.wait_ge(scan, gs[-1] + 1)
                    if n >= 1:
                        rotate_back(n - 1)
                rotate_back(len(batches) - 1)
                ab = [e.par.pw[:, z, L5:L5 + 1, :].to_broadcast((P, NB, G)) for z in range(2)]
                ch.after(tt(fa[:, :, :], e.par.h0[:, 0], ab[0], ALU.mult))
                ch.after(tt(fb[:, :, :], e.par.h0[:, 1], ab[1], ALU.mult))
                ch.wait()
                ch.after(tt(fa[:, :, :], fa[:, :, :], fb[:, :, :], ALU.add))
                ch.wait()
                ch.after(tt(snew[:, :, :], fa[:, :, :], xs[:, :, :].rearrange("p g b -> p b g"), ALU.add))
                ch.wait()
                dve.sem_inc(fins, 2)

            @block.scalar
            def _(act):
                for n, gs in enumerate(batches):
                    k = len(gs)
                    act.wait_ge(y_mm, n + 1)
                    act.activation(ycut[:, gs[0]:gs[-1] + 1, :], ps[6 + n % 2][:, 0:k * J5].rearrange("p (g j) -> p g j", g=k), ACT.Copy).then_inc(y_sb, 1)
                act.wait_ge(finflip, 2)
                act.activation(fin_rows[:, :], ps[0][0:G, 0:P], ACT.Copy).then_inc(fin_sb, 1)
                act.activation(s_rows[:, :, :], ps[1][:, 0:2 * P].rearrange("p (q n) -> p q n", q=2), ACT.Copy).then_inc(fin_sb, 1)

            @block.sync
            def _(sp):
                for n, gs in enumerate(batches):
                    gr = slice(gs[0], gs[-1] + 1)
                    sp.wait_ge(y_sb, n + 1)
                    sp.dma_start(e.y5_scr[:, gr], ycut[:, gr, :]).then_inc(y_st, 16)
                sp.wait_ge(fin_sb, 2)
                for z, n in enumerate(("re", "im")):
                    zs = slice(HD * z, HD * z + HD)
                    sp.dma_start(e.outs["p_s5_" + n][0, 0], fin_rows[:, zs]).then_inc(out_st, 16)
                    sp.dma_start(e.outs["s_s5_" + n][0].rearrange("b g n -> (b g) n").rearrange("(q p) n -> p q n", p=P), s_rows[:, :, zs]).then_inc(out_st, 16)
                sp.wait_ge(y_st, 16 * len(batches))
                sp.wait_ge(out_st, 64)


UP_WEIGHTS = ("w_up_s5", "w_up_rwkv", "w_up_pool")


def load_up(sp, io, e, n):
    sp.dma_start(e.up_wst[:, n], io[UP_WEIGHTS[n]][0].rearrange("(k p) (m n) -> m p k n", p=P, n=P)[0]).then_inc(e.up_loaded[n], 16)


def phase_glu(nc, io, e):
    YB = 3
    with ExitStack() as ctx:
        sem = lambda n: ctx.enter_context(nc.semaphore(n))
        sb = lambda n, s, d=F32: ctx.enter_context(nc.sbuf_tensor(n, s, d))
        yc, u = sb("glu_yc", [P, WB, L5, J5]), sb("glu_u", [P, WB, NT])
        z5 = u
        act_y, gate = sb("glu_act", [P, WB, NT]), sb("glu_gate", [P, 2, CH[0][1]])
        w = sb("glu_w", [P, WB, W])
        y, z = sb("up_y", [P, YB, NT]), sb("up_z", [P, YB, NT])
        ps = [ctx.enter_context(nc.psum_tensor(f"glu_ps{i}", [P, 512], F32)) for i in range(8)]
        loaded, w_loaded, z_loaded, gelu, mm_done, sig, out, z_silu, out2 = [sem("glu_" + n) for n in (
            "loaded", "w_loaded", "z_loaded", "gelu", "mm", "sig", "out", "z_silu", "out2")]
        yz_loaded = [sem(f"up_loaded{i}") for i in range(YB)]
        silu, prod, hi, lo, lo5 = sem("up_silu"), sem("up_prod"), sem("up_yhi"), sem("up_ylo"), sem("up_ylo5")
        units = [(br, b) for br in (1, 2) for b in range(WB)]
        order = [("unit", n) for n in range(WB)] + [("s5", 0), ("s5", 1)] + [("unit", n) for n in range(WB, len(units))] + [("s5", 2), ("s5", 3)]
        with nc.Block() as block:
            @block.sync
            def _(sp):
                def load(n):
                    br, b = units[n]
                    if n >= YB:
                        sp.wait_ge(lo, n - YB + 1)
                    sp.dma_start(y[:, n % YB], e.y_scr[br, :, b, :]).then_inc(yz_loaded[n % YB], 16)
                    if br == 1:
                        sp.dma_start(z[:, n % YB], e.scratch[B_RWZ + b, :, 1:1 + NT]).then_inc(yz_loaded[n % YB], 16)
                for q in range(8):
                    sp.dma_start(yc[GC * q:GC * q + GC], e.y5_scr.rearrange("(t c) (b q) j -> q c b t j", c=GC, q=8)[q]).then_inc(loaded, 16)
                sp.dma_start(w[:, :, :], io["s5_w_glu"][0].rearrange("(k p) m -> p k m", p=P)).then_inc(w_loaded, 16)
                sp.dma_start(z5[:, :, :], e.scratch[B_S5Z:B_S5Z + WB, :, 1:1 + NT].rearrange("b p t -> p b t")).then_inc(z_loaded, 16)
                for n in range(len(units)):
                    load(n)
                    if n == YB:
                        for w2 in range(2):
                            load_up(sp, io, e, w2)

            @block.vector
            def _(dve):
                def product(n):
                    dve.wait_ge(silu, n + 1)
                    dve.tensor_tensor(y[:, n % YB], y[:, n % YB], z[:, n % YB], ALU.mult).then_inc(prod, 1)
                for m in range(WB):
                    dve.wait_ge(z_silu, m + 1)
                    dve.tensor_tensor(u[:, m, :], act_y[:, m, :], z5[:, m, :], ALU.mult).then_inc(out2, 1)

                def low(m):
                    dve.wait_ge(hi, order.index(("s5", m)) + 1)
                    dve.tensor_tensor(e.yl[:, 0, m], u[:, m, :], e.yh[:, 0, m].bitcast(F32), ALU.subtract).then_inc(lo5, 1)
                for kind, m in order:
                    if kind == "unit":
                        if units[m][0] == 1:
                            product(m)
                        continue
                    dve.wait_ge(out2, m + 1)
                    for c, (at, n) in enumerate(CH):
                        q = m * 3 + c
                        dve.wait_ge(sig, q + 1)
                        dve.tensor_tensor(u[:, m, at:at + n], u[:, m, at:at + n], gate[:, q % 2, 0:n], ALU.mult).then_inc(out, 1)
                    if m:
                        low(m - 1)
                low(WB - 1)
                dve.wait_ge(lo5, WB)

            @block.gpsimd
            def _(pool):
                for n, (br, b) in enumerate(units):
                    pool.wait_ge(hi, order.index(("unit", n)) + 1)
                    pool.tensor_tensor(e.yl[:, br, b], y[:, n % YB], e.yh[:, br, b].bitcast(F32), ALU.subtract).then_inc(lo, 1)
                for w2 in range(2):
                    pool.wait_ge(e.up_hi, w2 + 1)
                    pool.tensor_tensor(e.up_wlo[:, w2], e.up_wst[:, w2], e.up_whi[:, w2].bitcast(F32), ALU.subtract).then_inc(e.up_lo, 1)
                pool.wait_ge(lo, len(units))

            @block.scalar
            def _(act):
                def high(kind, n):
                    br, b = units[n] if kind == "unit" else (0, n)
                    if kind == "unit" and br == 1:
                        act.wait_ge(prod, n + 1)
                    elif kind == "s5":
                        act.wait_ge(out, 3 * (n + 1))
                    act.activation(e.yh[:, br, b], y[:, n % YB] if kind == "unit" else u[:, n, :], ACT.Copy).then_inc(hi, 1)
                act.wait_ge(loaded, 16 * 8)
                for b in range(WB):
                    act.activation(act_y[:, b, :].rearrange("p (j t) -> p j t", t=L5), yc[:, b].rearrange("p t j -> p j t"),
                                   ACT.Gelu_apprx_tanh).then_inc(gelu, 1)
                act.wait_ge(z_loaded, 16)
                for b in range(WB):
                    act.activation(z5[:, b, :], z5[:, b, :], ACT.Silu).then_inc(z_silu, 1)
                for at, (kind, m) in enumerate(order):
                    if kind == "unit":
                        act.wait_ge(yz_loaded[m % YB], sum(32 if k < WB else 16 for k in range(m % YB, m + 1, YB)))
                        if units[m][0] == 1:
                            act.activation(z[:, m % YB], z[:, m % YB], ACT.Silu).then_inc(silu, 1)
                    else:
                        for c, (_, n) in enumerate(CH):
                            q = m * 3 + c
                            act.wait_ge(mm_done, q + 1)
                            if q >= 2:
                                act.wait_ge(out, q - 1)
                            act.activation(gate[:, q % 2, 0:n], ps[q % 8][:, 0:n], ACT.Sigmoid).then_inc(sig, 1)
                    if at:
                        high(*order[at - 1])
                    if at == len(order) - 2:
                        for w2 in range(2):
                            act.wait_ge(e.up_loaded[w2], 16)
                            act.activation(e.up_whi[:, w2], e.up_wst[:, w2], ACT.Copy).then_inc(e.up_hi, 1)
                high(*order[-1])

            @block.tensor
            def _(pe):
                pe.wait_ge(w_loaded, 16)
                pe.wait_ge(gelu, WB)
                for m in range(WB):
                    for c, (at, n) in enumerate(CH):
                        q = m * 3 + c
                        if q >= 8:
                            pe.wait_ge(sig, q - 7)
                        for k in range(WB):
                            mm = pe.matmul(ps[q % 8][:, 0:n], w[:, k, m * P:(m + 1) * P], act_y[:, k, at:at + n], start=k == 0, stop=k == WB - 1)
                        mm.then_inc(mm_done, 1)


def phase_up(nc, io, e):
    w_up = [io[n] for n in UP_WEIGHTS]
    NB3 = 3
    with ExitStack() as ctx:
        sem = lambda n: ctx.enter_context(nc.semaphore(n))
        yh, yl = e.yh, e.yl
        sb = lambda n, s, d=F32: ctx.enter_context(nc.sbuf_tensor(n, s, d))
        wst, whi, wlo, w_loaded, w_hi, w_lo = e.up_wst, e.up_whi, e.up_wlo, e.up_loaded, e.up_hi, e.up_lo
        gate = sb("up_gate", [P, 2, NT])
        gu = sb("up_gu", [P, 2, CH[0][1]])
        acc = sb("up_acc", [P, NT])
        ps = [ctx.enter_context(nc.psum_tensor(f"up_ps{i}", [P, 512], F32)) for i in range(6)]
        g_loaded = [sem(f"upg_loaded{i}") for i in range(2)]
        mm_done, sig, gated, summed, m_hi, m_lo = [sem("up_" + n) for n in ("mm", "sig", "gated", "summed", "m_hi", "m_lo")]
        UN = 2 * NB3
        with nc.Block() as block:
            @block.sync
            def _(sp):
                def load(i, u, first):
                    m, br = i * 2 + u // 3, u % 3
                    if not (first and u < 2):
                        sp.wait_ge(w_lo, i * UN + (u - 1))
                        sp.dma_start(wst[:, u % 2], w_up[br][0].rearrange("(k p) (m n) -> m p k n", p=P, n=P)[m]).then_inc(w_loaded[u % 2], 16)
                    if not (first and u < 2):
                        sp.wait_ge(gated, i * (3 * UN) + 3 * (u - 1))
                    sp.dma_start(gate[:, u % 2], e.scratch[B_GATE + br * KT:B_GATE + (br + 1) * KT][m, :, 1:1 + NT]).then_inc(g_loaded[u % 2], 16)
                for u in range(UN):
                    load(0, u, True)
                with sp.Fori(1, KT // 2) as i:
                    for u in range(UN):
                        load(i, u, False)

            @block.scalar
            def _(act):
                def body(i, first):
                    for u in range(UN):
                        if not (first and u < 2):
                            act.wait_ge(w_loaded[u % 2], i * (16 * 3) + 16 * (u // 2 + 1))
                            act.wait_ge(mm_done, i * (3 * UN) + 3 * (u - 1))
                            act.activation(whi[:, u % 2], wst[:, u % 2], ACT.Copy).then_inc(w_hi, 1)
                        act.wait_ge(g_loaded[u % 2], i * (16 * 3) + 16 * (u // 2 + 1))
                        act.activation(gate[:, u % 2], gate[:, u % 2], ACT.Sigmoid).then_inc(sig, 1)
                        if u in (0, 3) and not (first and u == 0):
                            merged_hi(i, u)

                def merged_hi(i, u):
                    act.wait_ge(summed, i * (3 * UN) + 3 * u)
                    act.activation(e.m_hi[:, i * 2 + (u // 3 - 1)], acc[:, :], ACT.Copy).then_inc(m_hi, 1)
                body(0, True)
                with act.Fori(1, KT // 2) as i:
                    body(i, False)
                merged_hi(KT // 2, 0)

            @block.gpsimd
            def _(pool):
                def merged_lo(i, u):
                    pool.wait_ge(m_hi, i * 2 + u // 3)
                    pool.tensor_tensor(e.m_lo[:, i * 2 + (u // 3 - 1)], acc[:, :], e.m_hi[:, i * 2 + (u // 3 - 1)].bitcast(F32), ALU.subtract).then_inc(m_lo, 1)

                def body(i, first):
                    for u in range(UN):
                        if not (first and u < 2):
                            pool.wait_ge(w_hi, i * UN + (u + 1))
                            pool.tensor_tensor(wlo[:, u % 2], wst[:, u % 2], whi[:, u % 2].bitcast(F32), ALU.subtract).then_inc(w_lo, 1)
                        if u in (0, 3) and not (first and u == 0):
                            merged_lo(i, u)
                body(0, True)
                with pool.Fori(1, KT // 2) as i:
                    body(i, False)
                merged_lo(KT // 2, 0)
                pool.wait_ge(m_lo, KT)

            @block.tensor
            def _(pe):
                def body(i, first):
                    for u in range(UN):
                        br = u % 3
                        pe.wait_ge(w_lo, i * UN + (u + 1))
                        for c, (at, n) in enumerate(CH):
                            q = 3 * u + c
                            if not (first and q < 6):
                                pe.wait_ge(gated, i * (3 * UN) + (q - 5))
                            for k in range(WB):
                                mm = split_mm(pe, ps[q % 6][:, 0:n], whi[:, u % 2, k], wlo[:, u % 2, k], yh[:, br, k, at:at + n],
                                              yl[:, br, k, at:at + n], k == 0, k == WB - 1)
                            mm.then_inc(mm_done, 1)
                body(0, True)
                with pe.Fori(1, KT // 2) as i:
                    body(i, False)

            @block.vector
            def _(dve):
                def body(i, first):
                    for u in range(UN):
                        dve.wait_ge(sig, i * UN + (u + 1))
                        if u in (0, 3) and not (first and u == 0):
                            dve.wait_ge(m_lo, i * 2 + u // 3)
                        for c, (at, n) in enumerate(CH):
                            q = 3 * u + c
                            dve.wait_ge(mm_done, i * (3 * UN) + (q + 1))
                            dst = acc[:, at:at + n] if u % 3 == 0 else gu[:, q % 2, 0:n]
                            dve.tensor_tensor(dst, ps[q % 6][:, 0:n], gate[:, u % 2, at:at + n], ALU.mult).then_inc(gated, 1)
                            dve.wait_ge(gated, i * (3 * UN) + (q + 1))
                            if u % 3 == 0:
                                dve.sem_inc(summed, 1)
                            else:
                                dve.tensor_tensor(acc[:, at:at + n], acc[:, at:at + n], dst, ALU.add).then_inc(summed, 1)
                                dve.wait_ge(summed, i * (3 * UN) + (q + 1))
                body(0, True)
                with dve.Fori(1, KT // 2) as i:
                    body(i, False)


def phase_out(nc, io, e):
    with ExitStack() as ctx:
        sem = lambda n: ctx.enter_context(nc.semaphore(n))
        sb = lambda n, s, d=F32: ctx.enter_context(nc.sbuf_tensor(n, s, d))
        wst = sb("wo", [P, 2, D])
        whi, wlo = sb("wo_hi", [P, KT, D], F32R), sb("wo_lo", [P, KT, D], F32R)
        gpost = sb("gpost_row", [P, D])
        xt, yt = sb("x_res", [P, 2, D]), sb("y_out_tile", [P, 2, D])
        junk = sb("out_junk", [P, 512])
        ss, s1, root, rstd = sb("o_ss", [P, 2, 9]), sb("o_s1", [P, 9]), sb("o_root", [P, 9]), sb("o_rstd", [P, 9])
        ps = [ctx.enter_context(nc.psum_tensor(f"out_ps{i}", [P, 512], F32)) for i in range(8)]
        w_loaded = [sem(f"wo_loaded{i}") for i in range(2)]
        x_loaded = [sem(f"xr_loaded{i}") for i in range(2)]
        y_stored = [sem(f"yo_stored{i}") for i in range(2)]
        g_loaded, w_hi, w_lo, mm_done, sq, s1_done, root_done, rs, normed, summed = [sem("o_" + n) for n in (
            "g_loaded", "w_hi", "w_lo", "mm", "sq", "s1_done", "root_done", "rs", "normed", "summed")]
        tiles = [(t * P, P if t < TILES else NB * NS) for t in range(TILES + 1)]
        with nc.Block() as block:
            @block.sync
            def _(sp):
                def rows(name, t, n):
                    a = io[name] if name[0] == "x" else e.outs[name]
                    return a[0, t * P:t * P + n, :] if t < TILES else a.rearrange("b t d -> (b t) d")

                def load_x(t):
                    n = tiles[t][1]
                    sp.dma_start(xt[0:n, t % 2], rows("x_prompt" if t < TILES else "x_sample", t, n)).then_inc(x_loaded[t % 2], 16)
                for k in range(KT):
                    if k >= 2:
                        sp.wait_ge(w_lo, k - 1)
                    sp.dma_start(wst[:, k % 2], io["w_o"][0, k * P:(k + 1) * P, :]).then_inc(w_loaded[k % 2], 16)
                sp.dma_start(gpost[:, :], io["norm_post"].to_broadcast((P, D))).then_inc(g_loaded, 16)
                load_x(0)
                load_x(1)
                for t, (at, n) in enumerate(tiles):
                    sp.wait_ge(summed, t + 1)
                    sp.dma_start(rows("y_prompt" if t < TILES else "y_sample", t, n), yt[0:n, t % 2]).then_inc(y_stored[t % 2], 16)
                    if t + 2 < len(tiles):
                        load_x(t + 2)
                sp.wait_ge(y_stored[0], 16 * 5)
                sp.wait_ge(y_stored[1], 16 * 4)

            @block.gpsimd
            def _(pool):
                for k in range(KT):
                    pool.wait_ge(w_hi, k + 1)
                    pool.tensor_tensor(wlo[:, k], wst[:, k % 2], whi[:, k].bitcast(F32), ALU.subtract).then_inc(w_lo, 1)

            @block.tensor
            def _(pe):
                def products(t, k):
                    at, n = tiles[t]
                    for h in range(2):
                        d = slice(512 * h, 512 * h + 512)
                        mm = split_mm(pe, ps[2 * (t % 4) + h][0:n, :], e.m_hi[:, k, at:at + n], e.m_lo[:, k, at:at + n],
                                      whi[:, k, d], wlo[:, k, d], k == 0, k == KT - 1)
                    if k == KT - 1:
                        mm.then_inc(mm_done, 1)
                for k in range(KT):
                    pe.wait_ge(w_lo, k + 1)
                    for t in range(4):
                        products(t, k)
                for t in range(4, len(tiles)):
                    pe.wait_ge(normed, 2 * (t - 3))
                    for k in range(KT):
                        products(t, k)

            @block.scalar
            def _(act):
                for k in range(KT):
                    act.wait_ge(w_loaded[k % 2], 16 * (k // 2 + 1))
                    act.activation(whi[:, k], wst[:, k % 2], ACT.Copy).then_inc(w_hi, 1)
                for t, (at, n) in enumerate(tiles):
                    act.wait_ge(mm_done, t + 1)
                    for h in range(2):
                        if t or h:
                            act.wait_ge(sq, 2 * t + h)
                        act.activation(junk[0:n, :], ps[2 * (t % 4) + h][0:n, :], ACT.Square, accum_out=ss[0:n, h, t:t + 1]).then_inc(sq, 1)
                    act.wait_ge(s1_done, t + 1)
                    act.activation(root[0:n, t:t + 1], s1[0:n, t:t + 1], ACT.Sqrt, scale=1.0 / D, bias=e.eps[0:n, 0:1]).then_inc(root_done, 1)

            @block.vector
            def _(dve):
                dve.wait_ge(g_loaded, 16)
                for t, (at, n) in enumerate(tiles):
                    dve.wait_ge(sq, 2 * t + 2)
                    dve.tensor_tensor(s1[0:n, t:t + 1], ss[0:n, 0, t:t + 1], ss[0:n, 1, t:t + 1], ALU.add).then_inc(s1_done, 1)
                    dve.wait_ge(root_done, t + 1)
                    dve.reciprocal(rstd[0:n, t:t + 1], root[0:n, t:t + 1]).then_inc(rs, 1)
                    dve.wait_ge(rs, t + 1)
                    if t >= 2:
                        dve.wait_ge(y_stored[t % 2], 16 * (t // 2))
                    for h in range(2):
                        d = slice(512 * h, 512 * h + 512)
                        dve.scalar_tensor_tensor(out=yt[0:n, t % 2, d], in0=ps[2 * (t % 4) + h][0:n, :], scalar=rstd[0:n, t:t + 1],
                                                 in1=gpost[0:n, d], op0=ALU.mult, op1=ALU.mult).then_inc(normed, 1)
                    dve.wait_ge(x_loaded[t % 2], 16 * (t // 2 + 1))
                    dve.wait_ge(normed, 2 * t + 2)
                    dve.tensor_tensor(yt[0:n, t % 2], yt[0:n, t % 2], xt[0:n, t % 2], ALU.add).then_inc(summed, 1)


def build(nc, io, outs):
    e = Env()
    e.outs = outs
    dram = lambda n, s: nc.dram_tensor(n, s, F32).ap()
    e.scratch = dram("projected", (NIN, P, NT + 1))
    e.y_scr = dram("y_branches", (3, P, WB, NT))
    e.s0t_scr = dram("s0_turned", (HD, NB * H, HD))
    e.u5_scr = dram("s5_u_chunks", (P, WB, L5, J5))
    e.par_scr = dram("s5_params", (P, S5Params.SIZE))
    e.y5_scr = dram("s5_y_chunks", (P, G, J5))
    with ExitStack() as ctx:
        sb = lambda n, s, d=F32: ctx.enter_context(nc.sbuf_tensor(n, s, d))
        e.ident = sb("ident", [P, P])[:, :]
        e.vec = sb("vec", [P, NVEC])
        e.eps = sb("eps", [P, 2])
        e.s_a = sb("s_a", [P, 4, HD])
        with ExitStack() as rctx:
            sb = lambda n, s, d=F32: rctx.enter_context(nc.sbuf_tensor(n, s, d))
            e.ones_bd = sb("ones_bd", [P, P])[:, :]
            e.lv = sb("level_masks", [P, 5, P])[:, :, :]
            e.up_strict = sb("up_strict", [P, C])[:, :]
            e.up_incl = sb("up_incl", [P, C])[:, :]
            e.pair_st = sb("pair_st", [P, C])[:, :]
            e.s_strict = sb("s_strict", [NB * NS, C])[:, :]
            e.s_incl = sb("s_incl", [NB * NS, C])[:, :]
            e.keep_p = sb("keep_p", [P, WB * P])[:, :]
            e.keep_s = sb("keep_s", [P, WB * NB * NS])[:, :]
            e.seq_of = sb("seq_of", [NB * NS, NB])[:, :]
            e.one_minus_ka = sb("one_minus_ka", [P, 4])
            e.shiftT = sb("shiftT", [P, RB, NB])[:, :, :]
            e.lora_w = sb("lora_w", [P, W])
            e.h_hi = sb("h_hi", [P, KT, NT], F32R)
            e.h_lo = sb("h_lo", [P, KT, NT], F32R)
            with ExitStack() as pctx:
                sbp = lambda n, s, d=F32: pctx.enter_context(nc.sbuf_tensor(n, s, d))
                semp = lambda n: pctx.enter_context(nc.semaphore(n))
                e.wst, e.whi, e.wlo = sbp("wst", [P, RW, KT, P]), sbp("whi", [P, RW, KT, P], F32R), sbp("wlo", [P, RW, KT, P], F32R)
                e.w_loaded, e.w_hi, e.w_lo = [semp(f"pw_loaded{i}") for i in range(RW)], semp("pw_hi"), semp("pw_lo")
                with ExitStack() as nctx:
                    e.xt, e.gpre_row = (nctx.enter_context(nc.sbuf_tensor(n, s, F32, side="right")) for n, s in (
                        ("xt", [P, 3, D]), ("gpre_row", [P, D])))
                    e.x_loaded, e.g_loaded = [semp(f"x_loaded{i}") for i in range(3)], semp("g_loaded")
                    phase_start(nc, io, e)
                    phase_norm(nc, io, e)
                phase_project(nc, io, e)
            with nc.cleanup_on_exit():
                phase_rwkv(nc, io, e)
        with ExitStack() as sctx:
            sb = lambda n, s, d=F32: sctx.enter_context(nc.sbuf_tensor(n, s, d))
            e.toep = sb("s5_toep", [P, G, P])
            e.par_tile = sb("s5_par", [P, S5Params.SIZE])
            e.par = S5Params(e.par_tile)
            phase_pool(nc, io, e)
            e.es = sb("s5_es", [P, 2, G, P])
            e.dtab = sb("s5_dtab", [P, G, L5 + 1, GC])
            e.rot = sb("s5_rot", [P, 2, G, JP])
            e.u5 = sb("s5_u", [P, G, J5])
            e.hprev = sb("s5_hprev", [P, G, J5])
            e.u5_sem = sctx.enter_context(nc.semaphore("u5_chunks_loaded"))
            phase_s5_tables(nc, io, e)
            phase_s5(nc, io, e)
        sb = lambda n, s, d=F32: ctx.enter_context(nc.sbuf_tensor(n, s, d))
        with ExitStack() as mctx:
            e.yh, e.yl = (mctx.enter_context(nc.sbuf_tensor(n, [P, 3, WB, NT], F32R, side="right")) for n in ("branch_hi", "branch_lo"))
            right = lambda n, d: mctx.enter_context(nc.sbuf_tensor(n, [P, 2, WB, P], d, side="right"))
            e.up_wst, e.up_whi, e.up_wlo = right("up_w", F32), right("up_w_hi", F32R), right("up_w_lo", F32R)
            semu = lambda n: mctx.enter_context(nc.semaphore(n))
            e.up_loaded, e.up_hi, e.up_lo = [semu(f"upw_loaded{i}") for i in range(2)], semu("upw_hi"), semu("upw_lo")
            phase_glu(nc, io, e)
            e.m_hi = sb("merged_hi", [P, KT, NT], F32R)
            e.m_lo = sb("merged_lo", [P, KT, NT], F32R)
            phase_up(nc, io, e)
        phase_out(nc, io, e)


_INS = (
    "x_prompt",
    "x_sample",
    "state_s5_re",
    "state_s5_im",
    "state_rwkv",
    "state_shift",
    "state_pool",
    "norm_pre",
    "norm_post",
    "w_in",
    "s5_lam_re",
    "s5_lam_im",
    "s5_log_dt",
    "s5_b_re",
    "s5_b_im",
    "s5_c_re",
    "s5_c_im",
    "s5_d",
    "s5_w_glu",
    "rwkv_mu",
    "rwkv_w0",
    "rwkv_w_w2",
    "rwkv_a0",
    "rwkv_w_a2",
    "rwkv_k_k",
    "rwkv_k_a",
    "rwkv_r_k",
    "rwkv_gn_w",
    "rwkv_gn_b",
    "pool_w",
    "pool_scale",
    "w_up_s5",
    "w_up_rwkv",
    "w_up_pool",
    "w_o",
)
_OUTS = (
    ("y_prompt", (1, 1024, 1024)),
    ("y_sample", (8, 8, 1024)),
    ("p_s5_re", (1, 1, 32, 64)),
    ("p_s5_im", (1, 1, 32, 64)),
    ("p_rwkv", (1, 1, 8, 64, 64)),
    ("p_shift", (1, 1, 1664)),
    ("p_pool", (1, 1, 15, 512)),
    ("s_s5_re", (1, 8, 32, 64)),
    ("s_s5_im", (1, 8, 32, 64)),
    ("s_rwkv", (1, 8, 8, 64, 64)),
    ("s_shift", (1, 8, 1664)),
    ("s_pool", (1, 8, 15, 512)),
)


def kernel(**inputs):
    import numpy as _np
    import concourse.bacc as _bacc
    from concourse import mybir as _mybir
    from concourse.bass_utils import run_bass_kernel_spmd as _run

    nc = _bacc.Bacc("TRN2", target_bir_lowering=False, num_devices=1)
    arrays, io, outs = {}, {}, {}
    for name in _INS:
        a = _np.ascontiguousarray(inputs[name])
        arrays[f"in_{name}_dram"] = a
        io[name] = nc.dram_tensor(f"in_{name}_dram", a.shape, _mybir.dt.from_np(a.dtype), kind="ExternalInput").ap()
    for name, shape in _OUTS:
        outs[name] = nc.dram_tensor(f"out_{name}_dram", shape, _mybir.dt.float32, kind="ExternalOutput").ap()
    build(nc, io, outs)
    r = _run(nc, [arrays], core_ids=[0])
    return tuple(r.results[0][f"out_{name}_dram"] for name, _ in _OUTS)
```
